# Optimizing a Trainium2 kernel written in Bass

```python
import math
import jax
import jax.numpy as jnp
from jax import lax
import numpy as np

D_MODEL = 1024
BATCH = 1
SEQ = 256
DEPTH = 2

GRID_W = 64
CTX_LEN = 256
HEAD_DIM = 64
MIX_WIDTH = 1024
N_MOD = 9
FFN_HIDDEN = 2816
NORM_EPS = 1e-6
FOURIER_GROUPS = 4
FOURIER_WIDTH = FOURIER_GROUPS * HEAD_DIM
GLA_HEADS = 6
GLA_DK = 64
GLA_DV = 128
GLA_GATE_RANK = 16
GLA_TAU = 16.0
GLA_CHUNK = 64
CONV_GROUPS = 4
CONV_WIDTH = CONV_GROUPS * HEAD_DIM
CONV_TAPS = 3
DIFF_HEADS = 6
DIFF_DV = 2 * HEAD_DIM
Q_BLOCK = 128
ROPE_THETA = 10000.0
ROPE_AXIS_DIM = HEAD_DIM // 2
N_EVEN = (DEPTH + 1) // 2
N_ODD = DEPTH // 2
EVEN_SPLITS = (FOURIER_WIDTH, GLA_HEADS * GLA_DK, GLA_HEADS * GLA_DK, GLA_HEADS * GLA_DV, GLA_HEADS * GLA_DV, GLA_GATE_RANK, GLA_GATE_RANK)
EVEN_IN = sum(EVEN_SPLITS)
ODD_SPLITS = (CONV_WIDTH, CONV_WIDTH, CONV_WIDTH, DIFF_HEADS * 2 * HEAD_DIM, DIFF_HEADS * 2 * HEAD_DIM, DIFF_HEADS * DIFF_DV)
ODD_IN = sum(ODD_SPLITS)


def _split(z, sizes):
    idx = [int(i) for i in np.cumsum(sizes)[:-1]]
    return jnp.split(z, idx, axis=-1)

def _rmsnorm(x, g):
    xf = x.astype(jnp.float32)
    y = xf * lax.rsqrt(jnp.mean(xf * xf, axis=-1, keepdims=True) + NORM_EPS)
    return (y * g.astype(jnp.float32)).astype(x.dtype)

def _modulation(cond, w, b):
    m = jax.nn.silu(cond) @ w + b
    return jnp.split(m[..., None, :], N_MOD, axis=-1)

def _prenorm(h, gain, shift, scale):
    return _rmsnorm(h, gain) * (1.0 + scale) + shift

def _swiglu(h, w_in, w_out):
    g, u = jnp.split(h @ w_in, 2, axis=-1)
    return (jax.nn.silu(g) * u) @ w_out

def _axial_rope_tables(rows):
    row = jnp.repeat(jnp.arange(rows), GRID_W).astype(jnp.float32)
    col = jnp.tile(jnp.arange(GRID_W), rows).astype(jnp.float32)
    n = ROPE_AXIS_DIM // 2
    inv = ROPE_THETA ** (-jnp.arange(n, dtype=jnp.float32) / n)
    ang = jnp.concatenate([row[:, None] * inv, col[:, None] * inv], axis=-1)
    return jnp.cos(ang), jnp.sin(ang)

def _axial_rope(x, cos, sin):
    n = ROPE_AXIS_DIM // 2
    def rot(part, cs, sn):
        p1, p2 = jnp.split(part, 2, axis=-1)
        return jnp.concatenate([p1 * cs - p2 * sn, p1 * sn + p2 * cs], axis=-1)
    bc = lambda t: t[:, None, None, :]
    xr = rot(x[..., :ROPE_AXIS_DIM], bc(cos[:, :n]), bc(sin[:, :n]))
    xc = rot(x[..., ROPE_AXIS_DIM:], bc(cos[:, n:]), bc(sin[:, n:]))
    return jnp.concatenate([xr, xc], axis=-1).astype(x.dtype)

def _fourier_mix(z):
    bn, t, _ = z.shape
    zf = z.astype(jnp.float32).reshape(bn, t, FOURIER_GROUPS, HEAD_DIM)
    y = jnp.fft.fft2(zf, axes=(1, 3), norm='ortho').real
    return y.reshape(bn, t, FOURIER_WIDTH).astype(z.dtype)

def _gla_chunked(q, k, v, logg, s0):
    bn, h, t, dk = q.shape
    dv = v.shape[-1]
    n = t // GLA_CHUNK
    def chunks(a):
        return jnp.moveaxis(a.reshape(bn, h, n, GLA_CHUNK, a.shape[-1]), 2, 0)
    b = jnp.cumsum(chunks(logg), axis=-2)
    mask = jnp.tril(jnp.ones((GLA_CHUNK, GLA_CHUNK), dtype=bool))
    def step(s, inp):
        qc, kc, vc, bc = inp
        bl = bc[..., -1:, :]
        qd = qc * jnp.exp(bc)
        kd = kc * jnp.exp(-bc)
        att = jnp.where(mask, jnp.einsum('bhid,bhjd->bhij', qd, kd), 0.0)
        o = jnp.einsum('bhid,bhdv->bhiv', qd, s) + jnp.einsum('bhij,bhjv->bhiv', att, vc)
        s = s * jnp.exp(bl)[..., 0, :, None] + jnp.einsum('bhjd,bhjv->bhdv', kc * jnp.exp(bl - bc), vc)
        return s, o
    s, o = lax.scan(step, s0, (chunks(q), chunks(k), chunks(v), b))
    return jnp.moveaxis(o, 0, 2).reshape(bn, h, t, dv), s

def _even_mixer(z, s0_f, s0_b, gate_w, gate_b, gla_g):
    bn, t, _ = z.shape
    z_f, zq, zk, zv, zr, zgf, zgb = _split(z, EVEN_SPLITS)
    y_f = _fourier_mix(z_f)
    def heads(a, d):
        return a.astype(jnp.float32).reshape(bn, t, GLA_HEADS, d).transpose(0, 2, 1, 3)
    q = heads(zq, GLA_DK) * (GLA_DK ** -0.5)
    k = heads(zk, GLA_DK)
    v = heads(zv, GLA_DV)
    gw = gate_w.astype(jnp.float32)
    gb = gate_b.astype(jnp.float32)
    logg_f = heads(jax.nn.log_sigmoid(zgf.astype(jnp.float32) @ gw[0] + gb[0]), GLA_DK) / GLA_TAU
    logg_b = heads(jax.nn.log_sigmoid(zgb.astype(jnp.float32) @ gw[1] + gb[1]), GLA_DK) / GLA_TAU
    flip = lambda a: jnp.flip(a, axis=2)
    o_f, s_f = _gla_chunked(q, k, v, logg_f, s0_f)
    o_b, s_b = _gla_chunked(flip(q), flip(k), flip(v), flip(logg_b), s0_b)
    o = (o_f + flip(o_b)).transpose(0, 2, 1, 3)
    o = _rmsnorm(o, gla_g) * jax.nn.silu(zr.astype(jnp.float32).reshape(bn, t, GLA_HEADS, GLA_DV))
    y_g = o.reshape(bn, t, GLA_HEADS * GLA_DV).astype(z.dtype)
    return jnp.concatenate([y_f, y_g], axis=-1), s_f, s_b

def _short_conv(zb, zc, zx, w, b):
    u = zc * zx
    t = u.shape[1]
    up = jnp.pad(u, ((0, 0), (1, 1), (0, 0)))
    y = up[:, 0:t] * w[0] + up[:, 1:t + 1] * w[1] + up[:, 2:t + 2] * w[2] + b
    return zb * y

def _odd_parts(z):
    bn, t, _ = z.shape
    zb, zc, zx, q, k, v = _split(z, ODD_SPLITS)
    q = q.reshape(bn, t, DIFF_HEADS, 2, HEAD_DIM)
    k = k.reshape(bn, t, DIFF_HEADS, 2, HEAD_DIM)
    v = v.reshape(bn, t, DIFF_HEADS, DIFF_DV)
    return zb, zc, zx, q, k, v

def _diff_attn(q, k, v, lam):
    s = jnp.einsum('bqhsd,bkhsd->bhsqk', q, k, preferred_element_type=jnp.float32) * (HEAD_DIM ** -0.5)
    p = jax.nn.softmax(s, axis=-1)
    a = p[:, :, 0] - lam * p[:, :, 1]
    return jnp.einsum('bhqk,bkhv->bqhv', a, v.astype(jnp.float32))

def _diff_attn_blocked(q, k, v, lam):
    bn, t = q.shape[:2]
    nb = t // Q_BLOCK
    qb = jnp.moveaxis(q.reshape(bn, nb, Q_BLOCK, DIFF_HEADS, 2, HEAD_DIM), 1, 0)
    o = lax.map(lambda blk: _diff_attn(blk, k, v, lam), qb)
    return jnp.moveaxis(o, 0, 1).reshape(bn, t, DIFF_HEADS, DIFF_DV)

def _subln(o, g, lam_init, dtype):
    bn, t = o.shape[:2]
    return (_rmsnorm(o, g) * (1.0 - lam_init)).reshape(bn, t, DIFF_HEADS * DIFF_DV).astype(dtype)

def _odd_mixer(zl, zc, cos, sin, conv_w, conv_b, lam, lam_init, dnorm, with_ctx_out):
    lat = _odd_parts(zl)
    cx = _odd_parts(zc)
    ql = _axial_rope(lat[3], cos, sin)
    kl = _axial_rope(lat[4], cos, sin)
    k_all = jnp.concatenate([kl, cx[4]], axis=1)
    v_all = jnp.concatenate([lat[5], cx[5]], axis=1)
    att_l = _diff_attn_blocked(ql, k_all, v_all, lam)
    y_l = jnp.concatenate([_short_conv(lat[0], lat[1], lat[2], conv_w, conv_b),
                           _subln(att_l, dnorm, lam_init, zl.dtype)], axis=-1)
    if not with_ctx_out:
        return y_l, None
    att_c = _diff_attn(cx[3], cx[4], cx[5], lam)
    y_c = jnp.concatenate([_short_conv(cx[0], cx[1], cx[2], conv_w, conv_b),
                           _subln(att_c, dnorm, lam_init, zc.dtype)], axis=-1)
    return y_l, y_c

def first_inputs(seed: int = 0) -> dict:
    key = jax.random.key(seed)
    ks = jax.random.split(key, 28)
    nrm = lambda k, shape, s: jax.random.normal(k, shape, jnp.float32) * s
    gain = lambda k, shape: 1.0 + 0.05 * jax.random.normal(k, shape, jnp.float32)
    D = D_MODEL
    return {
        'x': nrm(ks[0], (BATCH, SEQ, D), 1.0),
        'c': nrm(ks[1], (BATCH, D), 1.0),
        'ctx': nrm(ks[2], (BATCH, CTX_LEN, D), 1.0),
        'c_ctx': nrm(ks[3], (D,), 1.0),
        'ada_w': nrm(ks[4], (DEPTH, D, N_MOD * D), 0.5 * D ** -0.5),
        'ada_b': nrm(ks[5], (DEPTH, N_MOD * D), 0.01),
        'norm_ffn1': gain(ks[6], (DEPTH, D)),
        'norm_mix': gain(ks[7], (DEPTH, D)),
        'norm_ffn2': gain(ks[8], (DEPTH, D)),
        'ffn1_w_in': nrm(ks[9], (DEPTH, D, 2 * FFN_HIDDEN), D ** -0.5),
        'ffn1_w_out': nrm(ks[10], (DEPTH, FFN_HIDDEN, D), FFN_HIDDEN ** -0.5),
        'ffn2_w_in': nrm(ks[11], (DEPTH, D, 2 * FFN_HIDDEN), D ** -0.5),
        'ffn2_w_out': nrm(ks[12], (DEPTH, FFN_HIDDEN, D), FFN_HIDDEN ** -0.5),
        'mix_w_out': nrm(ks[13], (DEPTH, MIX_WIDTH, D), MIX_WIDTH ** -0.5),
        'even_w_in': nrm(ks[14], (N_EVEN, D, EVEN_IN), D ** -0.5),
        'gla_gate_w': nrm(ks[15], (N_EVEN, 2, GLA_GATE_RANK, GLA_HEADS * GLA_DK), GLA_GATE_RANK ** -0.5),
        'gla_gate_b': nrm(ks[16], (N_EVEN, 2, GLA_HEADS * GLA_DK), 0.1),
        'gla_norm': gain(ks[17], (N_EVEN, GLA_DV)),
        'odd_w_in': nrm(ks[18], (N_ODD, D, ODD_IN), D ** -0.5),
        'conv_w': nrm(ks[19], (N_ODD, CONV_TAPS, CONV_WIDTH), CONV_TAPS ** -0.5),
        'conv_b': nrm(ks[20], (N_ODD, CONV_WIDTH), 0.01),
        'lambda_q1': nrm(ks[21], (N_ODD, HEAD_DIM), 0.1),
        'lambda_k1': nrm(ks[22], (N_ODD, HEAD_DIM), 0.1),
        'lambda_q2': nrm(ks[23], (N_ODD, HEAD_DIM), 0.1),
        'lambda_k2': nrm(ks[24], (N_ODD, HEAD_DIM), 0.1),
        'diff_norm': gain(ks[25], (N_ODD, DIFF_DV)),
        'final_norm': gain(ks[26], (D,)),
    }

def first_block(x, c, ctx, c_ctx, ada_w, ada_b, norm_ffn1, norm_mix, norm_ffn2, ffn1_w_in, ffn1_w_out,
              ffn2_w_in, ffn2_w_out, mix_w_out, even_w_in, gla_gate_w, gla_gate_b, gla_norm, odd_w_in,
              conv_w, conv_b, lambda_q1, lambda_k1, lambda_q2, lambda_k2, diff_norm, final_norm):
    bn = x.shape[0]
    rows = x.shape[1] // GRID_W
    cos, sin = _axial_rope_tables(rows)
    h, hc = x, ctx
    for layer in range(DEPTH):
        last = layer == DEPTH - 1
        sh1, sc1, g1, shm, scm, gm, sh2, sc2, g2 = _modulation(c, ada_w[layer], ada_b[layer])
        csh1, csc1, cg1, cshm, cscm, cgm, csh2, csc2, cg2 = _modulation(c_ctx, ada_w[layer], ada_b[layer])
        h = h + 0.5 * g1 * _swiglu(_prenorm(h, norm_ffn1[layer], sh1, sc1), ffn1_w_in[layer], ffn1_w_out[layer])
        hc = hc + 0.5 * cg1 * _swiglu(_prenorm(hc, norm_ffn1[layer], csh1, csc1), ffn1_w_in[layer], ffn1_w_out[layer])
        if layer % 2 == 0:
            i = layer // 2
            w_in = even_w_in[i]
            zl = _prenorm(h, norm_mix[layer], shm, scm) @ w_in
            zc = _prenorm(hc, norm_mix[layer], cshm, cscm) @ w_in
            s0 = jnp.zeros((bn, GLA_HEADS, GLA_DK, GLA_DV), jnp.float32)
            mix_c, s_f, s_b = _even_mixer(zc, s0, s0, gla_gate_w[i], gla_gate_b[i], gla_norm[i])
            mix_l, _, _ = _even_mixer(zl, s_f, s_b, gla_gate_w[i], gla_gate_b[i], gla_norm[i])
        else:
            i = layer // 2
            w_in = odd_w_in[i]
            zl = _prenorm(h, norm_mix[layer], shm, scm) @ w_in
            zc = _prenorm(hc, norm_mix[layer], cshm, cscm) @ w_in
            lam_init = 0.8 - 0.6 * math.exp(-0.3 * layer)
            lam = (jnp.exp(jnp.sum(lambda_q1[i].astype(jnp.float32) * lambda_k1[i].astype(jnp.float32)))
                   - jnp.exp(jnp.sum(lambda_q2[i].astype(jnp.float32) * lambda_k2[i].astype(jnp.float32)))
                   + lam_init)
            mix_l, mix_c = _odd_mixer(zl, zc, cos, sin, conv_w[i], conv_b[i], lam, lam_init, diff_norm[i],
                                      not last)
        h = h + gm * (mix_l @ mix_w_out[layer])
        h = h + 0.5 * g2 * _swiglu(_prenorm(h, norm_ffn2[layer], sh2, sc2), ffn2_w_in[layer], ffn2_w_out[layer])
        if not last:
            hc = hc + cgm * (mix_c @ mix_w_out[layer])
            hc = hc + 0.5 * cg2 * _swiglu(_prenorm(hc, norm_ffn2[layer], csh2, csc2), ffn2_w_in[layer], ffn2_w_out[layer])
    return _rmsnorm(h, final_norm)


BRANCH_WIDTH = 512
N_BRANCH = 4
SSM_HEADS = 8
SSM_HEAD_DIM = 64
SSM_INNER = SSM_HEADS * SSM_HEAD_DIM
SSM_GROUPS = 2
SSM_STATE = 128
SSM_CONV = 4
SSM_CHUNK = 256
SSM_CONV_CH = SSM_INNER + 2 * SSM_GROUPS * SSM_STATE
FOX_HEADS = 8
MOBA_HEADS = 8
MOBA_BLOCK = 256
MOBA_TOPK = 3
MOBA_Q_BLOCK = 64
DSA_HEADS = 8
IDX_HEADS = 4
IDX_DIM = 64
DSA_TOPK = 256
FFN_HIDDEN_2 = -(-8 * D_MODEL // (3 * 256)) * 256
EPS = 1e-6

IN_SPLITS = (
    SSM_INNER, SSM_INNER, SSM_GROUPS * SSM_STATE, SSM_GROUPS * SSM_STATE, SSM_HEADS,
    FOX_HEADS * HEAD_DIM, FOX_HEADS * HEAD_DIM, FOX_HEADS * HEAD_DIM, FOX_HEADS,
    MOBA_HEADS * HEAD_DIM, MOBA_HEADS * HEAD_DIM, MOBA_HEADS * HEAD_DIM,
    DSA_HEADS * HEAD_DIM, DSA_HEADS * HEAD_DIM, DSA_HEADS * HEAD_DIM,
    IDX_HEADS * IDX_DIM, IDX_DIM, IDX_HEADS,
)
D_IN = sum(IN_SPLITS)


def rms_norm(x, g):
    x32 = x.astype(jnp.float32)
    y = x32 * lax.rsqrt(jnp.mean(x32 * x32, axis=-1, keepdims=True) + EPS)
    return (y * g.astype(jnp.float32)).astype(x.dtype)

def rope_tables(seq):
    pos = jnp.arange(seq, dtype=jnp.float32)
    inv = ROPE_THETA ** (-jnp.arange(0, HEAD_DIM, 2, dtype=jnp.float32) / HEAD_DIM)
    ang = pos[:, None] * inv[None, :]
    return jnp.cos(ang), jnp.sin(ang)

def apply_rope(t, cos, sin):
    t1, t2 = jnp.split(t.astype(jnp.float32), 2, axis=-1)
    c = cos[None, :, None, :]
    s = sin[None, :, None, :]
    return jnp.concatenate([t1 * c - t2 * s, t2 * c + t1 * s], axis=-1).astype(t.dtype)

def split_heads(t, n_heads):
    return t.reshape(t.shape[0], t.shape[1], n_heads, -1)

def causal_dwconv(u, w, b):
    width = w.shape[0]
    up = jnp.pad(u, ((0, 0), (width - 1, 0), (0, 0)))
    y = lax.conv_general_dilated(up, w[:, None, :], window_strides=(1,), padding='VALID',
                                 dimension_numbers=('NWC', 'WIO', 'NWC'),
                                 feature_group_count=u.shape[-1])
    return y + b

def ssd_chunked(x, dt, a, bmat, cmat):
    bsz, seq, n_heads, hp = x.shape
    pad = (-seq) % SSM_CHUNK
    padl = lambda t: jnp.pad(t, ((0, 0), (0, pad)) + ((0, 0),) * (t.ndim - 2))
    n_chunk = (seq + pad) // SSM_CHUNK
    chunk = lambda t: padl(t).reshape((bsz, n_chunk, SSM_CHUNK) + t.shape[2:])
    xc, dtc, bc, cc = chunk(x), chunk(dt), chunk(bmat), chunk(cmat)
    a_cs = jnp.cumsum((dtc * a).transpose(0, 3, 1, 2), axis=-1)
    xdt = xc * dtc[..., None]
    causal = jnp.tril(jnp.ones((SSM_CHUNK, SSM_CHUNK), dtype=bool))
    seg = a_cs[..., :, None] - a_cs[..., None, :]
    decay = jnp.exp(jnp.where(causal, seg, -jnp.inf))
    scores = jnp.einsum('bclhn,bcshn->bhcls', cc, bc) * decay
    y_diag = jnp.einsum('bhcls,bcshp->bclhp', scores, xdt)
    decay_states = jnp.exp(a_cs[..., -1:] - a_cs)
    states = jnp.einsum('bclhn,bhcl,bclhp->bchpn', bc, decay_states, xdt)
    chunk_decay = jnp.exp(a_cs[..., -1])

    def step(h, inp):
        s_c, d_c = inp
        return h * d_c[..., None, None] + s_c, h

    h0 = jnp.zeros((bsz, n_heads, hp, bmat.shape[-1]), jnp.float32)
    _, prev = lax.scan(step, h0, (states.transpose(1, 0, 2, 3, 4), chunk_decay.transpose(2, 0, 1)))
    prev = prev.transpose(1, 0, 2, 3, 4)
    y_off = jnp.einsum('bclhn,bchpn,bhcl->bclhp', cc, prev, jnp.exp(a_cs))
    y = (y_diag + y_off).reshape(bsz, n_chunk * SSM_CHUNK, n_heads, hp)
    return y[:, :seq]

def mamba2_branch(z, xs, bs, cs, dt_raw, conv_w, conv_b, dt_bias, a_log, d_skip, norm_w):
    bsz, seq, _ = z.shape
    xbc = jax.nn.silu(causal_dwconv(jnp.concatenate([xs, bs, cs], axis=-1), conv_w, conv_b))
    xs, bs, cs = jnp.split(xbc, [SSM_INNER, SSM_INNER + SSM_GROUPS * SSM_STATE], axis=-1)
    rep = SSM_HEADS // SSM_GROUPS
    xh = xs.reshape(bsz, seq, SSM_HEADS, SSM_HEAD_DIM).astype(jnp.float32)
    bh = jnp.repeat(bs.reshape(bsz, seq, SSM_GROUPS, SSM_STATE), rep, axis=2).astype(jnp.float32)
    ch = jnp.repeat(cs.reshape(bsz, seq, SSM_GROUPS, SSM_STATE), rep, axis=2).astype(jnp.float32)
    dt = jax.nn.softplus(dt_raw.astype(jnp.float32) + dt_bias.astype(jnp.float32))
    a = -jnp.exp(a_log.astype(jnp.float32))
    y = ssd_chunked(xh, dt, a, bh, ch) + d_skip.astype(jnp.float32)[:, None] * xh
    y = y.reshape(bsz, seq, SSM_INNER) * jax.nn.silu(z.astype(jnp.float32))
    yg = y.reshape(bsz, seq, SSM_GROUPS, -1)
    yg = yg * lax.rsqrt(jnp.mean(yg * yg, axis=-1, keepdims=True) + EPS)
    return (yg.reshape(bsz, seq, SSM_INNER) * norm_w.astype(jnp.float32)).astype(z.dtype)

def fox_branch(q, k, v, f_logit, f_bias):
    bsz, seq, n_heads, hd = q.shape
    log_f = jax.nn.log_sigmoid(f_logit.astype(jnp.float32) + f_bias.astype(jnp.float32))
    cf = jnp.cumsum(log_f, axis=1).transpose(0, 2, 1)
    kpos = jnp.arange(seq)
    scale = hd ** -0.5

    def block(i):
        start = i * Q_BLOCK
        qb = lax.dynamic_slice_in_dim(q, start, Q_BLOCK, axis=1)
        cq = lax.dynamic_slice_in_dim(cf, start, Q_BLOCK, axis=2)
        qpos = start + jnp.arange(Q_BLOCK)
        logits = jnp.einsum('bqhd,bkhd->bhqk', qb, k).astype(jnp.float32) * scale
        logits = logits + cq[..., :, None] - cf[..., None, :]
        logits = jnp.where(kpos[None, :] <= qpos[:, None], logits, -jnp.inf)
        p = jax.nn.softmax(logits, axis=-1).astype(v.dtype)
        return jnp.einsum('bhqk,bkhd->bqhd', p, v)

    out = lax.map(block, jnp.arange(seq // Q_BLOCK))
    return out.transpose(1, 0, 2, 3, 4).reshape(bsz, seq, n_heads * hd)

def moba_branch(q, k, v):
    bsz, seq, n_heads, hd = q.shape
    n_blk = -(-seq // MOBA_BLOCK)
    pad = n_blk * MOBA_BLOCK - seq
    to_blocks = lambda t: jnp.pad(t, ((0, 0), (0, pad), (0, 0), (0, 0))).reshape(
        bsz, n_blk, MOBA_BLOCK, n_heads, hd).transpose(0, 3, 1, 2, 4)
    k_blk, v_blk = to_blocks(k), to_blocks(v)
    k_mean = jnp.mean(k_blk.astype(jnp.float32), axis=3)
    n_sel = min(MOBA_TOPK, n_blk)
    n_sel_keys = n_sel * MOBA_BLOCK
    scale = hd ** -0.5
    b_ix = jnp.arange(bsz)[:, None, None, None]
    h_ix = jnp.arange(n_heads)[None, None, :, None]
    blk_ids = jnp.arange(n_blk)

    def block(i):
        start = i * MOBA_Q_BLOCK
        qb = lax.dynamic_slice_in_dim(q, start, MOBA_Q_BLOCK, axis=1)
        qpos = start + jnp.arange(MOBA_Q_BLOCK)
        cur = start // MOBA_BLOCK
        gate = jnp.einsum('bqhd,bhnd->bqhn', qb.astype(jnp.float32), k_mean)
        gate = jnp.where(blk_ids < cur, gate, -jnp.inf)
        _, sel = lax.top_k(gate, n_sel)
        sel_ok = sel < cur
        k_sel = k_blk[b_ix, h_ix, sel]
        v_sel = v_blk[b_ix, h_ix, sel]
        s_sel = jnp.einsum('bqhd,bqhnkd->bqhnk', qb, k_sel).astype(jnp.float32) * scale
        s_sel = jnp.where(sel_ok[..., None], s_sel, -jnp.inf)
        k_own = lax.dynamic_index_in_dim(k_blk, cur, axis=2, keepdims=False)
        v_own = lax.dynamic_index_in_dim(v_blk, cur, axis=2, keepdims=False)
        own_pos = cur * MOBA_BLOCK + jnp.arange(MOBA_BLOCK)
        s_own = jnp.einsum('bqhd,bhkd->bqhk', qb, k_own).astype(jnp.float32) * scale
        s_own = jnp.where(own_pos[None, None, None, :] <= qpos[None, :, None, None], s_own, -jnp.inf)
        logits = jnp.concatenate([s_sel.reshape(bsz, MOBA_Q_BLOCK, n_heads, n_sel_keys), s_own], axis=-1)
        p = jax.nn.softmax(logits, axis=-1).astype(v.dtype)
        p_sel = p[..., :n_sel_keys].reshape(bsz, MOBA_Q_BLOCK, n_heads, n_sel, MOBA_BLOCK)
        p_own = p[..., n_sel_keys:]
        return (jnp.einsum('bqhnk,bqhnkd->bqhd', p_sel, v_sel)
                + jnp.einsum('bqhk,bhkd->bqhd', p_own, v_own))

    out = lax.map(block, jnp.arange(seq // MOBA_Q_BLOCK))
    return out.transpose(1, 0, 2, 3, 4).reshape(bsz, seq, n_heads * hd)

def dsa_branch(q, k, v, qi, ki, wi):
    bsz, seq, n_heads, hd = q.shape
    n_keep = min(DSA_TOPK, seq // 4)
    kpos = jnp.arange(seq)
    scale = hd ** -0.5
    idx_scale = IDX_DIM ** -0.5
    w_scale = IDX_HEADS ** -0.5
    b_ix = jnp.arange(bsz)[:, None, None]

    def block(i):
        start = i * Q_BLOCK
        qb = lax.dynamic_slice_in_dim(q, start, Q_BLOCK, axis=1)
        qib = lax.dynamic_slice_in_dim(qi, start, Q_BLOCK, axis=1)
        wib = lax.dynamic_slice_in_dim(wi, start, Q_BLOCK, axis=1)
        qpos = start + jnp.arange(Q_BLOCK)
        isc = jax.nn.relu(jnp.einsum('bqhd,bkd->bqhk', qib, ki).astype(jnp.float32) * idx_scale)
        isc = jnp.einsum('bqh,bqhk->bqk', wib.astype(jnp.float32) * w_scale, isc)
        isc = jnp.where(kpos[None, None, :] <= qpos[None, :, None], isc, -jnp.inf)
        _, sel = lax.top_k(isc, n_keep)
        ok = sel <= qpos[None, :, None]
        k_sel = k[b_ix, sel]
        v_sel = v[b_ix, sel]
        logits = jnp.einsum('bqhd,bqkhd->bqhk', qb, k_sel).astype(jnp.float32) * scale
        logits = jnp.where(ok[:, :, None, :], logits, -jnp.inf)
        p = jax.nn.softmax(logits, axis=-1).astype(v.dtype)
        return jnp.einsum('bqhk,bqkhd->bqhd', p, v_sel)

    out = lax.map(block, jnp.arange(seq // Q_BLOCK))
    return out.transpose(1, 0, 2, 3, 4).reshape(bsz, seq, n_heads * hd)

def hybrid_mixer(h, w_in, conv_w, conv_b, dt_bias, a_log, d_skip, ssm_norm, fox_fbias,
                 w_gate, b_gate, w_branch, w_out, cos, sin):
    bsz, seq, _ = h.shape
    u = h @ w_in
    (z, xs, bs, cs, dt_raw, fq, fk, fv, ff, mq, mk, mv, dq, dk, dv, iq, ik, iw) = jnp.split(
        u, np.cumsum(IN_SPLITS)[:-1].tolist(), axis=-1)
    y_ssm = mamba2_branch(z, xs, bs, cs, dt_raw, conv_w, conv_b, dt_bias, a_log, d_skip, ssm_norm)
    y_fox = fox_branch(split_heads(fq, FOX_HEADS), split_heads(fk, FOX_HEADS),
                       split_heads(fv, FOX_HEADS), ff, fox_fbias)
    y_moba = moba_branch(apply_rope(split_heads(mq, MOBA_HEADS), cos, sin),
                         apply_rope(split_heads(mk, MOBA_HEADS), cos, sin),
                         split_heads(mv, MOBA_HEADS))
    y_dsa = dsa_branch(apply_rope(split_heads(dq, DSA_HEADS), cos, sin),
                       apply_rope(split_heads(dk, DSA_HEADS), cos, sin),
                       split_heads(dv, DSA_HEADS),
                       apply_rope(split_heads(iq, IDX_HEADS), cos, sin),
                       apply_rope(ik[:, :, None, :], cos, sin)[:, :, 0, :],
                       iw)
    ys = jnp.stack([y_ssm, y_fox, y_moba, y_dsa], axis=2)
    proj = jnp.einsum('bsnc,ncd->bsnd', ys, w_branch)
    gates = jax.nn.sigmoid(h @ w_gate + b_gate).reshape(bsz, seq, N_BRANCH, D_MODEL)
    merged = jnp.sum(gates * proj, axis=2)
    return merged @ w_out

def swiglu(h, w_in, w_out):
    g, up = jnp.split(h @ w_in, 2, axis=-1)
    return (jax.nn.silu(g) * up) @ w_out

def second_inputs(seed: int = 0) -> dict:
    key = jax.random.key(seed)
    ks = jax.random.split(key, 19)
    f32 = jnp.float32
    nrm = lambda k, shape, scale: jax.random.normal(k, shape, f32) * scale
    gain = lambda k, shape: 1.0 + 0.05 * jax.random.normal(k, shape, f32)
    dt0 = jnp.exp(jax.random.uniform(ks[5], (DEPTH, SSM_HEADS), f32, math.log(1e-3), math.log(1e-1)))
    return {
        'x': nrm(ks[0], (BATCH, SEQ, D_MODEL), 1.0),
        'norm_mix_pre': gain(ks[1], (DEPTH, D_MODEL)),
        'w_in': nrm(ks[2], (DEPTH, D_MODEL, D_IN), D_MODEL ** -0.5),
        'conv_w': nrm(ks[3], (DEPTH, SSM_CONV, SSM_CONV_CH), SSM_CONV ** -0.5),
        'conv_b': nrm(ks[4], (DEPTH, SSM_CONV_CH), 0.02),
        'dt_bias': dt0 + jnp.log(-jnp.expm1(-dt0)),
        'a_log': jnp.log(jax.random.uniform(ks[6], (DEPTH, SSM_HEADS), f32, 1.0, 16.0)),
        'd_skip': 1.0 + 0.1 * jax.random.normal(ks[7], (DEPTH, SSM_HEADS), f32),
        'ssm_norm': gain(ks[8], (DEPTH, SSM_INNER)),
        'fox_fbias': 3.0 + 0.5 * jax.random.normal(ks[9], (DEPTH, FOX_HEADS), f32),
        'w_gate': nrm(ks[10], (DEPTH, D_MODEL, N_BRANCH * D_MODEL), D_MODEL ** -0.5),
        'b_gate': nrm(ks[11], (DEPTH, N_BRANCH * D_MODEL), 0.02),
        'w_branch': nrm(ks[12], (DEPTH, N_BRANCH, BRANCH_WIDTH, D_MODEL), BRANCH_WIDTH ** -0.5),
        'w_out': nrm(ks[13], (DEPTH, D_MODEL, D_MODEL), D_MODEL ** -0.5),
        'norm_mix_post': gain(ks[14], (DEPTH, D_MODEL)),
        'norm_ffn_pre': gain(ks[15], (DEPTH, D_MODEL)),
        'w_ffn_in': nrm(ks[16], (DEPTH, D_MODEL, 2 * FFN_HIDDEN_2), D_MODEL ** -0.5),
        'w_ffn_out': nrm(ks[17], (DEPTH, FFN_HIDDEN_2, D_MODEL), FFN_HIDDEN_2 ** -0.5),
        'norm_ffn_post': gain(ks[18], (DEPTH, D_MODEL)),
    }

def second_block(x, norm_mix_pre, w_in, conv_w, conv_b, dt_bias, a_log, d_skip, ssm_norm, fox_fbias,
              w_gate, b_gate, w_branch, w_out, norm_mix_post, norm_ffn_pre, w_ffn_in, w_ffn_out,
              norm_ffn_post):
    cos, sin = rope_tables(x.shape[1])
    for l in range(DEPTH):
        h = rms_norm(x, norm_mix_pre[l])
        mix = hybrid_mixer(h, w_in[l], conv_w[l], conv_b[l], dt_bias[l], a_log[l], d_skip[l],
                           ssm_norm[l], fox_fbias[l], w_gate[l], b_gate[l], w_branch[l], w_out[l],
                           cos, sin)
        x = x + rms_norm(mix, norm_mix_post[l])
        h = rms_norm(x, norm_ffn_pre[l])
        x = x + rms_norm(swiglu(h, w_ffn_in[l], w_ffn_out[l]), norm_ffn_post[l])
    return x


def setup_inputs(seed=0):
    out = dict(first_inputs(seed))
    for name, value in second_inputs(seed + 1).items():
        if name != "x":
            out[name + "_2"] = value
    return out


def reference(
    x, c, ctx, c_ctx, ada_w, ada_b, norm_ffn1, norm_mix, norm_ffn2, ffn1_w_in, ffn1_w_out,
    ffn2_w_in, ffn2_w_out, mix_w_out, even_w_in, gla_gate_w, gla_gate_b, gla_norm, odd_w_in,
    conv_w, conv_b, lambda_q1, lambda_k1, lambda_q2, lambda_k2, diff_norm, final_norm,
    norm_mix_pre_2, w_in_2, conv_w_2, conv_b_2, dt_bias_2, a_log_2, d_skip_2, ssm_norm_2,
    fox_fbias_2, w_gate_2, b_gate_2, w_branch_2, w_out_2, norm_mix_post_2, norm_ffn_pre_2,
    w_ffn_in_2, w_ffn_out_2, norm_ffn_post_2,
):
    x = first_block(
        x, c, ctx, c_ctx, ada_w, ada_b, norm_ffn1, norm_mix, norm_ffn2, ffn1_w_in, ffn1_w_out,
        ffn2_w_in, ffn2_w_out, mix_w_out, even_w_in, gla_gate_w, gla_gate_b, gla_norm, odd_w_in,
        conv_w, conv_b, lambda_q1, lambda_k1, lambda_q2, lambda_k2, diff_norm, final_norm,
    )
    return second_block(
        x, norm_mix_pre_2, w_in_2, conv_w_2, conv_b_2, dt_bias_2, a_log_2, d_skip_2, ssm_norm_2,
        fox_fbias_2, w_gate_2, b_gate_2, w_branch_2, w_out_2, norm_mix_post_2, norm_ffn_pre_2,
        w_ffn_in_2, w_ffn_out_2, norm_ffn_post_2,
    )


_drawn_inputs = setup_inputs


def setup_inputs(seed=0):
    import zlib

    import numpy as np

    out = dict(_drawn_inputs(seed))
    spreads = {}
    factors = {'conv_b': 5.297, 'lambda_q1': 3.373, 'lambda_k1': 4.107, 'b_gate_2': 4.516}
    for name, (base, spread) in spreads.items():
        noise = np.random.default_rng([zlib.crc32(name.encode()), seed]).standard_normal(out[name].shape)
        drawn = base * np.exp(spread * noise) if base else spread * noise
        out[name] = jnp.asarray(drawn.astype(out[name].dtype))
    for name, factor in factors.items():
        out[name] = (out[name] * factor).astype(out[name].dtype)
    return out
```

```python
import math
from collections import Counter
from contextlib import ExitStack

import concourse.bass as bass
import numpy as np
from concourse import mybir

F32 = mybir.dt.float32
F32R = mybir.dt.float32r
U32 = mybir.dt.uint32
ALU = mybir.AluOpType
ACT = mybir.ActivationFunctionType
AX = mybir.AxisListType

P = 128
D = 1024
DC = D // P
T = 256
NT = T // P
FFN = 2816
FC = FFN // P
HALVES = (12, 10)
UNIT = 2048
EPS = 1e-6
HD = 64
NEG = -1e30
TAKEN = -3e38
N_MOD = 9
LAM_INIT = 0.8 - 0.6 * math.exp(-0.3)
DSA_KEEP = 64
Z0, DT0, FQ0, FV0, FF0, MQ0, MV0, DQ0, DV0, IQ0, IK0 = (
    0, 1536, 1544, 2568, 3080, 3088, 4112, 4624, 5648, 6160, 6416)


def constants():
    parts = {}
    eye = np.eye(P)
    parts["ident"] = eye
    parts["ones"] = np.ones((P, P))
    parts["eps"] = np.full((P, 1), EPS)
    t = np.arange(T)
    d = np.arange(HD)
    ang = 2 * np.pi * np.outer(d, d) / HD
    parts["dft_cos"] = np.kron(np.eye(2), np.cos(ang))
    parts["dft_sin"] = np.kron(np.eye(2), np.sin(ang))
    ang = 2 * np.pi * (np.outer(t, t) % T) / T
    scale = 1 / math.sqrt(T * HD)
    tiles = lambda a: a.reshape(NT, P, -1).transpose(1, 0, 2).reshape(P, -1)
    parts["dft_tok_cos"] = tiles(np.cos(ang) * scale)
    parts["dft_tok_nsin"] = tiles(-np.sin(ang) * scale)
    f32 = np.float32
    inv = (f32(10000.0) ** (-np.arange(0, HD, 2, dtype=f32) / f32(HD))).astype(f32)
    ang = (t[:, None].astype(f32) * inv[None]).astype(f32)
    row = np.concatenate([ang, ang], 1).T
    parts["rope_cos"] = np.cos(np.concatenate([row, row]))
    parts["rope_sin"] = np.sin(np.concatenate([row, row]))
    swap = np.zeros((P, P))
    for h in range(2):
        for i in range(32):
            swap[64 * h + 32 + i, 64 * h + i] = -1
            swap[64 * h + i, 64 * h + 32 + i] = 1
    parts["rope_swap"] = swap
    inv = (f32(10000.0) ** (-np.arange(16, dtype=f32) / f32(16))).astype(f32)
    rowang = ((t // 64)[:, None].astype(f32) * inv).astype(f32)
    colang = ((t % 64)[:, None].astype(f32) * inv).astype(f32)
    one = np.concatenate([rowang, rowang, colang, colang], 1).T
    parts["axial_cos"] = np.cos(np.concatenate([one, one]))
    parts["axial_sin"] = np.sin(np.concatenate([one, one]))
    swap = np.zeros((P, P))
    for h in range(4):
        for i in range(16):
            swap[32 * h + 16 + i, 32 * h + i] = -1
            swap[32 * h + i, 32 * h + 16 + i] = 1
    parts["axial_swap"] = swap
    i = np.arange(P)
    same = (i[:, None] // 64) == (i[None] // 64)
    parts["cum_fwd"] = (same & (i[:, None] <= i[None])).astype(float)
    parts["cum_bwd"] = (same & (i[:, None] >= i[None])).astype(float)
    parts["cum_all"] = tiles((t[:, None] <= t[None]).astype(float))
    parts["causal"] = np.where(i[None] <= i[:, None], 0.0, NEG)
    parts["causal_t"] = np.where(i[:, None] <= i[None], 0.0, NEG)
    spread = np.zeros((P, 8, P))
    for h in range(8):
        spread[h, h] = 1
    parts["spread"] = spread.reshape(P, -1)
    at, n = {}, 0
    for name, a in parts.items():
        at[name] = (n, n + a.shape[1])
        n += a.shape[1]
    return np.concatenate([np.asarray(a, np.float32) for a in parts.values()], 1), at

NAMES = (
    "x", "c", "ctx", "c_ctx", "ada_w", "ada_b", "norm_ffn1", "norm_mix", "norm_ffn2", "ffn1_w_in",
    "ffn1_w_out", "ffn2_w_in", "ffn2_w_out", "mix_w_out", "even_w_in", "gla_gate_w", "gla_gate_b",
    "gla_norm", "odd_w_in", "conv_w", "conv_b", "lambda_q1", "lambda_k1", "lambda_q2", "lambda_k2",
    "diff_norm", "final_norm", "norm_mix_pre_2", "w_in_2", "conv_w_2", "conv_b_2", "dt_bias_2",
    "a_log_2", "d_skip_2", "ssm_norm_2", "fox_fbias_2", "w_gate_2", "b_gate_2", "w_branch_2",
    "w_out_2", "norm_mix_post_2", "norm_ffn_pre_2", "w_ffn_in_2", "w_ffn_out_2", "norm_ffn_post_2",
)


def build(nc, io, const_at):
    ctx = ExitStack()
    with ctx:
        SLAB = 212704
        base = (nc.sbuf_base + 31) // 32 * 32
        ctx.enter_context(nc.sbuf_tensor("slab", [P, SLAB // 4], F32))

        class Region:

            def __init__(self, start, end=SLAB):
                self.at, self.end = start, end

            def __call__(self, name, shape, dt=F32):
                t = nc.alloc_sbuf_tensor_at(name, shape, dt, offset=base + self.at)
                self.at += (4 * int(np.prod(shape[1:])) + 31) // 32 * 32
                assert self.at <= self.end, (name, self.at, self.end)
                return t

        fixed = Region(0)
        n_const = max(b for _, b in const_at.values())
        consts = fixed("consts", [P, n_const])
        K = lambda name: consts[:, const_at[name][0]:const_at[name][1]]
        vec = fixed("vec", [P, 512])
        modp = fixed("modp", [P, 8 * N_MOD, 4])
        mod = fixed("mod", [P, 8 * N_MOD, 2])
        gains = fixed("gains", [P, 3, DC, 2])
        cond_hl = fixed("cond_hl", [P, DC, 4], F32R)
        cond32 = fixed("cond32", [P, 2, DC])
        bcast = fixed("bcast", [P, 64])
        lam = fixed("lam", [P, 4])
        rstd = fixed("rstd", [P, 2 * T])
        root = fixed("root", [P, 2 * T])
        raw = fixed("raw", [P, 2, UNIT])
        whi = fixed("whi", [P, 2, UNIT], F32R)
        wlo = fixed("wlo", [P, 2, UNIT], F32R)
        wide = fixed.at
        hT = fixed("hT", [P, DC, 2 * T])
        xh_at = fixed.at
        xh = fixed("xh", [P, DC, 2 * T], F32R)
        xl_at = fixed.at
        xl = fixed("xl", [P, DC, 2 * T], F32R)
        overlay = fixed.at

        first = Region(overlay)
        hid_h = first("hid_h", [P, max(HALVES), 2 * T], F32R)
        hid_l = first("hid_l", [P, max(HALVES), 2 * T], F32R)
        ffn_end = first.at
        act32 = first("act32", [P, 2, 2 * T])
        hid32 = first("hid32", [P, 2, 2 * T])
        sq = Region(overlay)("sq", [P, DC, 2 * T])
        start = Region(overlay)
        tok = start("tok", [P, 2 * NT, D])
        rows = start("rows", [P, 4, P])
        lam_in = start("lam_in", [HD, 4])
        lam_prod = start("lam_prod", [HD, 2])
        small_rows = start("small_rows", [1, 64])
        last = Region(overlay)
        y_tok = last("y_tok", [P, NT, D])


        ev = Region(overlay)
        e_z = ev("e_z", [P, 8, 2 * T])
        e_r = ev("e_r", [P, 6, 2 * T])
        e_v = ev("e_v", [P, 2 * NT, 768])
        e_small_at = ev.at
        e_small = ev("e_small", [P, DC, 32])
        e_small_h = ev("e_small_h", [P, DC, 32], F32R)
        e_small_l = ev("e_small_l", [P, DC, 32], F32R)
        e_gtok = ev("e_gtok", [P, 2 * NT, 32])
        e_gT = ev("e_gT", [33, 2 * T])
        e_gw = ev("e_gw", [33, 2, 384])
        e_abs = Region(e_small_at)("e_abs", [P, 384])
        e_log = ev("e_log", [P, 2, 384])
        e_up = ev("e_up", [P, 3, P])
        e_dn = ev("e_dn", [P, 3, P])
        e_kk = ev("e_kk", [P, 3, P])
        e_last = ev("e_last", [P, 2, NT, 3, 2])
        e_kd = ev("e_kd", [P, 3, T])
        e_qd = ev("e_qd", [P, 3, T])
        e_kkT = ev("e_kkT", [P, 2, NT, 384])
        e_S = ev("e_S", [P, 2, 5, 3, P])
        e_ab = e_kkT[:, 0, :, 0:2 * P]
        at_xh = Region(xh_at, xh_at + 8 * T * 2)
        e_att = at_xh("e_att", [P, 2, 512])
        at_xl = Region(xl_at, xl_at + 8 * T * 2)
        e_osq = at_xl("e_osq", [P, 512])
        e_y = at_xl("e_y", [P, 512])

        od = Region(overlay)
        o_z = od("o_z", [P, 6, T])
        o_q = od("o_q", [P, 6, T])
        o_k = od("o_k", [P, 6, 2 * T])
        o_v = od("o_v", [P, 2 * NT, 768])
        o_turn = od("o_turn", [P, 2, T])
        o_p = od("o_p", [P, 2, 2, 2 * T])
        o_aT = od("o_aT", [P, 2, 2 * T])
        o_o = od("o_o", [P, 6, T])
        o_sq = od("o_sq", [P, 6, T])
        o_u = od("o_u", [P, 2, T + 2])
        o_c = od("o_c", [P, 2, T])
        o_st = od("o_st", [P, 12, 6])

        out_at = first.at
        h_out = Region(out_at)("h_out", [P, DC, T])
        hy = Region(overlay)
        h_small = hy("h_small", [P, NT, 84])
        h_yh = hy("h_yh", [P, 4, T], F32R)
        h_yl = hy("h_yl", [P, 4, T], F32R)
        h_merged = hy("h_merged", [P, DC, T])
        h_gate = hy("h_gate", [P, 2, T])
        h_prod = hy("h_prod", [P, 2, T])
        branch = hy.at
        hm = Region(branch)
        m_in = hm("m_in", [P, 12, T])
        m_cv = hm("m_cv", [P, 8, T])
        m_sw = hm("m_sw", [P, DC, 84])
        m_sw_h = hm("m_sw_h", [P, DC, 84], F32R)
        m_sw_l = hm("m_sw_l", [P, DC, 84], F32R)
        m_x = hm("m_x", [P, NT, 512])
        m_dt = hm("m_dt", [P, 6, 16])
        m_cs = hm("m_cs", [8, T])
        m_ncs = hm("m_ncs", [P, 16])
        m_e = hm("m_e", [P, 2, 384])
        m_y = hm("m_y", [P, 4, T])
        m_sq = hm("m_sq", [P, 4, T])
        m_d = hm("m_d", [P, 4])
        ha = Region(branch)
        a_qk = ha("a_qk", [P, 8, T])
        a_v = ha("a_v", [P, NT, 512])
        a_p = ha("a_p", [P, 2, T])
        a_pT = ha("a_pT", [P, 2, T])
        a_st = ha("a_st", [P, 16, 3])
        a_bias = ha("a_bias", [P, 2, 384])
        a_turn = ha("a_turn", [P, 2, T])
        a_f = ha("a_f", [P, 4, 16])
        a_cf = ha("a_cf", [8, T])
        a_iq = ha("a_iq", [P, 2, T])
        a_ik2 = ha("a_ik2", [P, NT, P])
        a_ik = ha("a_ik", [P, T])
        a_isc = ha("a_isc", [P, T])
        a_relu = ha("a_relu", [P, T])
        a_top = ha("a_top", [P, 8])
        a_w = ha("a_w", [P, NT, 4])

        ps = ctx.enter_context(nc.psum_tensor("ps", [P, 8, 512], F32))

        sems = {}

        def S(name):
            if name not in sems:
                sems[name] = ctx.enter_context(nc.semaphore(name))
            return sems[name]

        vec_at, row_parts, n = {}, [], 0
        for name, ap in io["vectors"]:
            r = ap.shape[0]
            vec_at[name] = n
            done = 0
            while done < r:
                m = min(r - done, P - n % P)
                row_parts.append((n // P, n % P, m, ap[done:done + m, :]))
                done += m
                n += m
        n_rows = n
        assert n_rows <= 512
        V = lambda name, i=0, k=1: vec[:, vec_at[name] + i:vec_at[name] + i + k]

        def e_keys(dr, q):
            sl = slice((1 - q) * T, (2 - q) * T)
            return (e_kd, e_qd) if dr == 0 else (e_z[:, 5:8, sl], e_z[:, 2:5, sl])

        class Count:
            def __init__(self):
                self.units = 0
                self.hidden = 0
                self.of = Counter()

            def add(self, **events):
                self.of.update(events)

        CREDIT = 2

        def landed(eng, u_half, slot):
            eng.wait_ge(S(f"raw_landed{slot}"), u_half * 32 + 32)

        def sp_units(sp, c, pairs, source, width):
            def pair(i):
                for s in range(2):
                    w = width[s] if isinstance(width, tuple) else width
                    sp.wait_ge(S("lo_ready"), 2 * i + (c.units + s + 1))
                    for half in range(2):
                        src = source(i, s, half)
                        dst = raw[:, s, half * w // 2:(half + 1) * w // 2]
                        sp.dma_start(dst.rearrange("p (k n) -> p k n", n=src.shape[2]), src)\
                            .then_inc(S(f"raw_landed{s}"), 16)
            if pairs == 1:
                pair(0)
            else:
                with sp.Fori(0, pairs) as i:
                    pair(i)
            c.units += 2 * pairs

        def columns(w, k0, kc, n0, step, width):
            v = w[k0 * P:(k0 + kc) * P, :].rearrange("(c p) n -> p c n", p=P)
            return lambda i, s, half: v[:, half * kc // 2:(half + 1) * kc // 2,
                                        bass.ds(i * (2 * step) + (n0 + step * s), width)]

        def act_split(act, i, s, u):
            landed(act, i + u // 2, s)
            act.wait_ge(S("mm_done"), 2 * i + (u + 1))
            nc.scalar.activation(whi[:, s, :], raw[:, s, :], ACT.Copy).then_inc(S("hi_ready"), 1)

        def dve_split(dve, i, s, u):
            dve.wait_ge(S("hi_ready"), 2 * i + (u + 1))
            nc.vector.tensor_tensor(wlo[:, s, :], raw[:, s, :], whi[:, s, :].bitcast(F32),
                                    ALU.subtract).then_inc(S("lo_ready"), 1)

        def pairs_of(eng, c, pairs, body, ahead=None, final=False):
            def pair(i, last):
                for s in range(2):
                    if ahead is not None and not (last and s == 1):
                        ahead(eng, i, 1 - s, c.units + s + 1)
                    body(i, s)
            rolled = pairs - 1 if final else pairs
            if rolled >= 2:
                with eng.Fori(0, rolled) as i:
                    pair(i, False)
            elif rolled == 1:
                pair(0, False)
            if final:
                pair(pairs - 1, True)
            c.units += 2 * pairs

        def pe_unit_ready(pe, c, i, s):
            pe.wait_ge(S("lo_ready"), 2 * i + (c.units + s + 1 + CREDIT))
            pe.wait_ge(S("evac_done"), 2 * i + (c.units + s + 1))

        def three(dst, w_h, w_l, x_h, x_l, start, stop):
            nc.tensor.matmul(dst, w_h, x_h, start=start, stop=False)
            nc.tensor.matmul(dst, w_h, x_l, start=False, stop=False)
            return nc.tensor.matmul(dst, w_l, x_h, start=False, stop=stop)

        def tiles_of(s, kc, width):
            v = lambda w: w[:, s, 0:kc * width].rearrange("p (k n) -> p k n", n=width)
            return v(whi), v(wlo)

        def pe_blocks(s, kc, n_tok, x_h, x_l, blocks, width, k0=0):
            w_h, w_l = tiles_of(s, kc, width)
            flat = ps[:, 2 * s:2 * s + 2, :].rearrange("p a b -> p (a b)")
            for b in range(blocks):
                for k in range(kc):
                    m = three(flat[:, b * (1024 // max(blocks, 2)):][:, 0:n_tok] if blocks > 1 else flat[:, 0:n_tok],
                              w_h[:, k, b * P:(b + 1) * P], w_l[:, k, b * P:(b + 1) * P],
                              x_h[:, k0 + k, 0:n_tok], x_l[:, k0 + k, 0:n_tok],
                              k == 0, k == kc - 1)
            m.then_inc(S("mm_done"), 1)

        def pe_tokens(s, kc, tok0, n_tiles, x_h, x_l, width):
            w_h, w_l = tiles_of(s, kc, width)
            flat = ps[:, 2 * s:2 * s + 2, :].rearrange("p a b -> p (a b)")
            for t in range(n_tiles):
                tt = slice(tok0 + t * P, tok0 + (t + 1) * P)
                for k in range(kc):
                    m = three(flat[:, t * width:(t + 1) * width], x_h[:, k, tt], x_l[:, k, tt],
                              w_h[:, k, :], w_l[:, k, :], k == 0, k == kc - 1)
            m.then_inc(S("mm_done"), 1)

        def dve_unit_done(dve, c, i, s):
            dve.wait_ge(S("mm_done"), 2 * i + (c.units + s + 1 + CREDIT))

        class Link:

            def __init__(self, eng, name):
                self.eng, self.sem, self.n = eng, S(name), 0

            def __call__(self, ins):
                self.n += 1
                ins.then_inc(self.sem, 1)
                self.eng.wait_ge(self.sem, self.n)

        def fm_evac(dst, c0, n_tok):
            def body(dve, c, i, s):
                dve_unit_done(dve, c, i, s)
                nc.vector.tensor_copy(dst[:, bass.ds(i * 4 + (c0 + 2 * s), 2), 0:n_tok],
                                      ps[:, 2 * s:2 * s + 2, 0:n_tok]).then_inc(S("evac_done"), 1)
            return body


        schedule = []
        g = lambda n: (lambda k, j: gains[:, n, k, j:j + 1])
        sh = lambda n: (lambda k, j: mod[:, 24 * n + k, j:j + 1])
        for layer, mixer, w_in in ((0, "even", io["even_w_in"][0]), (1, "odd", io["odd_w_in"][0])):
            nc_ = 2 - layer
            schedule += [
                ("mod", layer),
                ("norm", hT, 2, sh(0), g(0)),
                ("ffn", io["ffn1_w_in"][layer], io["ffn1_w_out"][layer], 2 * T, 16, False),
                ("norm", hT, 2, sh(1), g(1)),
                (mixer, w_in),
                ("out", io["mix_w_out"][layer], nc_ * T),
                ("norm", hT, nc_, sh(2), g(2)),
                ("ffn", io["ffn2_w_in"][layer], io["ffn2_w_out"][layer], nc_ * T, 64, False),
            ]
        schedule += [("renorm", hT, lambda k: V("final_norm", k))]
        for layer in range(2):
            gain = lambda name, l=layer: (lambda k, j=0: V(name, DC * l + k))
            w_in = io["w_in_2"][layer]
            schedule += [
                ("norm", hT, 1, None, gain("norm_mix_pre_2")),
                ("mamba", layer, w_in),
                ("merge", layer, 0),
                ("attention", layer, 0, w_in),
                ("merge", layer, 1),
                ("attention", layer, 1, w_in),
                ("merge", layer, 2),
                ("attention", layer, 2, w_in),
                ("merge", layer, 3),
                ("wout", layer, io["w_out_2"][layer]),
                ("renorm", h_out, gain("norm_mix_post_2")),
                ("norm", hT, 1, None, gain("norm_ffn_pre_2")),
                ("ffn", io["w_ffn_in_2"][layer], io["w_ffn_out_2"][layer], T, None, layer == 1),
                ("renorm", h_out, gain("norm_ffn_post_2")),
            ]
        schedule += [("store",)]

        block = ctx.enter_context(nc.Block())

        @block.sync
        def _(sp):
            c = Count()
            sp.dma_start(consts[:, :], io["consts"]).then_inc(S("consts_in"), 16)
            for tile, r0, m, src in row_parts:
                sp.dma_start(rows[r0:r0 + m, tile, :], src).then_inc(S("rows_in"), 16)
            for t in range(NT):
                sp.dma_start(tok[:, t, :], io["x"][0, t * P:(t + 1) * P, :]).then_inc(S("tok_in"), 16)
                sp.dma_start(tok[:, NT + t, :], io["ctx"][0, t * P:(t + 1) * P, :]).then_inc(S("tok_in"), 16)
            for j, name in enumerate(("lambda_q1", "lambda_k1", "lambda_q2", "lambda_k2")):
                sp.dma_start(lam_in[:, j:j + 1], io[name].rearrange("a d -> d a")).then_inc(S("lam_landed"), 16)
            for j, name in enumerate(("dt_bias_2", "a_log_2", "fox_fbias_2", "d_skip_2")):
                sp.dma_start(small_rows[0:1, 16 * j:16 * j + 16],
                             io[name].rearrange("(o l) h -> o (l h)", o=1)).then_inc(S("lam_landed"), 16)

            def ffn(w_in, w_out):
                j0 = 0
                for half in HALVES:
                    v = w_in.rearrange("(c p) (g f) -> p c g f", p=P, g=2)
                    sp_units(sp, c, half // 2,
                             lambda i, s, g: v[:, :, g, bass.ds(i * 256 + (j0 + s) * P, P)], UNIT)
                    sp_units(sp, c, 4, columns(w_out, j0, half, 0, P, P), half * P)
                    j0 += half


            def even(w_in):
                sp_units(sp, c, 2, columns(w_in, 0, DC, 0, 256, 256), UNIT)
                sp.wait_ge(S("norm_lo"), c.of["norm_hi"])
                sp.dma_start(e_small[:, :, :], w_in[:, 2560:2592].rearrange("(c p) n -> p c n", p=P))\
                    .then_inc(S("e_small_in"), 16)
                sp.wait_ge(S("e_gw_zero"), 1)
                for dr in range(2):
                    sp.dma_start(e_gw[16 * dr:16 * dr + 16, dr, :], io["gla_gate_w"][0, dr, :, :])\
                        .then_inc(S("e_gw_in"), 16)
                    sp.dma_start(e_gw[32:33, dr, :], io["gla_gate_b"][0, dr:dr + 1, :]).then_inc(S("e_gw_in"), 16)
                v = w_in.rearrange("(c p) n -> p c n", p=P)
                sp_units(sp, c, 3, lambda i, s, half: v[:, 4 * half:4 * half + 4,
                                                        bass.ds(i * 256 + (1792, 1024)[s], 256)], UNIT)

            def odd(w_in):
                v = w_in.rearrange("(c p) n -> p c n", p=P)
                for lo, hi in ((0, 768), (1536, 2304)):
                    sp_units(sp, c, 3, lambda i, s, half: v[:, 4 * half:4 * half + 4,
                                                            bass.ds(i * 256 + (lo, hi)[s], 256)], UNIT)

            def mamba(layer, w_in):
                sp_units(sp, c, 3, columns(w_in, 0, DC, Z0, 256, 256), UNIT)
                sp.wait_ge(S("norm_lo"), c.of["norm_hi"])
                for at, n0, n in ((0, DT0, 8), (8, FF0, 8), (16, IK0, 68)):
                    sp.dma_start(m_sw[:, :, at:at + n], w_in[:, n0:n0 + n].rearrange("(c p) n -> p c n", p=P))\
                        .then_inc(S("m_sw_in"), 16)

            def attention(layer, which, w_in):
                q0, v0 = ((FQ0, FV0), (MQ0, MV0), (DQ0, DV0))[which]
                sp_units(sp, c, 2, columns(w_in, 0, DC, q0, 256, 256), UNIT)
                sp_units(sp, c, 1, columns(w_in, 0, DC, v0, 256, 256), UNIT)
                if which == 2:
                    sp_units(sp, c, 1, columns(w_in, 0, DC, IQ0, P, P), DC * P)

            def merge(layer, n):
                gate = columns(io["w_gate_2"][layer], 0, DC, n * D, P, 256)
                proj = columns(io["w_branch_2"][layer, n], 0, 4, -P, P, 256)
                sp_units(sp, c, 4, lambda i, s, half: (gate, proj)[s](i, s, half), (UNIT, UNIT // 2))

            for stage, *args in schedule:
                if stage == "mod":
                    sp_units(sp, c, 2 * N_MOD, columns(io["ada_w"][args[0]], 0, DC, 0, 256, 256), UNIT)
                elif stage == "norm":
                    c.add(norm_hi=DC * args[1])
                elif stage in ("ffn", "ffn2"):
                    ffn(*args[:2])
                elif stage in ("even", "odd"):
                    {"even": even, "odd": odd}[stage](*args)
                elif stage == "out":
                    sp_units(sp, c, 2, columns(args[0], 0, DC, 0, 256, 256), UNIT)
                elif stage == "mamba":
                    mamba(*args)
                elif stage == "attention":
                    attention(*args)
                elif stage == "merge":
                    merge(*args)
                elif stage == "wout":
                    sp_units(sp, c, 2, columns(args[1], 0, DC, 0, 256, 256), UNIT)
                elif stage == "store":
                    sp.wait_ge(S("y_copied"), 2)
                    for t in range(NT):
                        sp.dma_start(io["out"][0, t * P:(t + 1) * P, :], y_tok[:, t, :]).then_inc(S("stored"), 16)
                    sp.wait_ge(S("stored"), 16 * NT)

        @block.tensor
        def _(pe):
            c = Count()
            pe.sem_inc(S("mm_done"), CREDIT)
            ident = K("ident")
            pe.wait_ge(S("consts_in"), 16)
            pe.wait_ge(S("rows_in"), 16 * len(row_parts))
            for t in range((n_rows + P - 1) // P):
                m = min(P, n_rows - t * P)
                ins = nc.tensor.transpose(ps[:, 7, t * P:t * P + m], rows[0:m, t, :], ident[0:m, 0:m])
            ins.then_inc(S("vec_t"), 1)
            pe.wait_ge(S("tok_in"), 16 * 2 * NT)
            for k in range(DC):
                if k == 7:
                    pe.wait_ge(S("vec_ready"), 1)
                for t in range(2 * NT):
                    ins = nc.tensor.transpose(ps[:, k, t * P:(t + 1) * P], tok[:, t, k * P:(k + 1) * P], ident)
                ins.then_inc(S("h_t"), 1)
            pe.wait_ge(S("lam_prod"), 1)
            pe.wait_ge(S("h_in"), DC)
            nc.tensor.matmul(ps[:, 6, 0:2], K("ones")[0:HD, :], lam_prod[:, :], start=True, stop=True)
            nc.tensor.matmul(ps[:, 6, 64:128], K("ones")[0:1, :], small_rows[0:1, :], start=True, stop=True)\
                .then_inc(S("bcast_mm"), 1)

            def squares(nc_):
                o = c.of
                n = T * nc_
                for k in range(DC):
                    if k % 4 == 0:
                        pe.wait_ge(S("sq_ready"), o["norm"] * 2 + k // 4 + 1)
                    ins = nc.tensor.matmul(ps[:, 4, 0:n], K("ones"), sq[:, k, 0:n], start=k == 0, stop=k == DC - 1)
                ins.then_inc(S("ss_ready"), 1)

            def ffn(n_tok):
                for half in HALVES:
                    def up(i, s):
                        pe_unit_ready(pe, c, i, s)
                        w_h = whi[:, s, :].rearrange("p (g k n) -> p k g n", k=DC, g=2)
                        w_l = wlo[:, s, :].rearrange("p (g k n) -> p k g n", k=DC, g=2)
                        for g in range(2):
                            for k in range(DC):
                                m = three(ps[:, 2 * s + g, 0:n_tok], w_h[:, k, g, :], w_l[:, k, g, :],
                                          xh[:, k, 0:n_tok], xl[:, k, 0:n_tok], k == 0, k == DC - 1)
                        m.then_inc(S("mm_done"), 1)
                    pairs_of(pe, c, half // 2, up)
                    c.hidden += half
                    pe.wait_ge(S("hid_l_ready"), c.hidden + CREDIT)
                    def down(i, s):
                        pe_unit_ready(pe, c, i, s)
                        pe_blocks(s, half, n_tok, hid_h, hid_l, 1, P)
                    pairs_of(pe, c, 4, down)


            def even():
                pairs_of(pe, c, 2, lambda i, s: (pe_unit_ready(pe, c, i, s),
                                                 pe_blocks(s, DC, 2 * T, xh, xl, 2, 256)))
                def r_and_v(i, s):
                    pe_unit_ready(pe, c, i, s)
                    if s == 0:
                        pe_blocks(s, DC, 2 * T, xh, xl, 2, 256)
                    else:
                        pe_tokens(s, DC, 0, 2 * NT, xh, xl, 256)
                pairs_of(pe, c, 3, r_and_v)
                pe.wait_ge(S("e_small_lo"), 1)
                for t in range(2 * NT):
                    tt = slice(t * P, (t + 1) * P)
                    for k in range(DC):
                        m = three(ps[:, 5, t * 32:(t + 1) * 32], xh[:, k, tt], xl[:, k, tt],
                                  e_small_h[:, k, :], e_small_l[:, k, :], k == 0, k == DC - 1)
                m.then_inc(S("e_gates_mm"), 1)
                pe.wait_ge(S("e_gtok"), 1)
                for t in range(2 * NT):
                    m = nc.tensor.transpose(ps[0:32, 6, t * P:(t + 1) * P], e_gtok[:, t, :], ident)
                m.then_inc(S("e_gates_t"), 1)
                pe.wait_ge(S("e_gT"), 1)
                pe.wait_ge(S("e_gw_in"), 16 * 4)
                pe.wait_ge(S("evac_done"), c.units + CREDIT)

                for q in range(2):
                    tile0 = (NT, 0)[q]
                    for n in range(4):
                        it, tile, dr = 4 * q + n, tile0 + n // 2, n % 2
                        if it >= 2:
                            pe.wait_ge(S("e_log"), it - 1)
                        nc.tensor.matmul(ps[:, dr, 0:384], e_gT[:, tile * P:(tile + 1) * P], e_gw[:, dr, :],
                                         start=True, stop=True).then_inc(S("e_logits"), 1)
                        pe.wait_ge(S("e_log"), it + 1)
                        if n == 0 and q:
                            pe.wait_ge(S("e_state"), 8 * q)
                        if it:
                            pe.wait_ge(S("e_exp"), it)
                        for p in range(3):
                            m = nc.tensor.matmul(ps[:, 2, p * P:(p + 1) * P], e_log[:, it % 2, p * P:(p + 1) * P],
                                                 K(("cum_fwd", "cum_bwd")[dr]), start=True, stop=True)
                        m.then_inc(S("e_cum"), 1)
                        pe.wait_ge(S("e_decayed"), it + 1)
                        if it:
                            pe.wait_ge(S("e_kkT"), it)
                        if n == 0 and q:
                            pe.wait_ge(S("e_oroot"), 3 * q)
                        for p in range(3):
                            m = nc.tensor.transpose(ps[:, 3, p * P:(p + 1) * P], e_kk[:, p, :], ident)
                        m.then_inc(S("e_kk_t"), 1)
                    pe.wait_ge(S("e_kkT"), 4 * q + 4)
                    pe.wait_ge(S("e_exp"), 4 * q + 4)
                    if q:
                        pe.wait_ge(S("e_y"), 3 * q)
                    for step in range(8):
                        dr = step % 2
                        ch = step // 2 if dr == 0 else 3 - step // 2
                        if step >= 2 or q:
                            pe.wait_ge(S("e_state"), 8 * q + step - 1)
                        rows_ = slice(64 * (ch % 2), 64 * (ch % 2) + 64)
                        for h in range(6):
                            m = nc.tensor.matmul(
                                ps[64 * (h % 2):64 * (h % 2) + 64, (6, 2)[dr], (h // 2) * P:(h // 2 + 1) * P],
                                e_kkT[rows_, dr, ch // 2, h * 64:(h + 1) * 64],
                                e_v[rows_, tile0 + ch // 2, h * P:(h + 1) * P], start=True, stop=True)
                        m.then_inc(S("e_kv"), 1)
                    pe.wait_ge(S("e_state"), 8 * q + 8)
                    for p in range(3):
                        o = 3 * q + p
                        if o:
                            pe.wait_ge(S("e_att"), o)
                        for dr in range(2):
                            kd, qd = e_keys(dr, q)
                            for t in range(NT):
                                tt = slice(t * P, (t + 1) * P)
                                for h in range(2):
                                    hh = slice(64 * h, 64 * h + 64)
                                    m = nc.tensor.matmul(ps[:, 4 + h, (2 * dr + t) * P:(2 * dr + t + 1) * P],
                                                         kd[hh, p, tt], qd[hh, p, tt], start=True, stop=True)
                        m.then_inc(S("e_att_mm"), 1)
                        pe.wait_ge(S("e_att"), o + 1)
                        if o:
                            pe.wait_ge(S("e_y"), o)
                        for h in range(2):
                            hh = slice(64 * h, 64 * h + 64)
                            for t in range(NT):
                                dst = ps[:, 6 + h, t * P:(t + 1) * P]
                                vv = e_v[:, tile0 + t, (2 * p + h) * P:(2 * p + h + 1) * P]
                                for dr in range(2):
                                    nc.tensor.matmul(dst, vv, e_att[:, h, (2 * dr + t) * P:(2 * dr + t + 1) * P],
                                                     start=dr == 0, stop=False)
                                for dr in range(2):
                                    qd = e_keys(dr, q)[1]
                                    for half in range(2):
                                        ch = 2 * t + half
                                        cc = slice(ch * 64, ch * 64 + 64)
                                        m = nc.tensor.matmul(ps[:, 6 + h, ch * 64:ch * 64 + 64],
                                                             e_S[hh, dr, ch if dr == 0 else 3 - ch, p, :],
                                                             qd[hh, p, cc], start=False,
                                                             stop=dr == 1 and half == 1)
                        m.then_inc(S("e_o"), 1)
                        pe.wait_ge(S("e_osq"), o + 1)
                        if o:
                            pe.wait_ge(S("e_oroot"), o)
                        nc.tensor.matmul(ps[:, 3, :], K("ones"), e_osq[:, :], start=True, stop=True)\
                            .then_inc(S("e_oss"), 1)
                pe.wait_ge(S("e_oroot"), 6)
                for n in range(4):
                    q, k = divmod(n, 2)
                    if n:
                        pe.wait_ge(S("e_fab"), n)
                    for t in range(NT):
                        m = nc.tensor.matmul(ps[:, 0, t * T:(t + 1) * T],
                                             e_z[:, k, q * T + t * P:q * T + (t + 1) * P],
                                             consts[:, const_at["dft_cos"][0]:const_at["dft_sin"][1]],
                                             start=True, stop=True)
                    m.then_inc(S("e_f1"), 1)
                    pe.wait_ge(S("e_fab"), n + 1)
                    if n:
                        pe.wait_ge(S("e_fl"), n)
                    for t in range(NT):
                        nc.tensor.matmul(ps[:, 1, 0:T], e_ab[:, t, 0:P], K("dft_tok_cos")[:, t * T:(t + 1) * T],
                                         start=t == 0, stop=False)
                        m = nc.tensor.matmul(ps[:, 1, 0:T], e_ab[:, t, P:2 * P],
                                             K("dft_tok_nsin")[:, t * T:(t + 1) * T],
                                             start=False, stop=t == NT - 1)
                    m.then_inc(S("e_f2"), 1)
                pe.wait_ge(S("e_fl"), 4)
                pe.wait_ge(S("e_yl"), 6)

            def odd():
                pairs_of(pe, c, 3, lambda i, s: (pe_unit_ready(pe, c, i, s),
                                                 pe_blocks(s, DC, T, xh, xl, 2, 256)))
                def k_and_v(i, s):
                    pe_unit_ready(pe, c, i, s)
                    if s == 0:
                        pe_blocks(s, DC, 2 * T, xh, xl, 2, 256)
                    else:
                        pe_tokens(s, DC, 0, 2 * NT, xh, xl, 256)
                pairs_of(pe, c, 3, k_and_v)
                pe.wait_ge(S("evac_done"), c.units + CREDIT)
                for n in range(6):
                    buf, k = (o_q, 2 * n) if n < 3 else (o_k, 2 * n - 6)
                    for j in range(2):
                        m = nc.tensor.matmul(ps[:, n, j * T:(j + 1) * T], K("axial_swap"), buf[:, k + j, 0:T],
                                             start=True, stop=True)
                    m.then_inc(S("o_swap"), 1)

                def scores(e):
                    h, qt = divmod(e, 2)
                    if e >= 2:
                        pe.wait_ge(S("o_exp"), e - 1)
                    for s in range(2):
                        rr = slice(64 * s, 64 * s + 64)
                        m = nc.tensor.matmul(ps[:, 4 + 2 * (e % 2) + s, :], o_q[rr, h, qt * P:(qt + 1) * P],
                                             o_k[rr, h, :], start=True, stop=True)
                    m.then_inc(S("o_scores"), 1)

                pe.wait_ge(S("o_turned"), 6)
                scores(0)
                for e in range(12):
                    h, qt = divmod(e, 2)
                    if e + 1 < 12:
                        scores(e + 1)
                    pe.wait_ge(S("o_a"), e + 1)
                    if e >= 2:
                        pe.wait_ge(S("o_aT"), e - 1)
                    for kt in range(2 * NT):
                        m = nc.tensor.transpose(ps[:, 2 + e % 2, kt * P:(kt + 1) * P],
                                                o_p[:, e % 2, 0, kt * P:(kt + 1) * P], ident)
                    m.then_inc(S("o_t"), 1)
                    pe.wait_ge(S("o_aT"), e + 1)
                    if qt == 0 and h >= 2:
                        pe.wait_ge(S("o_out"), h - 1)
                    for kt in range(2 * NT):
                        m = nc.tensor.matmul(ps[:, h % 2, qt * P:(qt + 1) * P], o_v[:, kt, h * P:(h + 1) * P],
                                             o_aT[:, e % 2, kt * P:(kt + 1) * P],
                                             start=kt == 0, stop=kt == 2 * NT - 1)
                    m.then_inc(S("o_pv"), 1)
                pe.wait_ge(S("o_sq"), 1)
                for p in range(3):
                    m = nc.tensor.matmul(ps[:, 4 + p, :], K("ones"),
                                         o_sq[:, 2 * p:2 * p + 2, :].rearrange("p a b -> p (a b)"),
                                         start=True, stop=True)
                m.then_inc(S("o_ss"), 1)
                pe.wait_ge(S("o_yl"), 2)

            def fm_pairs(pairs, kc, blocks, width, x_h=xh, x_l=xl):
                pairs_of(pe, c, pairs, lambda i, s: (pe_unit_ready(pe, c, i, s),
                                                     pe_blocks(s, kc, T, x_h, x_l, blocks, width)))

            def mamba(layer):
                fm_pairs(3, DC, 2, 256)
                pe.wait_ge(S("m_sw_lo"), layer + 1)
                for t in range(NT):
                    tt = slice(t * P, (t + 1) * P)
                    for k in range(DC):
                        m = three(ps[:, 5, t * 84:(t + 1) * 84], xh[:, k, tt], xl[:, k, tt],
                                  m_sw_h[:, k, :], m_sw_l[:, k, :], k == 0, k == DC - 1)
                m.then_inc(S("m_small_mm"), 1)
                pe.wait_ge(S("evac_done"), c.units + CREDIT)
                pe.wait_ge(S("m_dta"), layer + 1)
                for t in range(NT):
                    nc.tensor.matmul(ps[0:8, 2, 0:T], m_dt[:, 4, 8 * t:8 * t + 8], K("cum_all")[:, t * T:(t + 1) * T],
                                     start=t == 0, stop=t == NT - 1)
                for o in range(NT):
                    for t in range(NT):
                        m = nc.tensor.matmul(ps[:, 3, 8 * o:8 * o + 8],
                                             K("cum_all")[:, t * T + o * P:t * T + (o + 1) * P],
                                             m_dt[:, 4, 8 * t:8 * t + 8], start=t == 0, stop=t == NT - 1)
                m.then_inc(S("m_cs_mm"), 1)
                pe.wait_ge(S("m_conv"), layer + 1)
                pe.wait_ge(S("m_small"), layer + 1)
                for t in range(NT):
                    for k in range(4):
                        m = nc.tensor.transpose(ps[:, 4 + t, k * P:(k + 1) * P], m_cv[:, k, t * P:(t + 1) * P], ident)
                m.then_inc(S("m_x_t"), 1)
                for g in range(2):
                    for t in range(NT):
                        m = nc.tensor.matmul(ps[:, g, t * T:(t + 1) * T], m_cv[:, 4 + g, t * P:(t + 1) * P],
                                             m_cv[:, 6 + g, :], start=True, stop=True)
                m.then_inc(S("m_cb"), 1)
                pe.wait_ge(S("m_x"), layer + 1)
                pe.wait_ge(S("m_cs"), layer + 1)

                def spread(h):
                    if h >= 2:
                        pe.wait_ge(S("m_seg"), 8 * layer + h - 1)
                    nc.tensor.matmul(ps[:, 4 + h % 2, 0:T], K("spread")[0:8, h * P:(h + 1) * P], m_cs[:, :],
                                     start=True, stop=True).then_inc(S("m_row"), 1)
                spread(0)
                for h in range(8):
                    if h + 1 < 8:
                        spread(h + 1)
                    pe.wait_ge(S("m_score"), 8 * layer + h + 1)
                    p = h // 2
                    if h % 2 == 0 and p >= 2:
                        pe.wait_ge(S("m_y"), 4 * layer + p - 1)
                    hh = slice(64 * (h % 2), 64 * (h % 2) + 64)
                    nc.tensor.matmul(ps[hh, 6 + p % 2, 0:T], m_x[:, 0, h * 64:(h + 1) * 64], m_e[:, h % 2, 0:T],
                                     start=True, stop=False)
                    nc.tensor.matmul(ps[hh, 6 + p % 2, P:T], m_x[:, 1, h * 64:(h + 1) * 64], m_e[:, h % 2, T:T + P],
                                     start=False, stop=True).then_inc(S("m_o"), 1)
                pe.wait_ge(S("m_sq"), layer + 1)
                for g in range(2):
                    for k in range(2):
                        m = nc.tensor.matmul(ps[:, 2 + g, 0:T], K("ones"), m_sq[:, 2 * g + k, :],
                                             start=k == 0, stop=k == 1)
                m.then_inc(S("m_ss"), 1)
                pe.wait_ge(S("m_yl"), layer + 1)

            def turn(buf, k, n_chunks, bank):
                for j in range(n_chunks):
                    x = buf[:, k + j, :] if n_chunks == 2 else buf[:, :]
                    m = nc.tensor.matmul(ps[:, bank, j * T:(j + 1) * T], K("rope_swap"), x, start=True, stop=True)
                m.then_inc(S("a_swap"), 1)

            def attention(layer, which):
                a = 3 * layer + which
                fm_pairs(2, DC, 2, 256)
                pairs_of(pe, c, 1, lambda i, s: (pe_unit_ready(pe, c, i, s), pe_tokens(s, DC, 0, NT, xh, xl, 256)))
                if which == 2:
                    fm_pairs(1, DC, 1, P)
                pe.wait_ge(S("evac_done"), c.units + CREDIT)
                if which == 0:
                    pe.wait_ge(S("a_logf"), layer + 1)
                    for t in range(NT):
                        nc.tensor.matmul(ps[0:8, 2, 0:T], a_f[:, 2, 8 * t:8 * t + 8],
                                         K("cum_all")[:, t * T:(t + 1) * T], start=t == 0, stop=t == NT - 1)
                    for o in range(NT):
                        for t in range(NT):
                            m = nc.tensor.matmul(ps[:, 3, 8 * o:8 * o + 8],
                                                 K("cum_all")[:, t * T + o * P:t * T + (o + 1) * P],
                                                 a_f[:, 2, 8 * t:8 * t + 8], start=t == 0, stop=t == NT - 1)
                    m.then_inc(S("a_cf_mm"), 1)
                    pe.wait_ge(S("a_cf"), layer + 1)
                else:
                    r0 = 10 * layer + (0, 0, 4)[which]
                    for n in range(4):
                        turn(a_qk, 2 * n, 2, n)
                    if which == 2:
                        turn(a_iq, 0, 2, 4)
                        pe.wait_ge(S("a_ik2"), layer + 1)
                        for t in range(NT):
                            m = nc.tensor.transpose(ps[:, 6, t * P:(t + 1) * P], a_ik2[:, t, :], ident)
                        m.then_inc(S("a_ik_t"), 1)
                        pe.wait_ge(S("a_ik"), layer + 1)
                        turn(a_ik, 0, 1, 5)
                    pe.wait_ge(S("a_turned"), r0 + (0, 4, 6)[which])
                    if which == 2:
                        for qt in range(NT):
                            if qt:
                                pe.wait_ge(S("a_isc"), NT * layer + qt)
                            for h in range(4):
                                hh = slice(64 * (h % 2), 64 * (h % 2) + 64)
                                m = nc.tensor.matmul(ps[:, 4 + h, 0:(qt + 1) * P], a_iq[hh, h // 2, qt * P:(qt + 1) * P],
                                                     a_ik[hh, 0:(qt + 1) * P], start=True, stop=True)
                            m.then_inc(S("a_idx"), 1)
                        pe.wait_ge(S("a_isc"), NT * layer + NT)

                def spread(h):
                    if h >= 2:
                        pe.wait_ge(S("a_bias"), 8 * layer + h - 1)
                    nc.tensor.matmul(ps[:, 2 + h % 2, 0:T], K("spread")[0:8, h * P:(h + 1) * P], a_cf[:, :],
                                     start=True, stop=True).then_inc(S("a_row"), 1)

                def scores(e):
                    h, qt = divmod(e, 2)
                    if which == 0 and qt == 0:
                        spread(h)
                    if e >= 2:
                        pe.wait_ge(S("a_max"), 16 * a + e - 1)
                    hh = slice(64 * (h % 2), 64 * (h % 2) + 64)
                    nc.tensor.matmul(ps[:, 4 + e % 2, 0:(qt + 1) * P], a_qk[hh, h // 2, qt * P:(qt + 1) * P],
                                     a_qk[hh, 4 + h // 2, 0:(qt + 1) * P], start=True, stop=True)\
                        .then_inc(S("a_scores"), 1)

                scores(0)
                for e in range(16):
                    h, qt = divmod(e, 2)
                    p = h // 2
                    if e + 1 < 16:
                        scores(e + 1)
                    pe.wait_ge(S("a_p"), 16 * a + e + 1)
                    if e >= 2:
                        pe.wait_ge(S("a_pT"), 16 * a + e - 1)
                    for kt in range(qt + 1):
                        m = nc.tensor.transpose(ps[:, 6 + e % 2, kt * P:(kt + 1) * P],
                                                a_p[:, e % 2, kt * P:(kt + 1) * P], ident)
                    m.then_inc(S("a_t"), 1)
                    pe.wait_ge(S("a_pT"), 16 * a + e + 1)
                    if e % 4 == 0 and p >= 2:
                        pe.wait_ge(S("a_yl"), 4 * a + p - 1)
                    hh = slice(64 * (h % 2), 64 * (h % 2) + 64)
                    for kt in range(qt + 1):
                        m = nc.tensor.matmul(ps[hh, p % 2, qt * P:(qt + 1) * P], a_v[:, kt, h * 64:(h + 1) * 64],
                                             a_pT[:, e % 2, kt * P:(kt + 1) * P], start=kt == 0, stop=kt == qt)
                    m.then_inc(S("a_pv"), 1)
                pe.wait_ge(S("a_yl"), 4 * a + 4)

            def merge(layer, n):
                def unit(i, s):
                    pe_unit_ready(pe, c, i, s)
                    if s == 0:
                        pe_blocks(0, DC, T, xh, xl, 2, 256)
                    else:
                        pe_blocks(1, 4, T, h_yh, h_yl, 2, 256)
                pairs_of(pe, c, 4, unit)

            for stage, *args in schedule:
                if stage == "mod":
                    if args[0] == 0:
                        pe.wait_ge(S("cond_ready"), 1)
                        pe.wait_ge(S("bcast_ready"), 1)
                    def unit(i, s):
                        pe_unit_ready(pe, c, i, s)
                        w_h, w_l = tiles_of(s, DC, 256)
                        for b in range(2):
                            for k in range(DC):
                                dst = ps[:, 2 * s, 4 * b:4 * b + 4]
                                nc.tensor.matmul(dst, w_h[:, k, b * P:(b + 1) * P], cond_hl[:, k, :],
                                                 start=k == 0, stop=False)
                                m = nc.tensor.matmul(dst, w_l[:, k, b * P:(b + 1) * P], cond_hl[:, k, :],
                                                     start=False, stop=k == DC - 1)
                        m.then_inc(S("mm_done"), 1)
                    pairs_of(pe, c, 2 * N_MOD, unit)
                elif stage == "norm":
                    squares(args[1])
                    c.add(norm=1, norm_hi=DC * args[1])
                    pe.wait_ge(S("norm_lo"), c.of["norm_hi"])
                elif stage == "renorm":
                    squares(1)
                    c.add(norm=1, renorm=1)
                elif stage == "ffn":
                    ffn(args[2])
                elif stage == "even":
                    even()
                elif stage == "odd":
                    odd()
                elif stage == "out":
                    pairs_of(pe, c, 2, lambda i, s: (pe_unit_ready(pe, c, i, s),
                                                     pe_blocks(s, DC, args[1], xh, xl, 2, 256)))
                elif stage == "mamba":
                    mamba(args[0])
                elif stage == "attention":
                    attention(args[0], args[1])
                elif stage == "merge":
                    merge(*args)
                elif stage == "wout":
                    pe.wait_ge(S("h_merged_lo"), args[0] + 1)
                    fm_pairs(2, DC, 2, 256)
                elif stage == "store":
                    pe.wait_ge(S("evac_done"), c.units + CREDIT)
                    if c.of["renorm"]:
                        pe.wait_ge(S("renormed"), c.of["renorm"])
                    for t in range(NT):
                        for k in range(DC):
                            ins = nc.tensor.transpose(ps[:, 2 * t + k // 4, (k % 4) * P:(k % 4 + 1) * P],
                                                      hT[:, k, t * P:(t + 1) * P], ident)
                        ins.then_inc(S("y_t"), 1)

        @block.scalar
        def _(act):
            c = Count()
            link = Link(act, "act_link")
            act.wait_ge(S("vec_ready"), 1)
            nc.scalar.activation(cond32[:, 0, :], V("c", 0, DC), ACT.Silu)
            nc.scalar.activation(cond32[:, 1, :], V("c_ctx", 0, DC), ACT.Silu).then_inc(S("cond32"), 1)
            act.wait_ge(S("cond32"), 1)
            nc.scalar.activation(cond_hl[:, :, 0:2], cond32[:, :, :].rearrange("p j k -> p k j"), ACT.Copy)\
                .then_inc(S("cond_hi"), 1)
            act.wait_ge(S("bcast_mm"), 1)
            nc.scalar.activation(lam[:, 0:2], ps[:, 6, 0:2], ACT.Exp).then_inc(S("lam_exp"), 1)
            act_split(act, 0, 0, 0)

            def root_of_squares(src, nc_):
                o = c.of
                n = T * nc_
                act.wait_ge(S("evac_done"), c.units + CREDIT)
                if o["renorm"]:
                    act.wait_ge(S("renormed"), o["renorm"])
                if o["norm_hi"]:
                    act.wait_ge(S("norm_lo"), o["norm_hi"])
                for q in range(2):
                    nc.scalar.activation(sq[:, 4 * q:4 * q + 4, 0:n], src[:, 4 * q:4 * q + 4, 0:n],
                                         ACT.Square).then_inc(S("sq_ready"), 1)
                act.wait_ge(S("ss_ready"), o["norm"] + 1)
                nc.scalar.activation(root[:, 0:n], ps[:, 4, 0:n], ACT.Sqrt, bias=K("eps"), scale=1.0 / D)\
                    .then_inc(S("root_ready"), 1)

            def norm(src, nc_, shift, gain):
                o = c.of
                root_of_squares(src, nc_)
                for k in range(DC):
                    for j in range(nc_):
                        e = o["norm_hi"] + k * nc_ + j
                        act.wait_ge(S("norm_prod"), e + 1)
                        sl = slice(j * T, (j + 1) * T)
                        nc.scalar.activation(xh[:, k, sl], sq[:, k, sl], ACT.Identity,
                                             bias=shift(k, j) if shift else 0.0).then_inc(S("norm_hi"), 1)
                c.add(norm=1, norm_hi=DC * nc_)

            def ffn(n_tok, final):
                for h, half in enumerate(HALVES):
                    a0 = c.hidden
                    def up(i, s):
                        act.wait_ge(S("mm_done"), 2 * i + (c.units + s + 1 + CREDIT))
                        nc.scalar.activation(act32[:, s, 0:n_tok], ps[:, 2 * s, 0:n_tok], ACT.Silu)\
                            .then_inc(S("act_ready"), 1)
                        act.wait_ge(S("evac_done"), 2 * i + (c.units + s + 1 + CREDIT))
                        nc.scalar.activation(hid_h[:, bass.ds(i * 2 + s, 1), 0:n_tok],
                                             hid32[:, s:s + 1, 0:n_tok], ACT.Copy).then_inc(S("hid_h_ready"), 1)
                    pairs_of(act, c, half // 2, up, ahead=act_split)
                    c.hidden += half
                    pairs_of(act, c, 4, lambda i, s: None, ahead=act_split, final=final and h == 1)


            def even():
                pairs_of(act, c, 2, lambda i, s: None, ahead=act_split)
                pairs_of(act, c, 3, lambda i, s: None, ahead=act_split)
                act.wait_ge(S("e_small_in"), 16)
                nc.scalar.activation(e_small_h[:, :, :], e_small[:, :, :], ACT.Copy).then_inc(S("e_small_hi"), 1)
                act.wait_ge(S("evac_done"), c.units + CREDIT)
                nc.scalar.activation(e_r[:, :, :], e_r[:, :, :], ACT.Silu).then_inc(S("e_silu"), 1)
                for q in range(2):
                    for n in range(4):
                        it, dr = 4 * q + n, n % 2
                        act.wait_ge(S("e_logits"), it + 1)
                        if it:
                            act.wait_ge(S("e_log"), it)
                        link(nc.scalar.activation(e_abs[:, :], ps[:, dr, 0:384], ACT.Abs))
                        link(nc.scalar.activation(e_abs[:, :], e_abs[:, :], ACT.Exp, scale=-1.0))
                        nc.scalar.activation(e_abs[:, :], e_abs[:, :], ACT.Ln, bias=1.0).then_inc(S("e_ln"), 1)
                        act.wait_ge(S("e_cum"), it + 1)
                        if it:
                            act.wait_ge(S("e_decayed"), it)
                        flat = ps[:, 2, 0:384].rearrange("p (a b) -> p a b", b=P)
                        nc.scalar.activation(e_up[:, :, :], flat, ACT.Exp, scale=1.0 / 16)
                        nc.scalar.activation(e_dn[:, :, :], flat, ACT.Exp, scale=-1.0 / 16).then_inc(S("e_exp"), 1)
                        act.wait_ge(S("e_kk_t"), it + 1)
                        if q and n == 0:
                            act.wait_ge(S("e_kv"), 8 * q)
                        nc.scalar.activation(e_kkT[:, dr, n // 2, :], ps[:, 3, 0:384], ACT.Copy)\
                            .then_inc(S("e_kkT"), 1)
                    for p in range(3):
                        o = 3 * q + p
                        act.wait_ge(S("e_o"), o + 1)
                        if o:
                            act.wait_ge(S("e_oss"), o)
                        nc.scalar.activation(e_osq[:, :].rearrange("p (a b) -> p a b", a=2), ps[:, 6:8, 0:T], ACT.Square).then_inc(S("e_osq"), 1)
                        act.wait_ge(S("e_oss"), o + 1)
                        if o:
                            act.wait_ge(S("e_y"), o)
                        nc.scalar.activation(root[:, :], ps[:, 3, :], ACT.Sqrt, bias=K("eps"), scale=1.0 / P)\
                            .then_inc(S("e_oroot"), 1)
                        act.wait_ge(S("e_y"), o + 1)
                        sl = slice((1 - q) * T, (2 - q) * T)
                        nc.scalar.activation(xh[:, 2 + 2 * p:4 + 2 * p, sl],
                                             e_y[:, :].rearrange("p (a b) -> p a b", a=2), ACT.Copy)\
                            .then_inc(S("e_yh"), 1)
                act.wait_ge(S("e_yl"), 6)
                for n in range(4):
                    q, k = divmod(n, 2)
                    act.wait_ge(S("e_f1"), n + 1)
                    if n:
                        act.wait_ge(S("e_f2"), n)
                    nc.scalar.activation(e_ab, ps[:, 0, :].rearrange("p (a b) -> p a b", a=NT), ACT.Copy)\
                        .then_inc(S("e_fab"), 1)
                    act.wait_ge(S("e_f2"), n + 1)
                    nc.scalar.activation(xh[:, k, q * T:(q + 1) * T], ps[:, 1, 0:T], ACT.Copy)\
                        .then_inc(S("e_fh"), 1)

            def odd():
                pairs_of(act, c, 3, lambda i, s: None, ahead=act_split)
                pairs_of(act, c, 3, lambda i, s: None, ahead=act_split)
                for e in range(14):
                    if e < 12:
                        act.wait_ge(S("o_max"), e + 1)
                        if e >= 2:
                            act.wait_ge(S("o_t"), e - 1)
                        for s in range(2):
                            ins = nc.scalar.activation(o_p[:, e % 2, s, :], ps[:, 4 + 2 * (e % 2) + s, :], ACT.Exp,
                                                       bias=o_st[:, e, s:s + 1], scale=HD ** -0.5,
                                                       accum_out=o_st[:, e, 2 + s:3 + s])
                        ins.then_inc(S("o_exp"), 1)
                    if 1 <= e <= 12:
                        a = e - 1
                        act.wait_ge(S("o_t"), a + 1)
                        if a >= 2:
                            act.wait_ge(S("o_pv"), a - 1)
                        nc.scalar.activation(o_aT[:, a % 2, :], ps[:, 2 + a % 2, :], ACT.Copy).then_inc(S("o_aT"), 1)
                    if e >= 2 and e % 2 == 1:
                        h = (e - 3) // 2
                        act.wait_ge(S("o_pv"), 2 * h + 2)
                        nc.scalar.activation(o_o[:, h, :], ps[:, h % 2, 0:T], ACT.Copy).then_inc(S("o_out"), 1)
                act.wait_ge(S("o_out"), 6)
                nc.scalar.activation(o_sq[:, :, :], o_o[:, :, :], ACT.Square).then_inc(S("o_sq"), 1)
                act.wait_ge(S("o_ss"), 1)
                nc.scalar.activation(o_sq[:, :, :], ps[:, 4:7, :].rearrange("p a (b n) -> p (a b) n", n=T),
                                     ACT.Sqrt, bias=K("eps"), scale=1.0 / P).then_inc(S("o_root"), 1)
                act.wait_ge(S("o_conv"), 1)
                nc.scalar.activation(xh[:, 0:2, 0:T], o_c[:, :, :], ACT.Copy).then_inc(S("o_yh"), 1)
                act.wait_ge(S("o_y"), 1)
                nc.scalar.activation(xh[:, 2:8, 0:T], o_o[:, :, :], ACT.Copy).then_inc(S("o_yh"), 1)

            def mamba(layer):
                pairs_of(act, c, 3, lambda i, s: None, ahead=act_split)
                act.wait_ge(S("m_sw_in"), 48 * (layer + 1))
                nc.scalar.activation(m_sw_h[:, :, :], m_sw[:, :, :], ACT.Copy).then_inc(S("m_sw_hi"), 1)
                act.wait_ge(S("m_dt_in"), layer + 1)
                link(nc.scalar.activation(m_dt[:, 1, :], m_dt[:, 0, :], ACT.Abs))
                nc.scalar.activation(m_dt[:, 1, :], m_dt[:, 1, :], ACT.Exp, scale=-1.0).then_inc(S("m_dt_exp"), 1)
                nc.scalar.activation(m_dt[:, 5, 0:8], bcast[:, 16 + 8 * layer:24 + 8 * layer], ACT.Exp)
                act.wait_ge(S("m_dt_one"), layer + 1)
                nc.scalar.activation(m_dt[:, 3, :], m_dt[:, 2, :], ACT.Ln).then_inc(S("m_dt_ln"), 1)
                act.wait_ge(S("evac_done"), c.units + CREDIT)
                nc.scalar.activation(m_in[:, 0:4, :], m_in[:, 0:4, :], ACT.Silu)
                act.wait_ge(S("m_taps"), layer + 1)
                nc.scalar.activation(m_cv[:, :, :], m_cv[:, :, :], ACT.Silu).then_inc(S("m_conv"), 1)
                act.wait_ge(S("m_x_t"), layer + 1)
                nc.scalar.activation(m_x[:, :, :], ps[:, 4:6, :], ACT.Copy).then_inc(S("m_x"), 1)
                for h in range(8):
                    act.wait_ge(S("m_seg"), 8 * layer + h + 1)
                    nc.scalar.activation(m_e[:, h % 2, :], m_e[:, h % 2, :], ACT.Exp).then_inc(S("m_exp"), 1)
                act.wait_ge(S("m_gated"), layer + 1)
                nc.scalar.activation(m_sq[:, :, :], m_y[:, :, :], ACT.Square).then_inc(S("m_sq"), 1)
                act.wait_ge(S("m_ss"), layer + 1)
                nc.scalar.activation(root[:, :].rearrange("p (a b) -> p a b", a=2), ps[:, 2:4, 0:T], ACT.Sqrt,
                                     bias=K("eps"), scale=1.0 / T).then_inc(S("m_root"), 1)
                act.wait_ge(S("m_normed"), layer + 1)
                act.wait_ge(S("mm_done"), c.units + CREDIT)
                nc.scalar.activation(h_yh[:, :, :], m_y[:, :, :], ACT.Copy).then_inc(S("m_yh"), 1)

            def attention(layer, which):
                a = 3 * layer + which
                for pairs in (2, 1) + (1,) * (which == 2):
                    pairs_of(act, c, pairs, lambda i, s: None, ahead=act_split)
                if which == 0:
                    act.wait_ge(S("a_f_in"), layer + 1)
                    link(nc.scalar.activation(a_f[:, 1, :], a_f[:, 0, :], ACT.Abs))
                    link(nc.scalar.activation(a_f[:, 1, :], a_f[:, 1, :], ACT.Exp, scale=-1.0))
                    nc.scalar.activation(a_f[:, 1, :], a_f[:, 1, :], ACT.Ln, bias=1.0).then_inc(S("a_f_ln"), 1)
                for e in range(18):
                    if e < 16:
                        nk = (e % 2 + 1) * P
                        act.wait_ge(S("a_max"), 16 * a + e + 1)
                        nc.scalar.activation(a_p[:, e % 2, 0:nk], a_p[:, e % 2, 0:nk], ACT.Exp, bias=a_st[:, e, 0:1],
                                             accum_out=a_st[:, e, 1:2]).then_inc(S("a_exp"), 1)
                    if 1 <= e <= 16:
                        b = e - 1
                        nk = (b % 2 + 1) * P
                        act.wait_ge(S("a_t"), 16 * a + b + 1)
                        if b >= 2:
                            act.wait_ge(S("a_pv"), 16 * a + b - 1)
                        nc.scalar.activation(a_pT[:, b % 2, 0:nk], ps[:, 6 + b % 2, 0:nk], ACT.Copy)\
                            .then_inc(S("a_pT"), 1)
                    if e >= 5 and e % 4 == 1:
                        p = (e - 5) // 4
                        act.wait_ge(S("a_pv"), 16 * a + 4 * p + 4)
                        nc.scalar.activation(h_yh[:, p, :], ps[:, p % 2, 0:T], ACT.Copy).then_inc(S("a_yh"), 1)

            def merge(layer, n):
                def unit(i, s):
                    if s == 0:
                        act.wait_ge(S("evac_done"), 2 * i + (c.units + 1 + CREDIT))
                        b0 = vec_at["b_gate_2"] + 32 * layer + DC * n
                        for b in range(2):
                            ins = nc.scalar.activation(h_gate[:, b, :], h_gate[:, b, :], ACT.Sigmoid,
                                                       bias=vec[:, bass.ds(i * 2 + (b0 + b), 1)])
                        ins.then_inc(S("h_gate"), 1)
                pairs_of(act, c, 4, unit, ahead=act_split)

            def merged(layer):
                act.wait_ge(S("h_merged"), 12 * (layer + 1))
                act.wait_ge(S("mm_done"), c.units + CREDIT)
                nc.scalar.activation(xh[:, :, 0:T], h_merged[:, :, :], ACT.Copy).then_inc(S("h_merged_hi"), 1)

            for stage, *args in schedule:
                if stage == "mod":
                    pairs_of(act, c, 2 * N_MOD, lambda i, s: None, ahead=act_split)
                    act.wait_ge(S("mod_ready"), args[0] + 1)
                elif stage == "norm":
                    norm(*args)
                elif stage == "renorm":
                    root_of_squares(args[0], 1)
                    c.add(norm=1, renorm=1)
                elif stage == "ffn":
                    ffn(args[2], args[4])
                elif stage == "even":
                    even()
                elif stage == "odd":
                    odd()
                elif stage == "out":
                    pairs_of(act, c, 2, lambda i, s: None, ahead=act_split)
                elif stage == "mamba":
                    mamba(args[0])
                elif stage == "attention":
                    attention(args[0], args[1])
                elif stage == "merge":
                    merge(*args)
                elif stage == "wout":
                    merged(args[0])
                    pairs_of(act, c, 2, lambda i, s: None, ahead=act_split)

        @block.vector
        def _(dve):
            c = Count()
            link = Link(dve, "dve_link")
            dve.sem_inc(S("lo_ready"), CREDIT)
            dve.sem_inc(S("evac_done"), CREDIT)
            dve.sem_inc(S("hid_l_ready"), CREDIT)
            dve.wait_ge(S("vec_t"), 1)
            nc.vector.tensor_copy(vec[:, 0:n_rows], ps[:, 7, 0:n_rows]).then_inc(S("vec_ready"), 1)
            dve.wait_ge(S("lam_landed"), 16 * 8)
            for j in range(2):
                ins = nc.vector.tensor_tensor(lam_prod[:, j:j + 1], lam_in[:, 2 * j:2 * j + 1],
                                              lam_in[:, 2 * j + 1:2 * j + 2], ALU.mult)
            ins.then_inc(S("lam_prod"), 1)
            for k in range(DC):
                dve.wait_ge(S("h_t"), k + 1)
                nc.vector.tensor_copy(hT[:, k, :], ps[:, k, :]).then_inc(S("h_in"), 1)
            dve.wait_ge(S("cond_hi"), 1)
            nc.vector.tensor_tensor(cond_hl[:, :, 2:4], cond32[:, :, :].rearrange("p j k -> p k j"),
                                    cond_hl[:, :, 0:2].bitcast(F32), ALU.subtract).then_inc(S("cond_ready"), 1)
            dve.wait_ge(S("lam_exp"), 1)
            link(nc.vector.tensor_tensor(lam[:, 2:3], lam[:, 1:2], lam[:, 0:1], ALU.subtract))
            link(nc.vector.tensor_scalar(lam[:, 2:3], lam[:, 2:3], -LAM_INIT, None, ALU.add))
            dve.wait_ge(S("bcast_mm"), 1)
            nc.vector.tensor_copy(bcast[:, :], ps[:, 6, 64:128]).then_inc(S("bcast_ready"), 1)
            dve_split(dve, 0, 0, 0)

            def mod_ready(layer):
                dve.wait_ge(S("evac_done"), c.units + CREDIT)
                link(nc.vector.tensor_tensor(mod[:, :, :], modp[:, :, 0:2], modp[:, :, 2:4], ALU.add))
                for j in range(2):
                    link(nc.vector.tensor_tensor(mod[:, :, j], mod[:, :, j], V("ada_b", 72 * layer, 72), ALU.add))
                for n, name in enumerate(("norm_ffn1", "norm_mix", "norm_ffn2")):
                    for j in range(2):
                        link(nc.vector.scalar_tensor_tensor(
                            out=gains[:, n, :, j], in0=mod[:, 24 * n + 8:24 * n + 16, j], scalar=1.0,
                            in1=V(name, DC * layer, DC), op0=ALU.add, op1=ALU.mult))
                link(nc.vector.tensor_scalar(mod[:, 16:24, :], mod[:, 16:24, :], 0.5, None, ALU.mult))
                nc.vector.tensor_scalar(mod[:, 64:72, :], mod[:, 64:72, :], 0.5, None, ALU.mult)\
                    .then_inc(S("mod_ready"), 1)
                dve.wait_ge(S("mod_ready"), layer + 1)

            def norm(src, nc_, gain, shift):
                o = c.of
                n = T * nc_
                dve.wait_ge(S("root_ready"), o["norm"] + 1)
                link(nc.vector.reciprocal(rstd[:, 0:n], root[:, 0:n]))
                for k in range(DC):
                    for j in range(nc_):
                        sl = slice(j * T, (j + 1) * T)
                        nc.vector.scalar_tensor_tensor(out=sq[:, k, sl], in0=src[:, k, sl], scalar=gain(k, j),
                                                       in1=rstd[:, sl], op0=ALU.mult, op1=ALU.mult)\
                            .then_inc(S("norm_prod"), 1)
                for k in range(DC):
                    for j in range(nc_):
                        e = o["norm_hi"] + k * nc_ + j
                        sl = slice(j * T, (j + 1) * T)
                        dve.wait_ge(S("norm_hi"), e + 1)
                        nc.vector.scalar_tensor_tensor(out=xl[:, k, sl], in0=sq[:, k, sl],
                                                       scalar=shift(k, j) if shift else 0.0,
                                                       in1=xh[:, k, sl].bitcast(F32), op0=ALU.add,
                                                       op1=ALU.subtract).then_inc(S("norm_lo"), 1)
                c.add(norm=1, norm_hi=DC * nc_)

            def ffn(n_tok, add, final):
                for h, half in enumerate(HALVES):
                    a0 = c.hidden
                    def up(i, s):
                        a = 2 * i + (a0 + s)
                        dve.wait_ge(S("act_ready"), a + 1)
                        dve.wait_ge(S("hid_l_ready"), a + 1)
                        nc.vector.tensor_tensor(hid32[:, s, 0:n_tok], act32[:, s, 0:n_tok],
                                                ps[:, 2 * s + 1, 0:n_tok], ALU.mult).then_inc(S("evac_done"), 1)
                        dve.wait_ge(S("hid_h_ready"), a + 1)
                        nc.vector.tensor_tensor(hid_l[:, bass.ds(i * 2 + s, 1), 0:n_tok],
                                                hid32[:, s:s + 1, 0:n_tok],
                                                hid_h[:, bass.ds(i * 2 + s, 1), 0:n_tok].bitcast(F32),
                                                ALU.subtract).then_inc(S("hid_l_ready"), 1)
                    pairs_of(dve, c, half // 2, up, ahead=dve_split)
                    c.hidden += half
                    def down(i, s):
                        dve_unit_done(dve, c, i, s)
                        add(i, s, h)
                    pairs_of(dve, c, 4, down, ahead=dve_split, final=final and h == 1)

            def add_gated(gate0, nc_):
                def add(i, s, h):
                    n = bass.ds(i * 2 + s, 1)
                    for j in range(nc_):
                        sl = slice(j * T, (j + 1) * T)
                        ins = nc.vector.scalar_tensor_tensor(
                            out=hT[:, n, sl], in0=ps[:, 2 * s:2 * s + 1, sl],
                            scalar=mod[:, bass.ds(i * 2 + (gate0 + s), 1), j], in1=hT[:, n, sl],
                            op0=ALU.mult, op1=ALU.add)
                    ins.then_inc(S("evac_done"), 1)
                return add


            def even():
                link(nc.vector.memset(e_gw[:, :, :], 0.0))
                nc.vector.memset(e_gT[32:33, :], 1.0).then_inc(S("e_gw_zero"), 1)
                nc.vector.memset(e_S[:, :, 0, :, :], 0.0)
                def to_z(i, s):
                    fm_evac(e_z, 0, 2 * T)(dve, c, i, s)
                pairs_of(dve, c, 2, to_z, ahead=dve_split)
                def r_and_v(i, s):
                    dve_unit_done(dve, c, i, s)
                    if s == 0:
                        nc.vector.tensor_copy(e_r[:, bass.ds(i * 2, 2), :], ps[:, 0:2, :]).then_inc(S("evac_done"), 1)
                    else:
                        nc.vector.tensor_copy(e_v[:, :, bass.ds(i * 256, 256)],
                                              ps[:, 2:4, :].rearrange("p a (b n) -> p (a b) n", n=256))\
                            .then_inc(S("evac_done"), 1)
                pairs_of(dve, c, 3, r_and_v, ahead=dve_split)
                dve.wait_ge(S("e_small_hi"), 1)
                nc.vector.tensor_tensor(e_small_l[:, :, :], e_small[:, :, :], e_small_h[:, :, :].bitcast(F32),
                                        ALU.subtract).then_inc(S("e_small_lo"), 1)
                dve.wait_ge(S("e_gates_mm"), 1)
                nc.vector.memset(e_att[:, :, :], 0.0)
                nc.vector.tensor_copy(e_gtok[:, :, :].rearrange("p a b -> p (a b)"), ps[:, 5, 0:P])\
                    .then_inc(S("e_gtok"), 1)
                dve.wait_ge(S("e_gates_t"), 1)
                nc.vector.tensor_copy(e_gT[0:32, :], ps[0:32, 6, :]).then_inc(S("e_gT"), 1)
                for q in range(2):
                    for n in range(4):
                        it, tile, dr = 4 * q + n, n // 2, n % 2
                        tt = slice((1 - q) * T + tile * P, (1 - q) * T + (tile + 1) * P)
                        t0 = slice(tile * P, (tile + 1) * P)
                        dve.wait_ge(S("e_ln"), it + 1)
                        if it >= 2:
                            dve.wait_ge(S("e_cum"), it - 1)
                        nc.vector.scalar_tensor_tensor(out=e_log[:, it % 2, :], in0=ps[:, dr, 0:384], scalar=0.0,
                                                       in1=e_abs[:, :], op0=ALU.min, op1=ALU.subtract)\
                            .then_inc(S("e_log"), 1)
                        dve.wait_ge(S("e_exp"), it + 1)
                        if q and n == 0:
                            dve.wait_ge(S("e_o"), 3 * q)
                        kd, qd = e_keys(dr, q)
                        edge = e_up[:, :, 63:128:64] if dr == 0 else e_up[:, :, 0:128:64]
                        link(nc.vector.tensor_copy(e_last[:, dr, tile, :, :], edge))
                        nc.vector.scalar_tensor_tensor(out=qd[:, :, t0], in0=e_z[:, 2:5, tt], scalar=0.125,
                                                       in1=e_up[:, :, :], op0=ALU.mult, op1=ALU.mult)
                        link(nc.vector.tensor_tensor(kd[:, :, t0], e_z[:, 5:8, tt], e_dn[:, :, :], ALU.mult))
                        if it:
                            dve.wait_ge(S("e_kk_t"), it)
                        nc.vector.tensor_tensor(
                            e_kk[:, :, :].rearrange("p a (b n) -> p (a b) n", n=64),
                            kd[:, :, t0].rearrange("p a (b n) -> p a b n", n=64).rearrange("p a b n -> p a b n"),
                            e_last[:, dr, tile, :, :].unsqueeze(3).to_broadcast([P, 3, 2, 64]), ALU.mult)\
                            .then_inc(S("e_decayed"), 1)
                    if q:
                        link(nc.vector.tensor_copy(e_S[:, :, 0, :, :], e_S[:, :, 4, :, :]))
                    for step in range(8):
                        dr, n = step % 2, step // 2
                        ch = n if dr == 0 else 3 - n
                        dve.wait_ge(S("e_kv"), 8 * q + step + 1)
                        if step >= 2:
                            dve.wait_ge(S("e_state"), 8 * q + step - 1)
                        for p in range(3):
                            ins = nc.vector.scalar_tensor_tensor(
                                out=e_S[:, dr, n + 1, p, :], in0=e_S[:, dr, n, p, :],
                                scalar=e_last[:, dr, ch // 2, p, ch % 2:ch % 2 + 1],
                                in1=ps[:, (6, 2)[dr], p * P:(p + 1) * P], op0=ALU.mult, op1=ALU.add)
                        ins.then_inc(S("e_state"), 1)
                    for p in range(3):
                        o = 3 * q + p
                        dve.wait_ge(S("e_att_mm"), o + 1)
                        if o:
                            dve.wait_ge(S("e_o"), o)
                        for dr in range(2):
                            mask = K(("cum_fwd", "cum_bwd")[dr]).bitcast(U32)
                            cols = slice(2 * dr * P, 2 * dr * P + 2 * P)
                            for h in range(2):
                                ins = nc.vector.copy_predicated(
                                    e_att[:, h, cols].rearrange("p (a b) -> p a b", b=P),
                                    mask.unsqueeze(1).to_broadcast([P, 2, P]),
                                    ps[:, 4 + h, cols].rearrange("p (a b) -> p a b", b=P))
                        ins.then_inc(S("e_att"), 1)
                        dve.wait_ge(S("e_oroot"), o + 1)
                        y2 = e_y[:, :].rearrange("p (a b) -> p a b", a=2)
                        link(nc.vector.reciprocal(rstd[:, :], root[:, :]))
                        if o:
                            dve.wait_ge(S("e_yl"), o)
                        link(nc.vector.scalar_tensor_tensor(out=y2, in0=ps[:, 6:8, 0:T], scalar=V("gla_norm"),
                                                            in1=rstd[:, :].rearrange("p (a b) -> p a b", a=2), op0=ALU.mult, op1=ALU.mult))
                        sl = slice((1 - q) * T, (2 - q) * T)
                        if o == 0:
                            dve.wait_ge(S("e_silu"), 1)
                        nc.vector.tensor_tensor(y2, y2, e_r[:, 2 * p:2 * p + 2, sl], ALU.mult).then_inc(S("e_y"), 1)
                        dve.wait_ge(S("e_yh"), o + 1)
                        nc.vector.tensor_tensor(xl[:, 2 + 2 * p:4 + 2 * p, sl], y2,
                                                xh[:, 2 + 2 * p:4 + 2 * p, sl].bitcast(F32), ALU.subtract)\
                            .then_inc(S("e_yl"), 1)
                for n in range(4):
                    q, k = divmod(n, 2)
                    dve.wait_ge(S("e_fh"), n + 1)
                    sl = slice(q * T, (q + 1) * T)
                    nc.vector.tensor_tensor(xl[:, k, sl], ps[:, 1, 0:T], xh[:, k, sl].bitcast(F32), ALU.subtract)\
                        .then_inc(S("e_fl"), 1)

            def odd():
                def first(i, s):
                    dve_unit_done(dve, c, i, s)
                    nc.vector.tensor_copy((o_z, o_q)[s][:, bass.ds(i * 2, 2), :], ps[:, 2 * s:2 * s + 2, 0:T])\
                        .then_inc(S("evac_done"), 1)
                pairs_of(dve, c, 3, first, ahead=dve_split)
                def k_and_v(i, s):
                    dve_unit_done(dve, c, i, s)
                    if s == 0:
                        nc.vector.tensor_copy(o_k[:, bass.ds(i * 2, 2), :], ps[:, 0:2, :]).then_inc(S("evac_done"), 1)
                    else:
                        nc.vector.tensor_copy(o_v[:, :, bass.ds(i * 256, 256)],
                                              ps[:, 2:4, :].rearrange("p a (b n) -> p (a b) n", n=256))\
                            .then_inc(S("evac_done"), 1)
                pairs_of(dve, c, 3, k_and_v, ahead=dve_split)
                dve.wait_ge(S("evac_done"), c.units + CREDIT)
                cos = K("axial_cos").unsqueeze(1).to_broadcast([P, 2, T])
                sin = K("axial_sin").unsqueeze(1).to_broadcast([P, 2, T])
                for n in range(6):
                    buf, k = (o_q, 2 * n) if n < 3 else (o_k, 2 * n - 6)
                    x = buf[:, k:k + 2, 0:T]
                    dve.wait_ge(S("o_swap"), n + 1)
                    if n:
                        dve.wait_ge(S("o_turned"), n)
                    nc.vector.tensor_tensor(o_turn[:, :, :], ps[:, n, :].rearrange("p (a b) -> p a b", a=2), sin, ALU.mult)
                    link(nc.vector.tensor_tensor(x, x, cos, ALU.mult))
                    nc.vector.tensor_tensor(x, x, o_turn[:, :, :], ALU.add).then_inc(S("o_turned"), 1)

                def probs(e):
                    st = o_st[:, e, :]
                    dve.wait_ge(S("o_exp"), e + 1)
                    link(nc.vector.reciprocal(st[:, 4:6], st[:, 2:4]))
                    nc.vector.tensor_scalar(o_p[:, e % 2, 0, :], o_p[:, e % 2, 0, :], st[:, 4:5], None, ALU.mult)
                    link(nc.vector.tensor_tensor(st[:, 5:6], st[:, 5:6], lam[:, 2:3], ALU.mult))
                    nc.vector.scalar_tensor_tensor(out=o_p[:, e % 2, 0, :], in0=o_p[:, e % 2, 1, :], scalar=st[:, 5:6],
                                                   in1=o_p[:, e % 2, 0, :], op0=ALU.mult, op1=ALU.add)\
                        .then_inc(S("o_a"), 1)

                for e in range(13):
                    if e < 12:
                        dve.wait_ge(S("o_scores"), e + 1)
                        b = 4 + 2 * (e % 2)
                        link(nc.vector.tensor_reduce(o_st[:, e, 0:2], ps[:, b:b + 2, :], AX.X, ALU.max, negate=True))
                        nc.vector.tensor_scalar(o_st[:, e, 0:2], o_st[:, e, 0:2], HD ** -0.5, None, ALU.mult)\
                            .then_inc(S("o_max"), 1)
                    if e:
                        probs(e - 1)
                link(nc.vector.memset(o_u[:, :, :], 0.0))
                link(nc.vector.tensor_tensor(o_u[:, :, 1:T + 1], o_z[:, 2:4, :], o_z[:, 4:6, :], ALU.mult))
                for b in range(2):
                    link(nc.vector.tensor_scalar(o_c[:, b, :], o_u[:, b, 0:T], V("conv_w", b), V("conv_b", b),
                                                 ALU.mult, ALU.add))
                    for tap in (1, 2):
                        link(nc.vector.scalar_tensor_tensor(out=o_c[:, b, :], in0=o_u[:, b, tap:tap + T],
                                                            scalar=V("conv_w", 2 * tap + b), in1=o_c[:, b, :],
                                                            op0=ALU.mult, op1=ALU.add))
                nc.vector.tensor_tensor(o_c[:, :, :], o_c[:, :, :], o_z[:, 0:2, :], ALU.mult).then_inc(S("o_conv"), 1)
                link(nc.vector.tensor_scalar(lam[:, 3:4], V("diff_norm"), 1.0 - LAM_INIT, None, ALU.mult))
                dve.wait_ge(S("o_root"), 1)
                link(nc.vector.reciprocal(o_sq[:, :, :], o_sq[:, :, :]))
                nc.vector.scalar_tensor_tensor(out=o_o[:, :, :], in0=o_o[:, :, :], scalar=lam[:, 3:4],
                                               in1=o_sq[:, :, :], op0=ALU.mult, op1=ALU.mult).then_inc(S("o_y"), 1)
                for n, (c0, buf) in enumerate(((0, o_c), (2, o_o))):
                    dve.wait_ge(S("o_yh"), n + 1)
                    k = buf.shape[1]
                    nc.vector.tensor_tensor(xl[:, c0:c0 + k, 0:T], buf[:, :, :],
                                            xh[:, c0:c0 + k, 0:T].bitcast(F32), ALU.subtract).then_inc(S("o_yl"), 1)

            def mamba(layer):
                def unit(i, s):
                    fm_evac(m_in, 0, T)(dve, c, i, s)
                pairs_of(dve, c, 3, unit, ahead=dve_split)
                dve.wait_ge(S("m_sw_hi"), layer + 1)
                nc.vector.tensor_tensor(m_sw_l[:, :, :], m_sw[:, :, :], m_sw_h[:, :, :].bitcast(F32), ALU.subtract)\
                    .then_inc(S("m_sw_lo"), 1)
                dve.wait_ge(S("m_small_mm"), layer + 1)
                nc.vector.tensor_copy(h_small[:, :, :].rearrange("p a b -> p (a b)"), ps[:, 5, 0:NT * 84])\
                    .then_inc(S("m_small"), 1)
                dve.wait_ge(S("m_small"), layer + 1)
                for t in range(NT):
                    ins = nc.vector.tensor_tensor(m_dt[:, 0, 8 * t:8 * t + 8], h_small[:, t, 0:8],
                                                  bcast[:, 8 * layer:8 * layer + 8], ALU.add)
                ins.then_inc(S("m_dt_in"), 1)
                dve.wait_ge(S("m_dt_exp"), layer + 1)
                nc.vector.tensor_scalar(m_dt[:, 2, :], m_dt[:, 1, :], 1.0, None, ALU.add).then_inc(S("m_dt_one"), 1)
                dve.wait_ge(S("m_dt_one"), layer + 1)
                link(nc.vector.tensor_scalar(m_dt[:, 4, :], m_dt[:, 2, :], -1.0, None, ALU.add))
                link(nc.vector.tensor_tensor(m_dt[:, 1, :], m_dt[:, 1, :], m_dt[:, 4, :], ALU.subtract))
                link(nc.vector.reciprocal(m_dt[:, 4, :], m_dt[:, 2, :]))
                link(nc.vector.tensor_tensor(m_dt[:, 1, :], m_dt[:, 1, :], m_dt[:, 4, :], ALU.mult))
                dve.wait_ge(S("m_dt_ln"), layer + 1)
                link(nc.vector.tensor_tensor(m_dt[:, 1, :], m_dt[:, 1, :], m_dt[:, 3, :], ALU.add))
                link(nc.vector.scalar_tensor_tensor(out=m_dt[:, 0, :], in0=m_dt[:, 0, :], scalar=0.0,
                                                    in1=m_dt[:, 1, :], op0=ALU.max, op1=ALU.add))
                for t in range(NT):
                    ins = nc.vector.scalar_tensor_tensor(out=m_dt[:, 4, 8 * t:8 * t + 8], in0=m_dt[:, 0, 8 * t:8 * t + 8],
                                                         scalar=-1.0, in1=m_dt[:, 5, 0:8], op0=ALU.mult, op1=ALU.mult)
                ins.then_inc(S("m_dta"), 1)
                for k in range(8):
                    w = lambda tap: V("conv_w_2", 32 * layer + 8 * tap + k)
                    link(nc.vector.tensor_scalar(m_cv[:, k, :], m_in[:, 4 + k, :], w(3),
                                                 V("conv_b_2", 8 * layer + k), ALU.mult, ALU.add))
                    for back in (1, 2, 3):
                        ins = nc.vector.scalar_tensor_tensor(out=m_cv[:, k, back:T], in0=m_in[:, 4 + k, 0:T - back],
                                                             scalar=w(3 - back), in1=m_cv[:, k, back:T],
                                                             op0=ALU.mult, op1=ALU.add)
                        if k == 7 and back == 3:
                            ins.then_inc(S("m_taps"), 1)
                        else:
                            link(ins)
                dve.wait_ge(S("m_cs_mm"), layer + 1)
                nc.vector.tensor_copy(m_cs[:, :], ps[0:8, 2, 0:T])
                nc.vector.tensor_scalar(m_ncs[:, :], ps[:, 3, 0:16], -1.0, None, ALU.mult).then_inc(S("m_cs"), 1)
                dve.wait_ge(S("m_cs"), layer + 1)
                d0 = 48 + 8 * layer
                for j in range(2):
                    hh = slice(64 * j, 64 * j + 64)
                    ins = nc.vector.tensor_copy(m_d[hh, :], bcast[hh, d0 + j:d0 + 8:2])
                link(ins)
                dve.wait_ge(S("m_cb"), layer + 1)

                def seg(h):
                    dve.wait_ge(S("m_row"), 8 * layer + h + 1)
                    if h >= 2:
                        dve.wait_ge(S("m_o"), 8 * layer + h - 1)
                    row = ps[:, 4 + h % 2, 0:T]
                    e = m_e[:, h % 2, :]
                    for t in range(NT):
                        ins = nc.vector.scalar_tensor_tensor(out=e[:, t * T:t * T + P], in0=row[:, t * P:(t + 1) * P],
                                                             scalar=m_ncs[:, 8 * t + h:8 * t + h + 1],
                                                             in1=K("causal_t"), op0=ALU.add, op1=ALU.add)
                    nc.vector.tensor_scalar(e[:, P:T], row[:, P:T], m_ncs[:, h:h + 1], None, ALU.add)\
                        .then_inc(S("m_seg"), 1)

                seg(0)
                for h in range(8):
                    if h + 1 < 8:
                        seg(h + 1)
                    dve.wait_ge(S("m_exp"), 8 * layer + h + 1)
                    g = h // 4
                    e = m_e[:, h % 2, :]
                    nc.vector.scalar_tensor_tensor(out=e[:, 0:T], in0=e[:, 0:T], scalar=m_dt[:, 0, h:h + 1],
                                                   in1=ps[:, g, 0:T], op0=ALU.mult, op1=ALU.mult)
                    nc.vector.scalar_tensor_tensor(out=e[:, T:T + P], in0=e[:, T:T + P], scalar=m_dt[:, 0, 8 + h:9 + h],
                                                   in1=ps[:, g, T + P:2 * T], op0=ALU.mult, op1=ALU.mult)\
                        .then_inc(S("m_score"), 1)
                    if h % 2:
                        p = h // 2
                        dve.wait_ge(S("m_o"), 8 * layer + h + 1)
                        nc.vector.scalar_tensor_tensor(out=m_y[:, p, :], in0=m_cv[:, p, :], scalar=m_d[:, p:p + 1],
                                                       in1=ps[:, 6 + p % 2, 0:T], op0=ALU.mult, op1=ALU.add)\
                            .then_inc(S("m_y"), 1)
                dve.wait_ge(S("m_y"), 4 * layer + 4)
                nc.vector.tensor_tensor(m_y[:, :, :], m_y[:, :, :], m_in[:, 0:4, :], ALU.mult).then_inc(S("m_gated"), 1)
                dve.wait_ge(S("m_root"), layer + 1)
                link(nc.vector.reciprocal(rstd[:, :], root[:, :]))
                for k in range(4):
                    ins = nc.vector.scalar_tensor_tensor(out=m_y[:, k, :], in0=m_y[:, k, :],
                                                         scalar=V("ssm_norm_2", 4 * layer + k),
                                                         in1=rstd[:, (k // 2) * T:(k // 2 + 1) * T],
                                                         op0=ALU.mult, op1=ALU.mult)
                ins.then_inc(S("m_normed"), 1)
                dve.wait_ge(S("m_yh"), layer + 1)
                nc.vector.tensor_tensor(h_yl[:, :, :], m_y[:, :, :], h_yh[:, :, :].bitcast(F32), ALU.subtract)\
                    .then_inc(S("m_yl"), 1)

            def turn(n, buf, bank, n_chunks, count):
                dve.wait_ge(S("a_swap"), count)
                if count > 1:
                    dve.wait_ge(S("a_turned"), count - 1)
                if n_chunks == 2:
                    spreadto = lambda t: K(t).unsqueeze(1).to_broadcast([P, 2, T])
                    x, t, s = buf, a_turn[:, :, :], ps[:, bank, :].rearrange("p (a b) -> p a b", a=2)
                else:
                    spreadto = K
                    x, t, s = buf, a_turn[:, 0, :], ps[:, bank, 0:T]
                nc.vector.tensor_tensor(t, s, spreadto("rope_sin"), ALU.mult)
                link(nc.vector.tensor_tensor(x, x, spreadto("rope_cos"), ALU.mult))
                nc.vector.tensor_tensor(x, x, t, ALU.add).then_inc(S("a_turned"), 1)

            def choose(layer):
                link(nc.vector.tensor_scalar(a_w[:, :, :], h_small[:, :, 80:84], 0.5, None, ALU.mult))
                for qt in range(NT):
                    nk = (qt + 1) * P
                    dve.wait_ge(S("a_idx"), NT * layer + qt + 1)
                    for h in range(4):
                        link(nc.vector.tensor_scalar(a_relu[:, 0:nk], ps[:, 4 + h, 0:nk], HD ** -0.5, 0.0,
                                                     ALU.mult, ALU.max))
                        w = a_w[:, qt, h:h + 1]
                        if h == 0:
                            link(nc.vector.tensor_scalar(a_isc[:, 0:nk], a_relu[:, 0:nk], w, None, ALU.mult))
                        else:
                            link(nc.vector.scalar_tensor_tensor(out=a_isc[:, 0:nk], in0=a_relu[:, 0:nk], scalar=w,
                                                                in1=a_isc[:, 0:nk], op0=ALU.mult, op1=ALU.add))
                    diag = slice(nk - P, nk)
                    nc.vector.tensor_tensor(a_isc[:, diag], a_isc[:, diag], K("causal"), ALU.add).then_inc(S("a_isc"), 1)
                    dve.wait_ge(S("a_isc"), NT * layer + qt + 1)
                    for _ in range(DSA_KEEP // 8):
                        link(nc.vector.max(a_top[:, :], a_isc[:, 0:nk]))
                        link(nc.vector.match_replace(a_isc[:, 0:nk], a_top[:, :], a_isc[:, 0:nk], TAKEN))
                    b0 = (0, P)[qt]
                    link(nc.vector.tensor_scalar(a_bias[:, 0, b0:b0 + nk], a_isc[:, 0:nk], TAKEN, NEG,
                                                 ALU.not_equal, ALU.mult))
                    bd = a_bias[:, 0, b0 + nk - P:b0 + nk]
                    link(nc.vector.tensor_tensor(bd, bd, K("causal"), ALU.add))

            def attention(layer, which):
                a = 3 * layer + which
                def qk(i, s):
                    fm_evac(a_qk, 0, T)(dve, c, i, s)
                pairs_of(dve, c, 2, qk, ahead=dve_split)
                def vv(i, s):
                    dve_unit_done(dve, c, i, s)
                    nc.vector.tensor_copy(a_v[:, :, s * 256:(s + 1) * 256],
                                          ps[:, 2 * s, :].rearrange("p (a b) -> p a b", a=NT)).then_inc(S("evac_done"), 1)
                pairs_of(dve, c, 1, vv, ahead=dve_split)
                if which == 0:
                    f0 = 32 + 8 * layer
                    for t in range(NT):
                        ins = nc.vector.tensor_tensor(a_f[:, 0, 8 * t:8 * t + 8], h_small[:, t, 8:16],
                                                      bcast[:, f0:f0 + 8], ALU.add)
                    ins.then_inc(S("a_f_in"), 1)
                    dve.wait_ge(S("a_f_ln"), layer + 1)
                    nc.vector.scalar_tensor_tensor(out=a_f[:, 2, :], in0=a_f[:, 0, :], scalar=0.0, in1=a_f[:, 1, :],
                                                   op0=ALU.min, op1=ALU.subtract).then_inc(S("a_logf"), 1)
                    dve.wait_ge(S("a_cf_mm"), layer + 1)
                    nc.vector.tensor_scalar(a_cf[:, :], ps[0:8, 2, 0:T], -1.0, None, ALU.mult)
                    nc.vector.tensor_copy(a_f[:, 3, :], ps[:, 3, 0:16]).then_inc(S("a_cf"), 1)
                    dve.wait_ge(S("a_cf"), layer + 1)
                else:
                    if which == 2:
                        def iq(i, s):
                            dve_unit_done(dve, c, i, s)
                            nc.vector.tensor_copy(a_iq[:, s, :], ps[:, 2 * s, 0:T]).then_inc(S("evac_done"), 1)
                        pairs_of(dve, c, 1, iq, ahead=dve_split)
                        for j in range(2):
                            ins = nc.vector.tensor_copy(a_ik2[:, :, 64 * j:64 * j + 64], h_small[:, :, 16:80])
                        ins.then_inc(S("a_ik2"), 1)
                    dve.wait_ge(S("evac_done"), c.units + CREDIT)
                    r0 = 10 * layer + (0, 0, 4)[which]
                    for n in range(4):
                        turn(n, a_qk[:, 2 * n:2 * n + 2, :], n, 2, r0 + n + 1)
                    if which == 2:
                        dve.wait_ge(S("a_ik_t"), layer + 1)
                        nc.vector.tensor_copy(a_ik[:, :], ps[:, 6, 0:T]).then_inc(S("a_ik"), 1)
                        dve.wait_ge(S("a_ik"), layer + 1)
                        turn(4, a_iq[:, :, :], 4, 2, r0 + 5)
                        turn(5, a_ik[:, :], 5, 1, r0 + 6)
                        choose(layer)
                    else:
                        nc.vector.memset(a_bias[:, 0, P:2 * P], 0.0)
                        nc.vector.tensor_copy(a_bias[:, 0, 0:P], K("causal"))
                        link(nc.vector.tensor_copy(a_bias[:, 0, 2 * P:3 * P], K("causal")))

                def forget_bias(h):
                    dve.wait_ge(S("a_row"), 8 * layer + h + 1)
                    row = ps[:, 2 + h % 2, 0:T]
                    b = a_bias[:, h % 2, :]
                    cq = lambda t: a_f[:, 3, 8 * t + h:8 * t + h + 1]
                    nc.vector.scalar_tensor_tensor(out=b[:, 0:P], in0=row[:, 0:P], scalar=cq(0), in1=K("causal"),
                                                   op0=ALU.add, op1=ALU.add)
                    nc.vector.tensor_scalar(b[:, P:2 * P], row[:, 0:P], cq(1), None, ALU.add)
                    nc.vector.scalar_tensor_tensor(out=b[:, 2 * P:3 * P], in0=row[:, P:T], scalar=cq(1),
                                                   in1=K("causal"), op0=ALU.add, op1=ALU.add).then_inc(S("a_bias"), 1)
                    dve.wait_ge(S("a_bias"), 8 * layer + h + 1)

                for e in range(20):
                    if e < 16:
                        h, qt = divmod(e, 2)
                        nk = (qt + 1) * P
                        if which == 0 and qt == 0:
                            forget_bias(h)
                        b0 = (0, P)[qt]
                        bias = a_bias[:, h % 2 if which == 0 else 0, b0:b0 + nk]
                        dve.wait_ge(S("a_scores"), 16 * a + e + 1)
                        if e >= 2:
                            dve.wait_ge(S("a_t"), 16 * a + e - 1)
                        link(nc.vector.scalar_tensor_tensor(out=a_p[:, e % 2, 0:nk], in0=ps[:, 4 + e % 2, 0:nk],
                                                            scalar=HD ** -0.5, in1=bias, op0=ALU.mult, op1=ALU.add))
                        nc.vector.tensor_reduce(a_st[:, e, 0:1], a_p[:, e % 2, 0:nk], AX.X, ALU.max, negate=True)\
                            .then_inc(S("a_max"), 1)
                    if 1 <= e <= 16:
                        b = e - 1
                        nk = (b % 2 + 1) * P
                        dve.wait_ge(S("a_exp"), 16 * a + b + 1)
                        link(nc.vector.reciprocal(a_st[:, b, 2:3], a_st[:, b, 1:2]))
                        nc.vector.tensor_scalar(a_p[:, b % 2, 0:nk], a_p[:, b % 2, 0:nk], a_st[:, b, 2:3], None, ALU.mult)\
                            .then_inc(S("a_p"), 1)
                    if e >= 7 and e % 4 == 3:
                        p = (e - 7) // 4
                        dve.wait_ge(S("a_yh"), 4 * a + p + 1)
                        nc.vector.tensor_tensor(h_yl[:, p, :], ps[:, p % 2, 0:T], h_yh[:, p, :].bitcast(F32),
                                                ALU.subtract).then_inc(S("a_yl"), 1)

            def merge(layer, n):
                def unit(i, s):
                    u = 2 * i + (c.units + s)
                    if s == 0:
                        dve.wait_ge(S("evac_done"), u + CREDIT)
                        dve_unit_done(dve, c, i, s)
                        nc.vector.tensor_copy(h_gate[:, :, :], ps[:, 0:2, 0:T]).then_inc(S("evac_done"), 1)
                    else:
                        dve_unit_done(dve, c, i, s)
                        dve.wait_ge(S("h_gate"), i + (4 * (4 * layer + n) + 1))
                        dst = h_merged[:, bass.ds(i * 2, 2), :]
                        to = dst if n == 0 else h_prod[:, :, :]
                        nc.vector.tensor_tensor(to, ps[:, 2:4, 0:T], h_gate[:, :, :], ALU.mult).then_inc(S("evac_done"), 1)
                        if n:
                            dve.wait_ge(S("evac_done"), u + 1 + CREDIT)
                            nc.vector.tensor_tensor(dst, dst, h_prod[:, :, :], ALU.add).then_inc(S("h_merged"), 1)
                pairs_of(dve, c, 4, unit, ahead=dve_split)

            def merged(layer):
                dve.wait_ge(S("h_merged_hi"), layer + 1)
                nc.vector.tensor_tensor(xl[:, :, 0:T], h_merged[:, :, :], xh[:, :, 0:T].bitcast(F32), ALU.subtract)\
                    .then_inc(S("h_merged_lo"), 1)

            def add_plain(i, s, h):
                dst = h_out[:, bass.ds(i * 2 + s, 1), :]
                src = ps[:, 2 * s:2 * s + 1, 0:T]
                if h == 0:
                    ins = nc.vector.tensor_copy(dst, src)
                else:
                    ins = nc.vector.tensor_tensor(dst, src, dst, ALU.add)
                ins.then_inc(S("evac_done"), 1)

            for stage, *args in schedule:
                if stage == "mod":
                    def unit(i, s):
                        dve_unit_done(dve, c, i, s)
                        nc.vector.tensor_copy(modp[:, bass.ds(i * 4 + 2 * s, 2), :].rearrange("p a b -> p (a b)"),
                                              ps[:, 2 * s, 0:8]).then_inc(S("evac_done"), 1)
                    pairs_of(dve, c, 2 * N_MOD, unit, ahead=dve_split)
                    mod_ready(args[0])
                elif stage == "norm":
                    norm(args[0], args[1], args[3], args[2])
                elif stage == "renorm":
                    dve.wait_ge(S("root_ready"), c.of["norm"] + 1)
                    link(nc.vector.reciprocal(rstd[:, 0:T], root[:, 0:T]))
                    src, gain = args
                    dst = hT if src is hT else sq
                    for k in range(DC):
                        ins = nc.vector.scalar_tensor_tensor(out=dst[:, k, 0:T], in0=src[:, k, 0:T], scalar=gain(k),
                                                             in1=rstd[:, 0:T], op0=ALU.mult, op1=ALU.mult)
                    if src is not hT:
                        link(ins)
                        ins = nc.vector.tensor_tensor(hT[:, :, 0:T], hT[:, :, 0:T], sq[:, :, 0:T], ALU.add)
                    ins.then_inc(S("renormed"), 1)
                    c.add(norm=1, renorm=1)
                elif stage == "ffn":
                    ffn(args[2], add_plain if args[3] is None else add_gated(args[3], args[2] // T), args[4])
                elif stage == "even":
                    even()
                elif stage == "odd":
                    odd()
                elif stage == "out":
                    def out_unit(i, s):
                        dve_unit_done(dve, c, i, s)
                        for b in range(2):
                            n = i * 4 + (2 * s + b)
                            for j in range(args[1] // T):
                                sl = slice(j * T, (j + 1) * T)
                                ins = nc.vector.scalar_tensor_tensor(
                                    out=hT[:, bass.ds(n, 1), sl], in0=ps[:, 2 * s + b:2 * s + b + 1, sl],
                                    scalar=mod[:, bass.ds(n + 40, 1), j], in1=hT[:, bass.ds(n, 1), sl],
                                    op0=ALU.mult, op1=ALU.add)
                        ins.then_inc(S("evac_done"), 1)
                    pairs_of(dve, c, 2, out_unit, ahead=dve_split)
                elif stage == "mamba":
                    mamba(args[0])
                elif stage == "attention":
                    attention(args[0], args[1])
                elif stage == "merge":
                    merge(*args)
                elif stage == "wout":
                    merged(args[0])
                    pairs_of(dve, c, 2, lambda i, s: fm_evac(h_out, 0, T)(dve, c, i, s), ahead=dve_split)
                elif stage == "store":
                    for t in range(NT):
                        dve.wait_ge(S("y_t"), t + 1)
                        nc.vector.tensor_copy(y_tok[:, t, :].rearrange("p (a b) -> p a b", a=2),
                                              ps[:, 2 * t:2 * t + 2, :]).then_inc(S("y_copied"), 1)


def kernel(**inputs):
    import concourse.bacc as bacc
    from concourse.bass_utils import run_bass_kernel_spmd

    nc = bacc.Bacc("TRN2", target_bir_lowering=False, num_devices=1)
    table, const_at = constants()
    arrays, io = {"consts": table}, {}
    for name in NAMES:
        arrays[name] = np.ascontiguousarray(inputs[name])
    for name, a in arrays.items():
        io[name] = nc.dram_tensor(name, a.shape, F32, kind="ExternalInput").ap()
    io["out"] = nc.dram_tensor("out", (1, T, D), F32, kind="ExternalOutput").ap()
    chunked = lambda a, pat: io[a].rearrange(pat, p=P)
    io["vectors"] = [
        ("ada_b", chunked("ada_b", "l (b p) -> (l b) p")),
        ("norm_ffn1", chunked("norm_ffn1", "l (b p) -> (l b) p")),
        ("norm_mix", chunked("norm_mix", "l (b p) -> (l b) p")),
        ("norm_ffn2", chunked("norm_ffn2", "l (b p) -> (l b) p")),
        ("final_norm", chunked("final_norm", "(b p) -> b p")),
        ("c", chunked("c", "l (b p) -> (l b) p")),
        ("c_ctx", chunked("c_ctx", "(b p) -> b p")),
        ("gla_norm", io["gla_norm"]),
        ("diff_norm", io["diff_norm"]),
        ("conv_w", chunked("conv_w", "l k (b p) -> (l k b) p")),
        ("conv_b", chunked("conv_b", "l (b p) -> (l b) p")),
        ("norm_mix_pre_2", chunked("norm_mix_pre_2", "l (b p) -> (l b) p")),
        ("conv_w_2", chunked("conv_w_2", "l k (b p) -> (l k b) p")),
        ("conv_b_2", chunked("conv_b_2", "l (b p) -> (l b) p")),
        ("ssm_norm_2", chunked("ssm_norm_2", "l (b p) -> (l b) p")),
        ("norm_mix_post_2", chunked("norm_mix_post_2", "l (b p) -> (l b) p")),
        ("norm_ffn_pre_2", chunked("norm_ffn_pre_2", "l (b p) -> (l b) p")),
        ("norm_ffn_post_2", chunked("norm_ffn_post_2", "l (b p) -> (l b) p")),
        ("b_gate_2", chunked("b_gate_2", "l (b p) -> (l b) p")),
    ]
    build(nc, io, const_at)
    r = run_bass_kernel_spmd(nc, [arrays], core_ids=[0])
    return r.results[0]["out"]
```

```python
import math
from collections import Counter
from contextlib import ExitStack

import concourse.bass as bass
import numpy as np
from concourse import mybir

F32 = mybir.dt.float32
F32R = mybir.dt.float32r
U32 = mybir.dt.uint32
ALU = mybir.AluOpType
ACT = mybir.ActivationFunctionType
AX = mybir.AxisListType

P = 128
D = 1024
DC = D // P
T = 256
NT = T // P
FFN = 2816
FC = FFN // P
HALVES = (12, 10)
UNIT = 2048
EPS = 1e-6
HD = 64
NEG = -1e30
TAKEN = -3e38
N_MOD = 9
MOD_UNITS = 4 * N_MOD
MOD_FIRST = 8
LAM_INIT = 0.8 - 0.6 * math.exp(-0.3)
DSA_KEEP = 64
Z0, DT0, FQ0, FV0, FF0, MQ0, MV0, DQ0, DV0, IQ0, IK0 = (
    0, 1536, 1544, 2568, 3080, 3088, 4112, 4624, 5648, 6160, 6416)


def constants():
    parts = {}
    eye = np.eye(P)
    parts["ident"] = eye
    parts["ones"] = np.ones((P, P))
    parts["eps"] = np.full((P, 1), EPS)
    t = np.arange(T)
    d = np.arange(HD)
    ang = 2 * np.pi * np.outer(d, d) / HD
    parts["dft_cos"] = np.kron(np.eye(2), np.cos(ang))
    parts["dft_sin"] = np.kron(np.eye(2), np.sin(ang))
    ang = 2 * np.pi * (np.outer(t, t) % T) / T
    scale = 1 / math.sqrt(T * HD)
    tiles = lambda a: a.reshape(NT, P, -1).transpose(1, 0, 2).reshape(P, -1)
    parts["dft_tok_cos"] = tiles(np.cos(ang) * scale)
    parts["dft_tok_nsin"] = tiles(-np.sin(ang) * scale)
    f32 = np.float32
    inv = (f32(10000.0) ** (-np.arange(0, HD, 2, dtype=f32) / f32(HD))).astype(f32)
    ang = (t[:, None].astype(f32) * inv[None]).astype(f32)
    row = np.concatenate([ang, ang], 1).T
    parts["rope_cos"] = np.cos(np.concatenate([row, row]))
    parts["rope_sin"] = np.sin(np.concatenate([row, row]))
    swap = np.zeros((P, P))
    for h in range(2):
        for i in range(32):
            swap[64 * h + 32 + i, 64 * h + i] = -1
            swap[64 * h + i, 64 * h + 32 + i] = 1
    parts["rope_swap"] = swap
    inv = (f32(10000.0) ** (-np.arange(16, dtype=f32) / f32(16))).astype(f32)
    rowang = ((t // 64)[:, None].astype(f32) * inv).astype(f32)
    colang = ((t % 64)[:, None].astype(f32) * inv).astype(f32)
    one = np.concatenate([rowang, rowang, colang, colang], 1).T
    parts["axial_cos"] = np.cos(np.concatenate([one, one]))
    parts["axial_sin"] = np.sin(np.concatenate([one, one]))
    swap = np.zeros((P, P))
    for h in range(4):
        for i in range(16):
            swap[32 * h + 16 + i, 32 * h + i] = -1
            swap[32 * h + i, 32 * h + 16 + i] = 1
    parts["axial_swap"] = swap
    i = np.arange(P)
    same = (i[:, None] // 64) == (i[None] // 64)
    parts["cum_fwd"] = (same & (i[:, None] <= i[None])).astype(float)
    parts["cum_bwd"] = (same & (i[:, None] >= i[None])).astype(float)
    parts["cum_all"] = tiles((t[:, None] <= t[None]).astype(float))
    parts["causal"] = np.where(i[None] <= i[:, None], 0.0, NEG)
    parts["causal_t"] = np.where(i[:, None] <= i[None], 0.0, NEG)
    spread = np.zeros((P, 8, P))
    for h in range(8):
        spread[h, h] = 1
    parts["spread"] = spread.reshape(P, -1)
    at, n = {}, 0
    for name, a in parts.items():
        at[name] = (n, n + a.shape[1])
        n += a.shape[1]
    return np.concatenate([np.asarray(a, np.float32) for a in parts.values()], 1), at

NAMES = (
    "x", "c", "ctx", "c_ctx", "ada_w", "ada_b", "norm_ffn1", "norm_mix", "norm_ffn2", "ffn1_w_in",
    "ffn1_w_out", "ffn2_w_in", "ffn2_w_out", "mix_w_out", "even_w_in", "gla_gate_w", "gla_gate_b",
    "gla_norm", "odd_w_in", "conv_w", "conv_b", "lambda_q1", "lambda_k1", "lambda_q2", "lambda_k2",
    "diff_norm", "final_norm", "norm_mix_pre_2", "w_in_2", "conv_w_2", "conv_b_2", "dt_bias_2",
    "a_log_2", "d_skip_2", "ssm_norm_2", "fox_fbias_2", "w_gate_2", "b_gate_2", "w_branch_2",
    "w_out_2", "norm_mix_post_2", "norm_ffn_pre_2", "w_ffn_in_2", "w_ffn_out_2", "norm_ffn_post_2",
)


def build(nc, io, const_at):
    ctx = ExitStack()
    with ctx:
        SLAB = 212704
        base = (nc.sbuf_base + 31) // 32 * 32
        ctx.enter_context(nc.sbuf_tensor("slab", [P, SLAB // 4], F32))

        class Region:

            def __init__(self, start, end=SLAB):
                self.at, self.end = start, end

            def __call__(self, name, shape, dt=F32):
                t = nc.alloc_sbuf_tensor_at(name, shape, dt, offset=base + self.at)
                self.at += (4 * int(np.prod(shape[1:])) + 31) // 32 * 32
                assert self.at <= self.end, (name, self.at, self.end)
                return t

        fixed = Region(0)
        n_const = max(b for _, b in const_at.values())
        consts = fixed("consts", [P, n_const])
        K = lambda name: consts[:, const_at[name][0]:const_at[name][1]]
        vec = fixed("vec", [P, 512])
        mod = fixed("mod", [P, 2 * 8 * N_MOD, 2])
        gains = fixed("gains", [P, 2, 3, DC, 2])
        cond32 = fixed("cond32", [P, 2, DC])
        bcast = fixed("bcast", [P, 64])
        lam = fixed("lam", [P, 4])
        rstd = fixed("rstd", [P, 2 * T])
        root = fixed("root", [P, 2 * T])
        raw = fixed("raw", [P, 2, 2, UNIT // 2])
        whi = fixed("whi", [P, 2, 2, UNIT // 2], F32R)
        wlo = fixed("wlo", [P, 2, 2, UNIT // 2], F32R)
        wide = fixed.at
        hT = fixed("hT", [P, DC, 2 * T])
        xh_at = fixed.at
        xh = fixed("xh", [P, DC, 2 * T], F32R)
        xl_at = fixed.at
        xl = fixed("xl", [P, DC, 2 * T], F32R)
        overlay = fixed.at

        first = Region(overlay)
        hid_h = first("hid_h", [P, max(HALVES), 2 * T], F32R)
        hid_l = first("hid_l", [P, max(HALVES), 2 * T], F32R)
        ffn_end = first.at
        act32 = first("act32", [P, 2, 2 * T])
        hid32 = first("hid32", [P, 2, 2 * T])
        mod_w = first("mod_w", [P, 2, DC, 2 * P])
        sq = Region(overlay)("sq", [P, DC, 2 * T])
        start = Region(overlay)
        tok = start("tok", [P, 2 * NT, D])
        rows = start("rows", [P, 4, P])
        lam_in = start("lam_in", [HD, 4])
        lam_prod = start("lam_prod", [HD, 2])
        small_rows = start("small_rows", [1, 64])
        mod_first = start("mod_first", [P, MOD_FIRST, DC, 2 * P])
        last = Region(overlay)
        y_tok = last("y_tok", [P, NT, D])


        ev = Region(overlay)
        e_z = ev("e_z", [P, 8, 2 * T])
        e_r = ev("e_r", [P, 6, 2 * T])
        e_v = ev("e_v", [P, 2 * NT, 768])
        e_small_at = ev.at
        e_small = ev("e_small", [P, DC, 32])
        e_small_h = ev("e_small_h", [P, DC, 32], F32R)
        e_small_l = ev("e_small_l", [P, DC, 32], F32R)
        e_gtok = ev("e_gtok", [P, 2 * NT, 32])
        e_gT = ev("e_gT", [33, 2 * T])
        e_gw = ev("e_gw", [33, 2, 384])
        e_abs = Region(e_small_at)("e_abs", [P, 384])
        e_log = ev("e_log", [P, 2, 384])
        e_up = ev("e_up", [P, 3, P])
        e_dn = ev("e_dn", [P, 3, P])
        e_kk = ev("e_kk", [P, 3, P])
        e_last = ev("e_last", [P, 2, NT, 3, 2])
        e_kd = ev("e_kd", [P, 3, T])
        e_qd = ev("e_qd", [P, 3, T])
        e_kkT = ev("e_kkT", [P, 2, NT, 384])
        e_S = ev("e_S", [P, 2, 5, 3, P])
        e_ab = e_kkT[:, 0, :, 0:2 * P]
        at_xh = Region(xh_at, xh_at + 8 * T * 2)
        e_att = at_xh("e_att", [P, 2, 512])
        at_xl = Region(xl_at, xl_at + 8 * T * 2)
        e_osq = at_xl("e_osq", [P, 512])
        e_y = at_xl("e_y", [P, 512])

        od = Region(overlay)
        o_z = od("o_z", [P, 6, T])
        o_q = od("o_q", [P, 6, T])
        o_k = od("o_k", [P, 6, 2 * T])
        o_v = od("o_v", [P, 2 * NT, 768])
        o_turn = od("o_turn", [P, 2, T])
        o_p = od("o_p", [P, 2, 2, 2 * T])
        o_aT = od("o_aT", [P, 2, 2 * T])
        o_o = od("o_o", [P, 6, T])
        o_sq = od("o_sq", [P, 6, T])
        o_u = od("o_u", [P, 2, T + 2])
        o_c = od("o_c", [P, 2, T])
        o_st = od("o_st", [P, 12, 6])

        out_at = first.at
        h_out = Region(out_at)("h_out", [P, DC, T])
        hy = Region(overlay)
        h_small = hy("h_small", [P, NT, 84])
        h_yh = hy("h_yh", [P, 4, T], F32R)
        h_yl = hy("h_yl", [P, 4, T], F32R)
        h_merged = hy("h_merged", [P, DC, T])
        h_gate = hy("h_gate", [P, 2, T])
        h_prod = hy("h_prod", [P, 2, T])
        branch = hy.at
        hm = Region(branch)
        m_in = hm("m_in", [P, 12, T])
        m_cv = hm("m_cv", [P, 8, T])
        m_sw = hm("m_sw", [P, DC, 84])
        m_sw_h = hm("m_sw_h", [P, DC, 84], F32R)
        m_sw_l = hm("m_sw_l", [P, DC, 84], F32R)
        m_x = hm("m_x", [P, NT, 512])
        m_dt = hm("m_dt", [P, 6, 16])
        m_cs = hm("m_cs", [8, T])
        m_ncs = hm("m_ncs", [P, 16])
        m_e = hm("m_e", [P, 2, 384])
        m_y = hm("m_y", [P, 4, T])
        m_sq = hm("m_sq", [P, 4, T])
        m_d = hm("m_d", [P, 4])
        ha = Region(branch)
        a_qk = ha("a_qk", [P, 8, T])
        a_v = ha("a_v", [P, NT, 512])
        a_p = ha("a_p", [P, 2, T])
        a_pT = ha("a_pT", [P, 2, T])
        a_st = ha("a_st", [P, 16, 3])
        a_bias = ha("a_bias", [P, 2, 384])
        a_turn = ha("a_turn", [P, 2, T])
        a_f = ha("a_f", [P, 4, 16])
        a_cf = ha("a_cf", [8, T])
        a_iq = ha("a_iq", [P, 2, T])
        a_ik2 = ha("a_ik2", [P, NT, P])
        a_ik = ha("a_ik", [P, T])
        a_isc = ha("a_isc", [P, T])
        a_relu = ha("a_relu", [P, T])
        a_top = ha("a_top", [P, 8])
        a_w = ha("a_w", [P, NT, 4])

        ps = ctx.enter_context(nc.psum_tensor("ps", [P, 8, 512], F32))

        sems = {}

        def S(name):
            if name not in sems:
                sems[name] = ctx.enter_context(nc.semaphore(name))
            return sems[name]

        vec_at, row_parts, n = {}, [], 0
        for name, ap in io["vectors"]:
            r = ap.shape[0]
            vec_at[name] = n
            done = 0
            while done < r:
                m = min(r - done, P - n % P)
                row_parts.append((n // P, n % P, m, ap[done:done + m, :]))
                done += m
                n += m
        n_rows = n
        assert n_rows <= 512
        V = lambda name, i=0, k=1: vec[:, vec_at[name] + i:vec_at[name] + i + k]

        def e_keys(dr, q):
            sl = slice((1 - q) * T, (2 - q) * T)
            return (e_kd, e_qd) if dr == 0 else (e_z[:, 5:8, sl], e_z[:, 2:5, sl])

        class Count:
            def __init__(self):
                self.units = 0
                self.hidden = 0
                self.of = Counter()

            def add(self, **events):
                self.of.update(events)

        CREDIT = 2
        HALF_CREDIT = 2 * CREDIT

        def halves(i, u, h):
            return 4 * i + (2 * u + h + 1)

        def half_free(i, u, h):
            return halves(i, u - CREDIT, h) + HALF_CREDIT

        def sp_units(sp, c, pairs, source, width, beside=None):
            def pair(i):
                for s in range(2):
                    w = width[s] if isinstance(width, tuple) else width
                    for half in range(2):
                        sp.wait_ge(S("lo_ready"), half_free(i, c.units + s, half))
                        src = source(i, s, half)
                        dst = raw[:, s, half, 0:w // 2]
                        sp.dma_start(dst.rearrange("p (k n) -> p k n", n=src.shape[2]), src)\
                            .then_inc(S(f"raw_landed{s}{half}"), 16)
                    if beside:
                        beside(i, s)
            if pairs == 1:
                pair(0)
            else:
                with sp.Fori(0, pairs) as i:
                    pair(i)
            c.units += 2 * pairs

        def columns(w, k0, kc, n0, step, width):
            v = w[k0 * P:(k0 + kc) * P, :].rearrange("(c p) n -> p c n", p=P)
            return lambda i, s, half: v[:, half * kc // 2:(half + 1) * kc // 2,
                                        bass.ds(i * (2 * step) + (n0 + step * s), width)]

        def act_split(act, i, s, u, w=UNIT // 2):
            for h in range(2):
                act.wait_ge(S(f"raw_landed{s}{h}"), (i + u // 2) * 16 + 16)
                act.wait_ge(S("mm_done"), half_free(i, u, h))
                nc.scalar.activation(whi[:, s, h, 0:w], raw[:, s, h, 0:w], ACT.Copy).then_inc(S("hi_ready"), 1)

        def dve_split(dve, i, s, u, w=UNIT // 2):
            for h in range(2):
                dve.wait_ge(S("hi_ready"), halves(i, u, h))
                nc.vector.tensor_tensor(wlo[:, s, h, 0:w], raw[:, s, h, 0:w], whi[:, s, h, 0:w].bitcast(F32),
                                        ALU.subtract).then_inc(S("lo_ready"), 1)

        def pairs_of(eng, c, pairs, body, ahead=None, final=False, w=(UNIT // 2, UNIT // 2)):
            def pair(i, last):
                for s in range(2):
                    if ahead is not None and not (last and s == 1):
                        ahead(eng, i, 1 - s, c.units + s + 1, w[1 - s])
                    body(i, s)
            rolled = pairs - 1 if final else pairs
            if rolled >= 2:
                with eng.Fori(0, rolled) as i:
                    pair(i, False)
            elif rolled == 1:
                pair(0, False)
            if final:
                pair(pairs - 1, True)
            c.units += 2 * pairs

        def pe_banks_free(pe, c, i, s):
            pe.wait_ge(S("evac_done"), 2 * i + (c.units + s + 1))

        def pe_half_ready(pe, c, i, s, h):
            pe.wait_ge(S("lo_ready"), halves(i, c.units + s, h) + HALF_CREDIT)

        def three(dst, w_h, w_l, x_h, x_l, start, stop):
            nc.tensor.matmul(dst, w_h, x_h, start=start, stop=False)
            nc.tensor.matmul(dst, w_h, x_l, start=False, stop=False)
            return nc.tensor.matmul(dst, w_l, x_h, start=False, stop=stop)

        def half_of(s, h, chunks, width):
            v = lambda w: w[:, s, h, 0:chunks * width].rearrange("p (k n) -> p k n", n=width)
            return v(whi), v(wlo)

        def pe_blocks(pe, c, i, s, kc, n_tok, x_h, x_l, blocks, width, half_ready=None):
            pe_banks_free(pe, c, i, s)
            for h in range(2):
                pe_half_ready(pe, c, i, s, h)
                if half_ready:
                    half_ready(h)
                w_h, w_l = half_of(s, h, kc // 2, width)
                for b in range(blocks):
                    for j in range(kc // 2):
                        k = h * (kc // 2) + j
                        m = three(ps[:, 2 * s + b, 0:n_tok], w_h[:, j, b * P:(b + 1) * P],
                                  w_l[:, j, b * P:(b + 1) * P], x_h[:, k, 0:n_tok], x_l[:, k, 0:n_tok],
                                  k == 0, k == kc - 1)
                m.then_inc(S("mm_done"), 1)

        def pe_tokens(pe, c, i, s, kc, n_tiles, x_h, x_l, width):
            pe_banks_free(pe, c, i, s)
            flat = ps[:, 2 * s:2 * s + 2, :].rearrange("p a b -> p (a b)")
            for h in range(2):
                pe_half_ready(pe, c, i, s, h)
            for t in range(n_tiles):
                for k in range(kc):
                    w_h, w_l = half_of(s, 2 * k // kc, kc // 2, width)
                    tt, j = slice(t * P, (t + 1) * P), k % (kc // 2)
                    m = three(flat[:, t * width:(t + 1) * width], x_h[:, k, tt], x_l[:, k, tt],
                              w_h[:, j, :], w_l[:, j, :], k == 0, k == kc - 1)
            m.then_inc(S("mm_done"), 2)

        def unit_done(eng, c, i, s, h=1):
            eng.wait_ge(S("mm_done"), halves(i, c.units + s, h) + HALF_CREDIT)

        class Link:

            def __init__(self, eng, name):
                self.eng, self.sem, self.n = eng, S(name), 0

            def __call__(self, ins):
                self.n += 1
                ins.then_inc(self.sem, 1)
                self.eng.wait_ge(self.sem, self.n)

        def fm_evac(dst, c0, n_tok):
            def body(dve, c, i, s):
                unit_done(dve, c, i, s)
                nc.vector.tensor_copy(dst[:, bass.ds(i * 4 + (c0 + 2 * s), 2), 0:n_tok],
                                      ps[:, 2 * s:2 * s + 2, 0:n_tok]).then_inc(S("evac_done"), 1)
            return body

        def mod_columns(layer, m):
            v = io["ada_w"][layer].rearrange("(c p) n -> p c n", p=P)
            return v[:, :, bass.ds(m * 256, 256)]

        def mod_landings(layer, m0):
            return 16 * ((MOD_UNITS * layer + m0 - MOD_FIRST) // 2 + 1)

        def mod_sums(w, dst):
            for b in range(2):
                for k in range(DC):
                    m = nc.tensor.matmul(dst[:, 2 * b:2 * b + 2], w[:, k, b * P:(b + 1) * P], cond32[:, :, k],
                                         start=k == 0, stop=k == DC - 1)
            return m

        def parts(pairs, mod_part):
            if not mod_part:
                return [(0, pairs, None)]
            layer, m0, n = mod_part
            return [(0, n, (layer, m0))] + ([(n, pairs - n, None)] if n < pairs else [])


        schedule = []
        none = (None,) * 4
        beside = {("ffn1", 0): ((0, 8, 6), (0, 20, 4), (0, 28, 4), (1, 0, 4)),
                  ("ffn2", 0): ((1, 8, 6), (1, 20, 4), (1, 28, 4), None)}
        for layer, mixer, w_in in ((0, "even", io["even_w_in"][0]), (1, "odd", io["odd_w_in"][0])):
            nc_ = 2 - layer
            b0 = 8 * N_MOD * layer
            g = lambda n, l=layer: (lambda k, j: gains[:, l, n, k, j:j + 1])
            sh = lambda n, b0=b0: (lambda k, j: mod[:, b0 + 24 * n + k, j:j + 1])
            schedule += [
                ("gains", layer, 0, "norm_ffn1"),
                ("norm", hT, 2, sh(0), g(0)),
                ("ffn", io["ffn1_w_in"][layer], io["ffn1_w_out"][layer], 2 * T, (layer, 0), False,
                 beside.get(("ffn1", layer), none)),
                ("gains", layer, 1, "norm_mix"),
                ("norm", hT, 2, sh(1), g(1)),
                (mixer, w_in),
                ("out", io["mix_w_out"][layer], nc_ * T, layer),
                ("gains", layer, 2, "norm_ffn2"),
                ("norm", hT, nc_, sh(2), g(2)),
                ("ffn", io["ffn2_w_in"][layer], io["ffn2_w_out"][layer], nc_ * T, (layer, 2), False,
                 beside.get(("ffn2", layer), none)),
            ]
        schedule += [("renorm", hT, lambda k: V("final_norm", k))]
        for layer in range(2):
            gain = lambda name, l=layer: (lambda k, j=0: V(name, DC * l + k))
            w_in = io["w_in_2"][layer]
            schedule += [
                ("norm", hT, 1, None, gain("norm_mix_pre_2")),
                ("mamba", layer, w_in),
                ("merge", layer, 0),
                ("attention", layer, 0, w_in),
                ("merge", layer, 1),
                ("attention", layer, 1, w_in),
                ("merge", layer, 2),
                ("attention", layer, 2, w_in),
                ("merge", layer, 3),
                ("wout", layer, io["w_out_2"][layer]),
                ("renorm", h_out, gain("norm_mix_post_2")),
                ("norm", hT, 1, None, gain("norm_ffn_pre_2")),
                ("ffn", io["w_ffn_in_2"][layer], io["w_ffn_out_2"][layer], T, None, layer == 1, none),
                ("renorm", h_out, gain("norm_ffn_post_2")),
            ]
        schedule += [("store",)]

        block = ctx.enter_context(nc.Block())

        @block.sync
        def _(sp):
            c = Count()
            sp.dma_start(consts[:, :], io["consts"]).then_inc(S("consts_in"), 16)
            for tile, r0, m, src in row_parts:
                sp.dma_start(rows[r0:r0 + m, tile, :], src).then_inc(S("rows_in"), 16)
            for m in range(MOD_FIRST):
                sp.dma_start(mod_first[:, m, :, :], mod_columns(0, m)).then_inc(S(f"mod_first_landed{m // 2}"), 16)
            for t in range(NT):
                sp.dma_start(tok[:, t, :], io["x"][0, t * P:(t + 1) * P, :]).then_inc(S("tok_in"), 16)
                sp.dma_start(tok[:, NT + t, :], io["ctx"][0, t * P:(t + 1) * P, :]).then_inc(S("tok_in"), 16)
            for j, name in enumerate(("lambda_q1", "lambda_k1", "lambda_q2", "lambda_k2")):
                sp.dma_start(lam_in[:, j:j + 1], io[name].rearrange("a d -> d a")).then_inc(S("lam_landed"), 16)
            for j, name in enumerate(("dt_bias_2", "a_log_2", "fox_fbias_2", "d_skip_2")):
                sp.dma_start(small_rows[0:1, 16 * j:16 * j + 16],
                             io[name].rearrange("(o l) h -> o (l h)", o=1)).then_inc(S("lam_landed"), 16)

            def mod_unit(layer, m0):
                def load(i, s):
                    sp.wait_ge(S("mod_mm"), 2 * i + (MOD_UNITS * layer + m0 + s - 1))
                    sp.dma_start(mod_w[:, s, :, :], mod_columns(layer, i * 2 + (m0 + s))).then_inc(S(f"mod_landed{s}"), 16)
                return load

            def ffn(w_in, w_out, mods):
                v = w_in.rearrange("(c p) (g f) -> p c g f", p=P, g=2)
                j0 = 0
                for n, half in enumerate(HALVES):
                    up = lambda p0: lambda i, s, g: v[:, :, g, bass.ds(i * 256 + (j0 + 2 * p0 + s) * P, P)]
                    for p0, pairs, mod_part in parts(half // 2, mods[2 * n]):
                        sp_units(sp, c, pairs, up(p0), UNIT, mod_part and mod_unit(*mod_part))
                    for p0, pairs, mod_part in parts(4, mods[2 * n + 1]):
                        sp_units(sp, c, pairs, columns(w_out, j0, half, 2 * p0 * P, P, P), half * P,
                                 mod_part and mod_unit(*mod_part))
                    j0 += half


            def even(w_in):
                sp_units(sp, c, 2, columns(w_in, 0, DC, 0, 256, 256), UNIT)
                sp.wait_ge(S("norm_lo"), c.of["norm_hi"])
                sp.dma_start(e_small[:, :, :], w_in[:, 2560:2592].rearrange("(c p) n -> p c n", p=P))\
                    .then_inc(S("e_small_in"), 16)
                sp.wait_ge(S("e_gw_zero"), 1)
                for dr in range(2):
                    sp.dma_start(e_gw[16 * dr:16 * dr + 16, dr, :], io["gla_gate_w"][0, dr, :, :])\
                        .then_inc(S("e_gw_in"), 16)
                    sp.dma_start(e_gw[32:33, dr, :], io["gla_gate_b"][0, dr:dr + 1, :]).then_inc(S("e_gw_in"), 16)
                v = w_in.rearrange("(c p) n -> p c n", p=P)
                sp_units(sp, c, 3, lambda i, s, half: v[:, 4 * half:4 * half + 4,
                                                        bass.ds(i * 256 + (1792, 1024)[s], 256)], UNIT)

            def odd(w_in):
                v = w_in.rearrange("(c p) n -> p c n", p=P)
                for lo, hi in ((0, 768), (1536, 2304)):
                    sp_units(sp, c, 3, lambda i, s, half: v[:, 4 * half:4 * half + 4,
                                                            bass.ds(i * 256 + (lo, hi)[s], 256)], UNIT)

            def mamba(layer, w_in):
                sp_units(sp, c, 3, columns(w_in, 0, DC, Z0, 256, 256), UNIT)
                sp.wait_ge(S("norm_lo"), c.of["norm_hi"])
                for at, n0, n in ((0, DT0, 8), (8, FF0, 8), (16, IK0, 68)):
                    sp.dma_start(m_sw[:, :, at:at + n], w_in[:, n0:n0 + n].rearrange("(c p) n -> p c n", p=P))\
                        .then_inc(S("m_sw_in"), 16)

            def attention(layer, which, w_in):
                q0, v0 = ((FQ0, FV0), (MQ0, MV0), (DQ0, DV0))[which]
                sp_units(sp, c, 2, columns(w_in, 0, DC, q0, 256, 256), UNIT)
                sp_units(sp, c, 1, columns(w_in, 0, DC, v0, 256, 256), UNIT)
                if which == 2:
                    sp_units(sp, c, 1, columns(w_in, 0, DC, IQ0, P, P), DC * P)

            def merge(layer, n):
                gate = columns(io["w_gate_2"][layer], 0, DC, n * D, P, 256)
                proj = columns(io["w_branch_2"][layer, n], 0, 4, -P, P, 256)
                sp_units(sp, c, 4, lambda i, s, half: (gate, proj)[s](i, s, half), (UNIT, UNIT // 2))

            for stage, *args in schedule:
                if stage == "norm":
                    c.add(norm_hi=DC * args[1])
                elif stage == "ffn":
                    ffn(args[0], args[1], args[5])
                elif stage in ("even", "odd"):
                    {"even": even, "odd": odd}[stage](*args)
                elif stage == "out":
                    sp_units(sp, c, 2, columns(args[0], 0, DC, 0, 256, 256), UNIT)
                elif stage == "mamba":
                    mamba(*args)
                elif stage == "attention":
                    attention(*args)
                elif stage == "merge":
                    merge(*args)
                elif stage == "wout":
                    sp_units(sp, c, 2, columns(args[1], 0, DC, 0, 256, 256), UNIT)
                elif stage == "store":
                    sp.wait_ge(S("y_copied"), 2)
                    for t in range(NT):
                        sp.dma_start(io["out"][0, t * P:(t + 1) * P, :], y_tok[:, t, :]).then_inc(S("stored"), 16)
                    sp.wait_ge(S("stored"), 16 * NT)

        @block.tensor
        def _(pe):
            c = Count()
            pe.sem_inc(S("mm_done"), HALF_CREDIT)
            ident = K("ident")
            pe.wait_ge(S("consts_in"), 16)
            pe.wait_ge(S("rows_in"), 16 * len(row_parts))
            for t in range((n_rows + P - 1) // P):
                m = min(P, n_rows - t * P)
                ins = nc.tensor.transpose(ps[:, 7, t * P:t * P + m], rows[0:m, t, :], ident[0:m, 0:m])
            ins.then_inc(S("vec_t"), 1)
            pe.wait_ge(S("tok_in"), 16 * 2 * NT)
            for k in range(DC):
                if k == 7:
                    pe.wait_ge(S("vec_ready"), 1)
                for t in range(2 * NT):
                    ins = nc.tensor.transpose(ps[:, k, t * P:(t + 1) * P], tok[:, t, k * P:(k + 1) * P], ident)
                ins.then_inc(S("h_t"), 1)
            pe.wait_ge(S("lam_prod"), 1)
            pe.wait_ge(S("h_in"), DC)
            nc.tensor.matmul(ps[:, 6, 0:2], K("ones")[0:HD, :], lam_prod[:, :], start=True, stop=True)
            nc.tensor.matmul(ps[:, 6, 64:128], K("ones")[0:1, :], small_rows[0:1, :], start=True, stop=True)\
                .then_inc(S("bcast_mm"), 1)
            pe.wait_ge(S("cond32"), 1)
            for m in range(MOD_FIRST):
                if m % 2 == 0:
                    pe.wait_ge(S(f"mod_first_landed{m // 2}"), 32)
                ins = mod_sums(mod_first[:, m, :, :], ps[:, 5, 4 * m:4 * m + 4])
            ins.then_inc(S("mod_mm"), MOD_FIRST)

            def mod_unit(layer, m0):
                def multiply(i, s):
                    pe.wait_ge(S(f"mod_landed{s}"), 16 * i + mod_landings(layer, m0))
                    pe.wait_ge(S("mod_evac"), 2 * i + (MOD_UNITS * layer + m0 + s - 1))
                    mod_sums(mod_w[:, s, :, :], ps[:, 6 + s, 0:4]).then_inc(S("mod_mm"), 1)
                return multiply

            def squares(nc_):
                o = c.of
                n = T * nc_
                for k in range(DC):
                    if k % 4 == 0:
                        pe.wait_ge(S("sq_ready"), o["norm"] * 2 + k // 4 + 1)
                    ins = nc.tensor.matmul(ps[:, 4, 0:n], K("ones"), sq[:, k, 0:n], start=k == 0, stop=k == DC - 1)
                ins.then_inc(S("ss_ready"), 1)

            def ffn(n_tok, mods):
                for n, half in enumerate(HALVES):
                    def up(i, s):
                        pe_banks_free(pe, c, i, s)
                        for g in range(2):
                            pe_half_ready(pe, c, i, s, g)
                            w_h, w_l = half_of(s, g, DC, P)
                            for k in range(DC):
                                m = three(ps[:, 2 * s + g, 0:n_tok], w_h[:, k, :], w_l[:, k, :],
                                          xh[:, k, 0:n_tok], xl[:, k, 0:n_tok], k == 0, k == DC - 1)
                            m.then_inc(S("mm_done"), 1)
                    hidden = c.hidden + CREDIT
                    def down(i, s):
                        pe_blocks(pe, c, i, s, half, n_tok, hid_h, hid_l, 1, P,
                                  lambda h: pe.wait_ge(S("hid_l_ready"), hidden + (h + 1) * half // 2))
                    for body, total, mod_part in ((up, half // 2, mods[2 * n]), (down, 4, mods[2 * n + 1])):
                        for _, pairs, part in parts(total, mod_part):
                            beside = part and mod_unit(*part)
                            pairs_of(pe, c, pairs, lambda i, s: (body(i, s), beside and beside(i, s)))
                    c.hidden += half


            def even():
                pairs_of(pe, c, 2, lambda i, s: pe_blocks(pe, c, i, s, DC, 2 * T, xh, xl, 2, 256))
                def r_and_v(i, s):
                    if s == 0:
                        pe_blocks(pe, c, i, s, DC, 2 * T, xh, xl, 2, 256)
                    else:
                        pe_tokens(pe, c, i, s, DC, 2 * NT, xh, xl, 256)
                pairs_of(pe, c, 3, r_and_v)
                pe.wait_ge(S("e_small_lo"), 1)
                for t in range(2 * NT):
                    tt = slice(t * P, (t + 1) * P)
                    for k in range(DC):
                        m = three(ps[:, 5, t * 32:(t + 1) * 32], xh[:, k, tt], xl[:, k, tt],
                                  e_small_h[:, k, :], e_small_l[:, k, :], k == 0, k == DC - 1)
                m.then_inc(S("e_gates_mm"), 1)
                pe.wait_ge(S("e_gtok"), 1)
                for t in range(2 * NT):
                    m = nc.tensor.transpose(ps[0:32, 6, t * P:(t + 1) * P], e_gtok[:, t, :], ident)
                m.then_inc(S("e_gates_t"), 1)
                pe.wait_ge(S("e_gT"), 1)
                pe.wait_ge(S("e_gw_in"), 16 * 4)
                pe.wait_ge(S("evac_done"), c.units + CREDIT)

                for q in range(2):
                    tile0 = (NT, 0)[q]
                    for n in range(4):
                        it, tile, dr = 4 * q + n, tile0 + n // 2, n % 2
                        if it >= 2:
                            pe.wait_ge(S("e_log"), it - 1)
                        nc.tensor.matmul(ps[:, dr, 0:384], e_gT[:, tile * P:(tile + 1) * P], e_gw[:, dr, :],
                                         start=True, stop=True).then_inc(S("e_logits"), 1)
                        pe.wait_ge(S("e_log"), it + 1)
                        if n == 0 and q:
                            pe.wait_ge(S("e_state"), 8 * q)
                        if it:
                            pe.wait_ge(S("e_exp"), it)
                        for p in range(3):
                            m = nc.tensor.matmul(ps[:, 2, p * P:(p + 1) * P], e_log[:, it % 2, p * P:(p + 1) * P],
                                                 K(("cum_fwd", "cum_bwd")[dr]), start=True, stop=True)
                        m.then_inc(S("e_cum"), 1)
                        pe.wait_ge(S("e_decayed"), it + 1)
                        if it:
                            pe.wait_ge(S("e_kkT"), it)
                        if n == 0 and q:
                            pe.wait_ge(S("e_oroot"), 3 * q)
                        for p in range(3):
                            m = nc.tensor.transpose(ps[:, 3, p * P:(p + 1) * P], e_kk[:, p, :], ident)
                        m.then_inc(S("e_kk_t"), 1)
                    pe.wait_ge(S("e_kkT"), 4 * q + 4)
                    pe.wait_ge(S("e_exp"), 4 * q + 4)
                    if q:
                        pe.wait_ge(S("e_y"), 3 * q)
                    for step in range(8):
                        dr = step % 2
                        ch = step // 2 if dr == 0 else 3 - step // 2
                        if step >= 2 or q:
                            pe.wait_ge(S("e_state"), 8 * q + step - 1)
                        rows_ = slice(64 * (ch % 2), 64 * (ch % 2) + 64)
                        for h in range(6):
                            m = nc.tensor.matmul(
                                ps[64 * (h % 2):64 * (h % 2) + 64, (6, 2)[dr], (h // 2) * P:(h // 2 + 1) * P],
                                e_kkT[rows_, dr, ch // 2, h * 64:(h + 1) * 64],
                                e_v[rows_, tile0 + ch // 2, h * P:(h + 1) * P], start=True, stop=True)
                        m.then_inc(S("e_kv"), 1)
                    pe.wait_ge(S("e_state"), 8 * q + 8)
                    for p in range(3):
                        o = 3 * q + p
                        if o:
                            pe.wait_ge(S("e_att"), o)
                        for dr in range(2):
                            kd, qd = e_keys(dr, q)
                            for t in range(NT):
                                tt = slice(t * P, (t + 1) * P)
                                for h in range(2):
                                    hh = slice(64 * h, 64 * h + 64)
                                    m = nc.tensor.matmul(ps[:, 4 + h, (2 * dr + t) * P:(2 * dr + t + 1) * P],
                                                         kd[hh, p, tt], qd[hh, p, tt], start=True, stop=True)
                        m.then_inc(S("e_att_mm"), 1)
                        pe.wait_ge(S("e_att"), o + 1)
                        if o:
                            pe.wait_ge(S("e_y"), o)
                        for h in range(2):
                            hh = slice(64 * h, 64 * h + 64)
                            for t in range(NT):
                                dst = ps[:, 6 + h, t * P:(t + 1) * P]
                                vv = e_v[:, tile0 + t, (2 * p + h) * P:(2 * p + h + 1) * P]
                                for dr in range(2):
                                    nc.tensor.matmul(dst, vv, e_att[:, h, (2 * dr + t) * P:(2 * dr + t + 1) * P],
                                                     start=dr == 0, stop=False)
                                for dr in range(2):
                                    qd = e_keys(dr, q)[1]
                                    for half in range(2):
                                        ch = 2 * t + half
                                        cc = slice(ch * 64, ch * 64 + 64)
                                        m = nc.tensor.matmul(ps[:, 6 + h, ch * 64:ch * 64 + 64],
                                                             e_S[hh, dr, ch if dr == 0 else 3 - ch, p, :],
                                                             qd[hh, p, cc], start=False,
                                                             stop=dr == 1 and half == 1)
                        m.then_inc(S("e_o"), 1)
                        pe.wait_ge(S("e_osq"), o + 1)
                        if o:
                            pe.wait_ge(S("e_oroot"), o)
                        nc.tensor.matmul(ps[:, 3, :], K("ones"), e_osq[:, :], start=True, stop=True)\
                            .then_inc(S("e_oss"), 1)
                pe.wait_ge(S("e_oroot"), 6)
                for n in range(4):
                    q, k = divmod(n, 2)
                    if n:
                        pe.wait_ge(S("e_fab"), n)
                    for t in range(NT):
                        m = nc.tensor.matmul(ps[:, 0, t * T:(t + 1) * T],
                                             e_z[:, k, q * T + t * P:q * T + (t + 1) * P],
                                             consts[:, const_at["dft_cos"][0]:const_at["dft_sin"][1]],
                                             start=True, stop=True)
                    m.then_inc(S("e_f1"), 1)
                    pe.wait_ge(S("e_fab"), n + 1)
                    if n:
                        pe.wait_ge(S("e_fl"), n)
                    for t in range(NT):
                        nc.tensor.matmul(ps[:, 1, 0:T], e_ab[:, t, 0:P], K("dft_tok_cos")[:, t * T:(t + 1) * T],
                                         start=t == 0, stop=False)
                        m = nc.tensor.matmul(ps[:, 1, 0:T], e_ab[:, t, P:2 * P],
                                             K("dft_tok_nsin")[:, t * T:(t + 1) * T],
                                             start=False, stop=t == NT - 1)
                    m.then_inc(S("e_f2"), 1)
                pe.wait_ge(S("e_fl"), 4)
                pe.wait_ge(S("e_yl"), 6)

            def odd():
                pairs_of(pe, c, 3, lambda i, s: pe_blocks(pe, c, i, s, DC, T, xh, xl, 2, 256))
                def k_and_v(i, s):
                    if s == 0:
                        pe_blocks(pe, c, i, s, DC, 2 * T, xh, xl, 2, 256)
                    else:
                        pe_tokens(pe, c, i, s, DC, 2 * NT, xh, xl, 256)
                pairs_of(pe, c, 3, k_and_v)
                pe.wait_ge(S("evac_done"), c.units + CREDIT)
                for n in range(6):
                    buf, k = (o_q, 2 * n) if n < 3 else (o_k, 2 * n - 6)
                    for j in range(2):
                        m = nc.tensor.matmul(ps[:, n, j * T:(j + 1) * T], K("axial_swap"), buf[:, k + j, 0:T],
                                             start=True, stop=True)
                    m.then_inc(S("o_swap"), 1)

                def scores(e):
                    h, qt = divmod(e, 2)
                    if e >= 2:
                        pe.wait_ge(S("o_exp"), e - 1)
                    for s in range(2):
                        rr = slice(64 * s, 64 * s + 64)
                        m = nc.tensor.matmul(ps[:, 4 + 2 * (e % 2) + s, :], o_q[rr, h, qt * P:(qt + 1) * P],
                                             o_k[rr, h, :], start=True, stop=True)
                    m.then_inc(S("o_scores"), 1)

                pe.wait_ge(S("o_turned"), 6)
                scores(0)
                for e in range(12):
                    h, qt = divmod(e, 2)
                    if e + 1 < 12:
                        scores(e + 1)
                    pe.wait_ge(S("o_a"), e + 1)
                    if e >= 2:
                        pe.wait_ge(S("o_aT"), e - 1)
                    for kt in range(2 * NT):
                        m = nc.tensor.transpose(ps[:, 2 + e % 2, kt * P:(kt + 1) * P],
                                                o_p[:, e % 2, 0, kt * P:(kt + 1) * P], ident)
                    m.then_inc(S("o_t"), 1)
                    pe.wait_ge(S("o_aT"), e + 1)
                    if qt == 0 and h >= 2:
                        pe.wait_ge(S("o_out"), h - 1)
                    for kt in range(2 * NT):
                        m = nc.tensor.matmul(ps[:, h % 2, qt * P:(qt + 1) * P], o_v[:, kt, h * P:(h + 1) * P],
                                             o_aT[:, e % 2, kt * P:(kt + 1) * P],
                                             start=kt == 0, stop=kt == 2 * NT - 1)
                    m.then_inc(S("o_pv"), 1)
                pe.wait_ge(S("o_sq"), 1)
                for p in range(3):
                    m = nc.tensor.matmul(ps[:, 4 + p, :], K("ones"),
                                         o_sq[:, 2 * p:2 * p + 2, :].rearrange("p a b -> p (a b)"),
                                         start=True, stop=True)
                m.then_inc(S("o_ss"), 1)
                pe.wait_ge(S("o_yl"), 2)

            def fm_pairs(pairs, kc, blocks, width, x_h=xh, x_l=xl):
                pairs_of(pe, c, pairs, lambda i, s: pe_blocks(pe, c, i, s, kc, T, x_h, x_l, blocks, width))

            def mamba(layer):
                fm_pairs(3, DC, 2, 256)
                pe.wait_ge(S("m_sw_lo"), layer + 1)
                for t in range(NT):
                    tt = slice(t * P, (t + 1) * P)
                    for k in range(DC):
                        m = three(ps[:, 5, t * 84:(t + 1) * 84], xh[:, k, tt], xl[:, k, tt],
                                  m_sw_h[:, k, :], m_sw_l[:, k, :], k == 0, k == DC - 1)
                m.then_inc(S("m_small_mm"), 1)
                pe.wait_ge(S("evac_done"), c.units + CREDIT)
                pe.wait_ge(S("m_dta"), layer + 1)
                for t in range(NT):
                    nc.tensor.matmul(ps[0:8, 2, 0:T], m_dt[:, 4, 8 * t:8 * t + 8], K("cum_all")[:, t * T:(t + 1) * T],
                                     start=t == 0, stop=t == NT - 1)
                for o in range(NT):
                    for t in range(NT):
                        m = nc.tensor.matmul(ps[:, 3, 8 * o:8 * o + 8],
                                             K("cum_all")[:, t * T + o * P:t * T + (o + 1) * P],
                                             m_dt[:, 4, 8 * t:8 * t + 8], start=t == 0, stop=t == NT - 1)
                m.then_inc(S("m_cs_mm"), 1)
                pe.wait_ge(S("m_conv"), layer + 1)
                pe.wait_ge(S("m_small"), layer + 1)
                for t in range(NT):
                    for k in range(4):
                        m = nc.tensor.transpose(ps[:, 4 + t, k * P:(k + 1) * P], m_cv[:, k, t * P:(t + 1) * P], ident)
                m.then_inc(S("m_x_t"), 1)
                for g in range(2):
                    for t in range(NT):
                        m = nc.tensor.matmul(ps[:, g, t * T:(t + 1) * T], m_cv[:, 4 + g, t * P:(t + 1) * P],
                                             m_cv[:, 6 + g, :], start=True, stop=True)
                m.then_inc(S("m_cb"), 1)
                pe.wait_ge(S("m_x"), layer + 1)
                pe.wait_ge(S("m_cs"), layer + 1)

                def spread(h):
                    if h >= 2:
                        pe.wait_ge(S("m_seg"), 8 * layer + h - 1)
                    nc.tensor.matmul(ps[:, 4 + h % 2, 0:T], K("spread")[0:8, h * P:(h + 1) * P], m_cs[:, :],
                                     start=True, stop=True).then_inc(S("m_row"), 1)
                spread(0)
                for h in range(8):
                    if h + 1 < 8:
                        spread(h + 1)
                    pe.wait_ge(S("m_score"), 8 * layer + h + 1)
                    p = h // 2
                    if h % 2 == 0 and p >= 2:
                        pe.wait_ge(S("m_y"), 4 * layer + p - 1)
                    hh = slice(64 * (h % 2), 64 * (h % 2) + 64)
                    nc.tensor.matmul(ps[hh, 6 + p % 2, 0:T], m_x[:, 0, h * 64:(h + 1) * 64], m_e[:, h % 2, 0:T],
                                     start=True, stop=False)
                    nc.tensor.matmul(ps[hh, 6 + p % 2, P:T], m_x[:, 1, h * 64:(h + 1) * 64], m_e[:, h % 2, T:T + P],
                                     start=False, stop=True).then_inc(S("m_o"), 1)
                pe.wait_ge(S("m_sq"), layer + 1)
                for g in range(2):
                    for k in range(2):
                        m = nc.tensor.matmul(ps[:, 2 + g, 0:T], K("ones"), m_sq[:, 2 * g + k, :],
                                             start=k == 0, stop=k == 1)
                m.then_inc(S("m_ss"), 1)
                pe.wait_ge(S("m_yl"), layer + 1)

            def turn(buf, k, n_chunks, bank):
                for j in range(n_chunks):
                    x = buf[:, k + j, :] if n_chunks == 2 else buf[:, :]
                    m = nc.tensor.matmul(ps[:, bank, j * T:(j + 1) * T], K("rope_swap"), x, start=True, stop=True)
                m.then_inc(S("a_swap"), 1)

            def attention(layer, which):
                a = 3 * layer + which
                fm_pairs(2, DC, 2, 256)
                pairs_of(pe, c, 1, lambda i, s: pe_tokens(pe, c, i, s, DC, NT, xh, xl, 256))
                if which == 2:
                    fm_pairs(1, DC, 1, P)
                pe.wait_ge(S("evac_done"), c.units + CREDIT)
                if which == 0:
                    pe.wait_ge(S("a_logf"), layer + 1)
                    for t in range(NT):
                        nc.tensor.matmul(ps[0:8, 2, 0:T], a_f[:, 2, 8 * t:8 * t + 8],
                                         K("cum_all")[:, t * T:(t + 1) * T], start=t == 0, stop=t == NT - 1)
                    for o in range(NT):
                        for t in range(NT):
                            m = nc.tensor.matmul(ps[:, 3, 8 * o:8 * o + 8],
                                                 K("cum_all")[:, t * T + o * P:t * T + (o + 1) * P],
                                                 a_f[:, 2, 8 * t:8 * t + 8], start=t == 0, stop=t == NT - 1)
                    m.then_inc(S("a_cf_mm"), 1)
                    pe.wait_ge(S("a_cf"), layer + 1)
                else:
                    r0 = 10 * layer + (0, 0, 4)[which]
                    for n in range(4):
                        turn(a_qk, 2 * n, 2, n)
                    if which == 2:
                        turn(a_iq, 0, 2, 4)
                        pe.wait_ge(S("a_ik2"), layer + 1)
                        for t in range(NT):
                            m = nc.tensor.transpose(ps[:, 6, t * P:(t + 1) * P], a_ik2[:, t, :], ident)
                        m.then_inc(S("a_ik_t"), 1)
                        pe.wait_ge(S("a_ik"), layer + 1)
                        turn(a_ik, 0, 1, 5)
                    pe.wait_ge(S("a_turned"), r0 + (0, 4, 6)[which])
                    if which == 2:
                        for qt in range(NT):
                            if qt:
                                pe.wait_ge(S("a_isc"), NT * layer + qt)
                            for h in range(4):
                                hh = slice(64 * (h % 2), 64 * (h % 2) + 64)
                                m = nc.tensor.matmul(ps[:, 4 + h, 0:(qt + 1) * P], a_iq[hh, h // 2, qt * P:(qt + 1) * P],
                                                     a_ik[hh, 0:(qt + 1) * P], start=True, stop=True)
                            m.then_inc(S("a_idx"), 1)
                        pe.wait_ge(S("a_isc"), NT * layer + NT)

                def spread(h):
                    if h >= 2:
                        pe.wait_ge(S("a_bias"), 8 * layer + h - 1)
                    nc.tensor.matmul(ps[:, 2 + h % 2, 0:T], K("spread")[0:8, h * P:(h + 1) * P], a_cf[:, :],
                                     start=True, stop=True).then_inc(S("a_row"), 1)

                def scores(e):
                    h, qt = divmod(e, 2)
                    if which == 0 and qt == 0:
                        spread(h)
                    if e >= 2:
                        pe.wait_ge(S("a_max"), 16 * a + e - 1)
                    hh = slice(64 * (h % 2), 64 * (h % 2) + 64)
                    nc.tensor.matmul(ps[:, 4 + e % 2, 0:(qt + 1) * P], a_qk[hh, h // 2, qt * P:(qt + 1) * P],
                                     a_qk[hh, 4 + h // 2, 0:(qt + 1) * P], start=True, stop=True)\
                        .then_inc(S("a_scores"), 1)

                scores(0)
                for e in range(16):
                    h, qt = divmod(e, 2)
                    p = h // 2
                    if e + 1 < 16:
                        scores(e + 1)
                    pe.wait_ge(S("a_p"), 16 * a + e + 1)
                    if e >= 2:
                        pe.wait_ge(S("a_pT"), 16 * a + e - 1)
                    for kt in range(qt + 1):
                        m = nc.tensor.transpose(ps[:, 6 + e % 2, kt * P:(kt + 1) * P],
                                                a_p[:, e % 2, kt * P:(kt + 1) * P], ident)
                    m.then_inc(S("a_t"), 1)
                    pe.wait_ge(S("a_pT"), 16 * a + e + 1)
                    if e % 4 == 0 and p >= 2:
                        pe.wait_ge(S("a_yl"), 4 * a + p - 1)
                    hh = slice(64 * (h % 2), 64 * (h % 2) + 64)
                    for kt in range(qt + 1):
                        m = nc.tensor.matmul(ps[hh, p % 2, qt * P:(qt + 1) * P], a_v[:, kt, h * 64:(h + 1) * 64],
                                             a_pT[:, e % 2, kt * P:(kt + 1) * P], start=kt == 0, stop=kt == qt)
                    m.then_inc(S("a_pv"), 1)
                pe.wait_ge(S("a_yl"), 4 * a + 4)

            def merge(layer, n):
                def unit(i, s):
                    if s == 0:
                        pe_blocks(pe, c, i, 0, DC, T, xh, xl, 2, 256)
                    else:
                        pe_blocks(pe, c, i, 1, 4, T, h_yh, h_yl, 2, 256)
                pairs_of(pe, c, 4, unit)

            for stage, *args in schedule:
                if stage == "norm":
                    squares(args[1])
                    c.add(norm=1, norm_hi=DC * args[1])
                    pe.wait_ge(S("norm_lo"), c.of["norm_hi"])
                elif stage == "renorm":
                    squares(1)
                    c.add(norm=1, renorm=1)
                elif stage == "ffn":
                    ffn(args[2], args[5])
                elif stage == "even":
                    even()
                elif stage == "odd":
                    odd()
                elif stage == "out":
                    pairs_of(pe, c, 2, lambda i, s: pe_blocks(pe, c, i, s, DC, args[1], xh, xl, 2, 256))
                elif stage == "mamba":
                    mamba(args[0])
                elif stage == "attention":
                    attention(args[0], args[1])
                elif stage == "merge":
                    merge(*args)
                elif stage == "wout":
                    pe.wait_ge(S("h_merged_lo"), args[0] + 1)
                    fm_pairs(2, DC, 2, 256)
                elif stage == "store":
                    pe.wait_ge(S("evac_done"), c.units + CREDIT)
                    if c.of["renorm"]:
                        pe.wait_ge(S("renormed"), c.of["renorm"])
                    for t in range(NT):
                        for k in range(DC):
                            ins = nc.tensor.transpose(ps[:, 2 * t + k // 4, (k % 4) * P:(k % 4 + 1) * P],
                                                      hT[:, k, t * P:(t + 1) * P], ident)
                        ins.then_inc(S("y_t"), 1)

        @block.scalar
        def _(act):
            c = Count()
            link = Link(act, "act_link")
            act.wait_ge(S("vec_ready"), 1)
            nc.scalar.activation(cond32[:, 0, :], V("c", 0, DC), ACT.Silu)
            nc.scalar.activation(cond32[:, 1, :], V("c_ctx", 0, DC), ACT.Silu).then_inc(S("cond32"), 1)
            act.wait_ge(S("bcast_mm"), 1)
            nc.scalar.activation(lam[:, 0:2], ps[:, 6, 0:2], ACT.Exp).then_inc(S("lam_exp"), 1)
            act_split(act, 0, 0, 0)

            def root_of_squares(src, nc_):
                o = c.of
                n = T * nc_
                act.wait_ge(S("evac_done"), c.units + CREDIT)
                if o["renorm"]:
                    act.wait_ge(S("renormed"), o["renorm"])
                if o["norm_hi"]:
                    act.wait_ge(S("norm_lo"), o["norm_hi"])
                for q in range(2):
                    nc.scalar.activation(sq[:, 4 * q:4 * q + 4, 0:n], src[:, 4 * q:4 * q + 4, 0:n],
                                         ACT.Square).then_inc(S("sq_ready"), 1)
                act.wait_ge(S("ss_ready"), o["norm"] + 1)
                nc.scalar.activation(root[:, 0:n], ps[:, 4, 0:n], ACT.Sqrt, bias=K("eps"), scale=1.0 / D)\
                    .then_inc(S("root_ready"), 1)

            def norm(src, nc_, shift, gain):
                o = c.of
                root_of_squares(src, nc_)
                for k in range(DC):
                    for j in range(nc_):
                        e = o["norm_hi"] + k * nc_ + j
                        act.wait_ge(S("norm_prod"), e + 1)
                        sl = slice(j * T, (j + 1) * T)
                        nc.scalar.activation(xh[:, k, sl], sq[:, k, sl], ACT.Identity,
                                             bias=shift(k, j) if shift else 0.0).then_inc(S("norm_hi"), 1)
                c.add(norm=1, norm_hi=DC * nc_)

            def ffn(n_tok, final, mods):
                for n, half in enumerate(HALVES):
                    def up(i, s):
                        unit_done(act, c, i, s, 0)
                        nc.scalar.activation(act32[:, s, 0:n_tok], ps[:, 2 * s, 0:n_tok], ACT.Silu)\
                            .then_inc(S("act_ready"), 1)
                        act.wait_ge(S("evac_done"), 2 * i + (c.units + s + 1 + CREDIT))
                        nc.scalar.activation(hid_h[:, bass.ds(i * 2 + (hid0 + s), 1), 0:n_tok],
                                             hid32[:, s:s + 1, 0:n_tok], ACT.Copy).then_inc(S("hid_h_ready"), 1)
                    hid0 = 0
                    for p0, pairs, _ in parts(half // 2, mods[2 * n]):
                        hid0 = 2 * p0
                        pairs_of(act, c, pairs, up, ahead=act_split)
                    c.hidden += half
                    for _, pairs, _ in parts(4, mods[2 * n + 1]):
                        pairs_of(act, c, pairs, lambda i, s: None, ahead=act_split, final=final and n == 1)


            def even():
                pairs_of(act, c, 2, lambda i, s: None, ahead=act_split)
                pairs_of(act, c, 3, lambda i, s: None, ahead=act_split)
                act.wait_ge(S("e_small_in"), 16)
                nc.scalar.activation(e_small_h[:, :, :], e_small[:, :, :], ACT.Copy).then_inc(S("e_small_hi"), 1)
                act.wait_ge(S("evac_done"), c.units + CREDIT)
                nc.scalar.activation(e_r[:, :, :], e_r[:, :, :], ACT.Silu).then_inc(S("e_silu"), 1)
                for q in range(2):
                    for n in range(4):
                        it, dr = 4 * q + n, n % 2
                        act.wait_ge(S("e_logits"), it + 1)
                        if it:
                            act.wait_ge(S("e_log"), it)
                        link(nc.scalar.activation(e_abs[:, :], ps[:, dr, 0:384], ACT.Abs))
                        link(nc.scalar.activation(e_abs[:, :], e_abs[:, :], ACT.Exp, scale=-1.0))
                        nc.scalar.activation(e_abs[:, :], e_abs[:, :], ACT.Ln, bias=1.0).then_inc(S("e_ln"), 1)
                        act.wait_ge(S("e_cum"), it + 1)
                        if it:
                            act.wait_ge(S("e_decayed"), it)
                        flat = ps[:, 2, 0:384].rearrange("p (a b) -> p a b", b=P)
                        nc.scalar.activation(e_up[:, :, :], flat, ACT.Exp, scale=1.0 / 16)
                        nc.scalar.activation(e_dn[:, :, :], flat, ACT.Exp, scale=-1.0 / 16).then_inc(S("e_exp"), 1)
                        act.wait_ge(S("e_kk_t"), it + 1)
                        if q and n == 0:
                            act.wait_ge(S("e_kv"), 8 * q)
                        nc.scalar.activation(e_kkT[:, dr, n // 2, :], ps[:, 3, 0:384], ACT.Copy)\
                            .then_inc(S("e_kkT"), 1)
                    for p in range(3):
                        o = 3 * q + p
                        act.wait_ge(S("e_o"), o + 1)
                        if o:
                            act.wait_ge(S("e_oss"), o)
                        nc.scalar.activation(e_osq[:, :].rearrange("p (a b) -> p a b", a=2), ps[:, 6:8, 0:T], ACT.Square).then_inc(S("e_osq"), 1)
                        act.wait_ge(S("e_oss"), o + 1)
                        if o:
                            act.wait_ge(S("e_y"), o)
                        nc.scalar.activation(root[:, :], ps[:, 3, :], ACT.Sqrt, bias=K("eps"), scale=1.0 / P)\
                            .then_inc(S("e_oroot"), 1)
                        act.wait_ge(S("e_y"), o + 1)
                        sl = slice((1 - q) * T, (2 - q) * T)
                        nc.scalar.activation(xh[:, 2 + 2 * p:4 + 2 * p, sl],
                                             e_y[:, :].rearrange("p (a b) -> p a b", a=2), ACT.Copy)\
                            .then_inc(S("e_yh"), 1)
                act.wait_ge(S("e_yl"), 6)
                for n in range(4):
                    q, k = divmod(n, 2)
                    act.wait_ge(S("e_f1"), n + 1)
                    if n:
                        act.wait_ge(S("e_f2"), n)
                    nc.scalar.activation(e_ab, ps[:, 0, :].rearrange("p (a b) -> p a b", a=NT), ACT.Copy)\
                        .then_inc(S("e_fab"), 1)
                    act.wait_ge(S("e_f2"), n + 1)
                    nc.scalar.activation(xh[:, k, q * T:(q + 1) * T], ps[:, 1, 0:T], ACT.Copy)\
                        .then_inc(S("e_fh"), 1)

            def odd():
                pairs_of(act, c, 3, lambda i, s: None, ahead=act_split)
                pairs_of(act, c, 3, lambda i, s: None, ahead=act_split)
                for e in range(14):
                    if e < 12:
                        act.wait_ge(S("o_max"), e + 1)
                        if e >= 2:
                            act.wait_ge(S("o_t"), e - 1)
                        for s in range(2):
                            ins = nc.scalar.activation(o_p[:, e % 2, s, :], ps[:, 4 + 2 * (e % 2) + s, :], ACT.Exp,
                                                       bias=o_st[:, e, s:s + 1], scale=HD ** -0.5,
                                                       accum_out=o_st[:, e, 2 + s:3 + s])
                        ins.then_inc(S("o_exp"), 1)
                    if 1 <= e <= 12:
                        a = e - 1
                        act.wait_ge(S("o_t"), a + 1)
                        if a >= 2:
                            act.wait_ge(S("o_pv"), a - 1)
                        nc.scalar.activation(o_aT[:, a % 2, :], ps[:, 2 + a % 2, :], ACT.Copy).then_inc(S("o_aT"), 1)
                    if e >= 2 and e % 2 == 1:
                        h = (e - 3) // 2
                        act.wait_ge(S("o_pv"), 2 * h + 2)
                        nc.scalar.activation(o_o[:, h, :], ps[:, h % 2, 0:T], ACT.Copy).then_inc(S("o_out"), 1)
                act.wait_ge(S("o_out"), 6)
                nc.scalar.activation(o_sq[:, :, :], o_o[:, :, :], ACT.Square).then_inc(S("o_sq"), 1)
                act.wait_ge(S("o_ss"), 1)
                nc.scalar.activation(o_sq[:, :, :], ps[:, 4:7, :].rearrange("p a (b n) -> p (a b) n", n=T),
                                     ACT.Sqrt, bias=K("eps"), scale=1.0 / P).then_inc(S("o_root"), 1)
                act.wait_ge(S("o_conv"), 1)
                nc.scalar.activation(xh[:, 0:2, 0:T], o_c[:, :, :], ACT.Copy).then_inc(S("o_yh"), 1)
                act.wait_ge(S("o_y"), 1)
                nc.scalar.activation(xh[:, 2:8, 0:T], o_o[:, :, :], ACT.Copy).then_inc(S("o_yh"), 1)

            def mamba(layer):
                pairs_of(act, c, 3, lambda i, s: None, ahead=act_split)
                act.wait_ge(S("m_sw_in"), 48 * (layer + 1))
                nc.scalar.activation(m_sw_h[:, :, :], m_sw[:, :, :], ACT.Copy).then_inc(S("m_sw_hi"), 1)
                act.wait_ge(S("m_dt_in"), layer + 1)
                link(nc.scalar.activation(m_dt[:, 1, :], m_dt[:, 0, :], ACT.Abs))
                nc.scalar.activation(m_dt[:, 1, :], m_dt[:, 1, :], ACT.Exp, scale=-1.0).then_inc(S("m_dt_exp"), 1)
                nc.scalar.activation(m_dt[:, 5, 0:8], bcast[:, 16 + 8 * layer:24 + 8 * layer], ACT.Exp)
                act.wait_ge(S("m_dt_one"), layer + 1)
                nc.scalar.activation(m_dt[:, 3, :], m_dt[:, 2, :], ACT.Ln).then_inc(S("m_dt_ln"), 1)
                act.wait_ge(S("evac_done"), c.units + CREDIT)
                nc.scalar.activation(m_in[:, 0:4, :], m_in[:, 0:4, :], ACT.Silu)
                act.wait_ge(S("m_taps"), layer + 1)
                nc.scalar.activation(m_cv[:, :, :], m_cv[:, :, :], ACT.Silu).then_inc(S("m_conv"), 1)
                act.wait_ge(S("m_x_t"), layer + 1)
                nc.scalar.activation(m_x[:, :, :], ps[:, 4:6, :], ACT.Copy).then_inc(S("m_x"), 1)
                for h in range(8):
                    act.wait_ge(S("m_seg"), 8 * layer + h + 1)
                    nc.scalar.activation(m_e[:, h % 2, :], m_e[:, h % 2, :], ACT.Exp).then_inc(S("m_exp"), 1)
                act.wait_ge(S("m_gated"), layer + 1)
                nc.scalar.activation(m_sq[:, :, :], m_y[:, :, :], ACT.Square).then_inc(S("m_sq"), 1)
                act.wait_ge(S("m_ss"), layer + 1)
                nc.scalar.activation(root[:, :].rearrange("p (a b) -> p a b", a=2), ps[:, 2:4, 0:T], ACT.Sqrt,
                                     bias=K("eps"), scale=1.0 / T).then_inc(S("m_root"), 1)
                act.wait_ge(S("m_normed"), layer + 1)
                act.wait_ge(S("mm_done"), 2 * c.units + HALF_CREDIT)
                nc.scalar.activation(h_yh[:, :, :], m_y[:, :, :], ACT.Copy).then_inc(S("m_yh"), 1)

            def attention(layer, which):
                a = 3 * layer + which
                for pairs in (2, 1) + (1,) * (which == 2):
                    pairs_of(act, c, pairs, lambda i, s: None, ahead=act_split)
                if which == 0:
                    act.wait_ge(S("a_f_in"), layer + 1)
                    link(nc.scalar.activation(a_f[:, 1, :], a_f[:, 0, :], ACT.Abs))
                    link(nc.scalar.activation(a_f[:, 1, :], a_f[:, 1, :], ACT.Exp, scale=-1.0))
                    nc.scalar.activation(a_f[:, 1, :], a_f[:, 1, :], ACT.Ln, bias=1.0).then_inc(S("a_f_ln"), 1)
                for e in range(18):
                    if e < 16:
                        nk = (e % 2 + 1) * P
                        act.wait_ge(S("a_max"), 16 * a + e + 1)
                        nc.scalar.activation(a_p[:, e % 2, 0:nk], a_p[:, e % 2, 0:nk], ACT.Exp, bias=a_st[:, e, 0:1],
                                             accum_out=a_st[:, e, 1:2]).then_inc(S("a_exp"), 1)
                    if 1 <= e <= 16:
                        b = e - 1
                        nk = (b % 2 + 1) * P
                        act.wait_ge(S("a_t"), 16 * a + b + 1)
                        if b >= 2:
                            act.wait_ge(S("a_pv"), 16 * a + b - 1)
                        nc.scalar.activation(a_pT[:, b % 2, 0:nk], ps[:, 6 + b % 2, 0:nk], ACT.Copy)\
                            .then_inc(S("a_pT"), 1)
                    if e >= 5 and e % 4 == 1:
                        p = (e - 5) // 4
                        act.wait_ge(S("a_pv"), 16 * a + 4 * p + 4)
                        nc.scalar.activation(h_yh[:, p, :], ps[:, p % 2, 0:T], ACT.Copy).then_inc(S("a_yh"), 1)

            def merge(layer, n):
                def unit(i, s):
                    if s == 0:
                        act.wait_ge(S("evac_done"), 2 * i + (c.units + 1 + CREDIT))
                        b0 = vec_at["b_gate_2"] + 32 * layer + DC * n
                        for b in range(2):
                            ins = nc.scalar.activation(h_gate[:, b, :], h_gate[:, b, :], ACT.Sigmoid,
                                                       bias=vec[:, bass.ds(i * 2 + (b0 + b), 1)])
                        ins.then_inc(S("h_gate"), 1)
                pairs_of(act, c, 4, unit, ahead=act_split, w=(UNIT // 2, UNIT // 4))

            def merged(layer):
                act.wait_ge(S("h_merged"), 12 * (layer + 1))
                act.wait_ge(S("mm_done"), 2 * c.units + HALF_CREDIT)
                nc.scalar.activation(xh[:, :, 0:T], h_merged[:, :, :], ACT.Copy).then_inc(S("h_merged_hi"), 1)

            for stage, *args in schedule:
                if stage == "norm":
                    norm(*args)
                elif stage == "renorm":
                    root_of_squares(args[0], 1)
                    c.add(norm=1, renorm=1)
                elif stage == "ffn":
                    ffn(args[2], args[4], args[5])
                elif stage == "even":
                    even()
                elif stage == "odd":
                    odd()
                elif stage == "out":
                    pairs_of(act, c, 2, lambda i, s: None, ahead=act_split)
                elif stage == "mamba":
                    mamba(args[0])
                elif stage == "attention":
                    attention(args[0], args[1])
                elif stage == "merge":
                    merge(*args)
                elif stage == "wout":
                    merged(args[0])
                    pairs_of(act, c, 2, lambda i, s: None, ahead=act_split)

        @block.vector
        def _(dve):
            c = Count()
            link = Link(dve, "dve_link")
            dve.sem_inc(S("lo_ready"), HALF_CREDIT)
            dve.sem_inc(S("evac_done"), CREDIT)
            dve.sem_inc(S("hid_l_ready"), CREDIT)
            dve.wait_ge(S("vec_t"), 1)
            nc.vector.tensor_copy(vec[:, 0:n_rows], ps[:, 7, 0:n_rows]).then_inc(S("vec_ready"), 1)
            dve.wait_ge(S("lam_landed"), 16 * 8)
            for j in range(2):
                ins = nc.vector.tensor_tensor(lam_prod[:, j:j + 1], lam_in[:, 2 * j:2 * j + 1],
                                              lam_in[:, 2 * j + 1:2 * j + 2], ALU.mult)
            ins.then_inc(S("lam_prod"), 1)
            for k in range(DC):
                dve.wait_ge(S("h_t"), k + 1)
                nc.vector.tensor_copy(hT[:, k, :], ps[:, k, :]).then_inc(S("h_in"), 1)
            dve.wait_ge(S("lam_exp"), 1)
            link(nc.vector.tensor_tensor(lam[:, 2:3], lam[:, 1:2], lam[:, 0:1], ALU.subtract))
            link(nc.vector.tensor_scalar(lam[:, 2:3], lam[:, 2:3], -LAM_INIT, None, ALU.add))
            dve.wait_ge(S("bcast_mm"), 1)
            nc.vector.tensor_copy(bcast[:, :], ps[:, 6, 64:128]).then_inc(S("bcast_ready"), 1)
            dve_split(dve, 0, 0, 0)

            def mod_unit(layer, m0):
                def read(i, s):
                    dve.wait_ge(S("mod_mm"), 2 * i + (MOD_UNITS * layer + m0 + s + 1))
                    at = i * 4 + (8 * N_MOD * layer + 2 * (m0 + s))
                    b0 = vec_at["ada_b"]
                    nc.vector.tensor_tensor(mod[:, bass.ds(at, 2), :], ps[:, 6 + s, 0:4].rearrange("p (a j) -> p a j", j=2),
                                            vec[:, bass.ds(at + b0, 2)].unsqueeze(2).to_broadcast([P, 2, 2]),
                                            ALU.add).then_inc(S("mod_evac"), 1)
                return read

            dve.wait_ge(S("mod_mm"), MOD_FIRST)
            nc.vector.tensor_tensor(mod[:, 0:2 * MOD_FIRST, :], ps[:, 5, 0:4 * MOD_FIRST].rearrange("p (a j) -> p a j", j=2),
                                    V("ada_b", 0, 2 * MOD_FIRST).unsqueeze(2).to_broadcast([P, 2 * MOD_FIRST, 2]),
                                    ALU.add).then_inc(S("mod_evac"), MOD_FIRST)

            def mod_blocks(layer, n, b):
                dve.wait_ge(S("mod_evac"), MOD_UNITS * layer + 4 * (3 * n + b) + 4)
                at = 8 * N_MOD * layer + 24 * n + 8 * b
                return mod[:, at:at + 8, :]

            def norm_gains(layer, n, name):
                scale = mod_blocks(layer, n, 1)
                for j in range(2):
                    link(nc.vector.scalar_tensor_tensor(out=gains[:, layer, n, :, j], in0=scale[:, :, j], scalar=1.0,
                                                        in1=V(name, DC * layer, DC), op0=ALU.add, op1=ALU.mult))

            def norm(src, nc_, gain, shift):
                o = c.of
                n = T * nc_
                dve.wait_ge(S("root_ready"), o["norm"] + 1)
                link(nc.vector.reciprocal(rstd[:, 0:n], root[:, 0:n]))
                for k in range(DC):
                    for j in range(nc_):
                        sl = slice(j * T, (j + 1) * T)
                        nc.vector.scalar_tensor_tensor(out=sq[:, k, sl], in0=src[:, k, sl], scalar=gain(k, j),
                                                       in1=rstd[:, sl], op0=ALU.mult, op1=ALU.mult)\
                            .then_inc(S("norm_prod"), 1)
                for k in range(DC):
                    for j in range(nc_):
                        e = o["norm_hi"] + k * nc_ + j
                        sl = slice(j * T, (j + 1) * T)
                        dve.wait_ge(S("norm_hi"), e + 1)
                        nc.vector.scalar_tensor_tensor(out=xl[:, k, sl], in0=sq[:, k, sl],
                                                       scalar=shift(k, j) if shift else 0.0,
                                                       in1=xh[:, k, sl].bitcast(F32), op0=ALU.add,
                                                       op1=ALU.subtract).then_inc(S("norm_lo"), 1)
                c.add(norm=1, norm_hi=DC * nc_)

            def ffn(n_tok, final, mods, gate):
                for n, half in enumerate(HALVES):
                    a0 = c.hidden
                    def up(i, s):
                        a = 2 * i + (a0 + hid0 + s)
                        dve.wait_ge(S("act_ready"), a + 1)
                        dve.wait_ge(S("hid_l_ready"), a + 1)
                        unit_done(dve, c, i, s)
                        nc.vector.tensor_tensor(hid32[:, s, 0:n_tok], act32[:, s, 0:n_tok],
                                                ps[:, 2 * s + 1, 0:n_tok], ALU.mult).then_inc(S("evac_done"), 1)
                        dve.wait_ge(S("hid_h_ready"), a + 1)
                        to = bass.ds(i * 2 + (hid0 + s), 1)
                        nc.vector.tensor_tensor(hid_l[:, to, 0:n_tok], hid32[:, s:s + 1, 0:n_tok],
                                                hid_h[:, to, 0:n_tok].bitcast(F32), ALU.subtract)\
                            .then_inc(S("hid_l_ready"), 1)
                    hid0 = 0
                    for p0, pairs, mod_part in parts(half // 2, mods[2 * n]):
                        hid0 = 2 * p0
                        beside = mod_part and mod_unit(*mod_part)
                        pairs_of(dve, c, pairs, lambda i, s: (up(i, s), beside and beside(i, s)), ahead=dve_split)
                    c.hidden += half
                    if gate and n == 0:
                        g = mod_blocks(gate[0], gate[1], 2)
                        link(nc.vector.tensor_scalar(g, g, 0.5, None, ALU.mult))
                    for p0, pairs, mod_part in parts(4, mods[2 * n + 1]):
                        beside = mod_part and mod_unit(*mod_part)
                        add = add_gated(gate, n_tok // T, 2 * p0) if gate else add_plain(n, 2 * p0)
                        def down(i, s):
                            unit_done(dve, c, i, s)
                            add(i, s)
                            if beside:
                                beside(i, s)
                        pairs_of(dve, c, pairs, down, ahead=dve_split, final=final and n == 1)

            def add_gated(gate, nc_, n0):
                gate0 = 8 * N_MOD * gate[0] + 24 * gate[1] + 16
                def add(i, s):
                    to = bass.ds(i * 2 + (n0 + s), 1)
                    for j in range(nc_):
                        sl = slice(j * T, (j + 1) * T)
                        ins = nc.vector.scalar_tensor_tensor(
                            out=hT[:, to, sl], in0=ps[:, 2 * s:2 * s + 1, sl],
                            scalar=mod[:, bass.ds(i * 2 + (gate0 + n0 + s), 1), j], in1=hT[:, to, sl],
                            op0=ALU.mult, op1=ALU.add)
                    ins.then_inc(S("evac_done"), 1)
                return add


            def even():
                link(nc.vector.memset(e_gw[:, :, :], 0.0))
                nc.vector.memset(e_gT[32:33, :], 1.0).then_inc(S("e_gw_zero"), 1)
                nc.vector.memset(e_S[:, :, 0, :, :], 0.0)
                def to_z(i, s):
                    fm_evac(e_z, 0, 2 * T)(dve, c, i, s)
                pairs_of(dve, c, 2, to_z, ahead=dve_split)
                def r_and_v(i, s):
                    unit_done(dve, c, i, s)
                    if s == 0:
                        nc.vector.tensor_copy(e_r[:, bass.ds(i * 2, 2), :], ps[:, 0:2, :]).then_inc(S("evac_done"), 1)
                    else:
                        nc.vector.tensor_copy(e_v[:, :, bass.ds(i * 256, 256)],
                                              ps[:, 2:4, :].rearrange("p a (b n) -> p (a b) n", n=256))\
                            .then_inc(S("evac_done"), 1)
                pairs_of(dve, c, 3, r_and_v, ahead=dve_split)
                dve.wait_ge(S("e_small_hi"), 1)
                nc.vector.tensor_tensor(e_small_l[:, :, :], e_small[:, :, :], e_small_h[:, :, :].bitcast(F32),
                                        ALU.subtract).then_inc(S("e_small_lo"), 1)
                dve.wait_ge(S("e_gates_mm"), 1)
                nc.vector.memset(e_att[:, :, :], 0.0)
                nc.vector.tensor_copy(e_gtok[:, :, :].rearrange("p a b -> p (a b)"), ps[:, 5, 0:P])\
                    .then_inc(S("e_gtok"), 1)
                dve.wait_ge(S("e_gates_t"), 1)
                nc.vector.tensor_copy(e_gT[0:32, :], ps[0:32, 6, :]).then_inc(S("e_gT"), 1)
                for q in range(2):
                    for n in range(4):
                        it, tile, dr = 4 * q + n, n // 2, n % 2
                        tt = slice((1 - q) * T + tile * P, (1 - q) * T + (tile + 1) * P)
                        t0 = slice(tile * P, (tile + 1) * P)
                        dve.wait_ge(S("e_ln"), it + 1)
                        if it >= 2:
                            dve.wait_ge(S("e_cum"), it - 1)
                        nc.vector.scalar_tensor_tensor(out=e_log[:, it % 2, :], in0=ps[:, dr, 0:384], scalar=0.0,
                                                       in1=e_abs[:, :], op0=ALU.min, op1=ALU.subtract)\
                            .then_inc(S("e_log"), 1)
                        dve.wait_ge(S("e_exp"), it + 1)
                        if q and n == 0:
                            dve.wait_ge(S("e_o"), 3 * q)
                        kd, qd = e_keys(dr, q)
                        edge = e_up[:, :, 63:128:64] if dr == 0 else e_up[:, :, 0:128:64]
                        link(nc.vector.tensor_copy(e_last[:, dr, tile, :, :], edge))
                        nc.vector.scalar_tensor_tensor(out=qd[:, :, t0], in0=e_z[:, 2:5, tt], scalar=0.125,
                                                       in1=e_up[:, :, :], op0=ALU.mult, op1=ALU.mult)
                        link(nc.vector.tensor_tensor(kd[:, :, t0], e_z[:, 5:8, tt], e_dn[:, :, :], ALU.mult))
                        if it:
                            dve.wait_ge(S("e_kk_t"), it)
                        nc.vector.tensor_tensor(
                            e_kk[:, :, :].rearrange("p a (b n) -> p (a b) n", n=64),
                            kd[:, :, t0].rearrange("p a (b n) -> p a b n", n=64).rearrange("p a b n -> p a b n"),
                            e_last[:, dr, tile, :, :].unsqueeze(3).to_broadcast([P, 3, 2, 64]), ALU.mult)\
                            .then_inc(S("e_decayed"), 1)
                    if q:
                        link(nc.vector.tensor_copy(e_S[:, :, 0, :, :], e_S[:, :, 4, :, :]))
                    for step in range(8):
                        dr, n = step % 2, step // 2
                        ch = n if dr == 0 else 3 - n
                        dve.wait_ge(S("e_kv"), 8 * q + step + 1)
                        if step >= 2:
                            dve.wait_ge(S("e_state"), 8 * q + step - 1)
                        for p in range(3):
                            ins = nc.vector.scalar_tensor_tensor(
                                out=e_S[:, dr, n + 1, p, :], in0=e_S[:, dr, n, p, :],
                                scalar=e_last[:, dr, ch // 2, p, ch % 2:ch % 2 + 1],
                                in1=ps[:, (6, 2)[dr], p * P:(p + 1) * P], op0=ALU.mult, op1=ALU.add)
                        ins.then_inc(S("e_state"), 1)
                    for p in range(3):
                        o = 3 * q + p
                        dve.wait_ge(S("e_att_mm"), o + 1)
                        if o:
                            dve.wait_ge(S("e_o"), o)
                        for dr in range(2):
                            mask = K(("cum_fwd", "cum_bwd")[dr]).bitcast(U32)
                            cols = slice(2 * dr * P, 2 * dr * P + 2 * P)
                            for h in range(2):
                                ins = nc.vector.copy_predicated(
                                    e_att[:, h, cols].rearrange("p (a b) -> p a b", b=P),
                                    mask.unsqueeze(1).to_broadcast([P, 2, P]),
                                    ps[:, 4 + h, cols].rearrange("p (a b) -> p a b", b=P))
                        ins.then_inc(S("e_att"), 1)
                        dve.wait_ge(S("e_oroot"), o + 1)
                        y2 = e_y[:, :].rearrange("p (a b) -> p a b", a=2)
                        link(nc.vector.reciprocal(rstd[:, :], root[:, :]))
                        if o:
                            dve.wait_ge(S("e_yl"), o)
                        link(nc.vector.scalar_tensor_tensor(out=y2, in0=ps[:, 6:8, 0:T], scalar=V("gla_norm"),
                                                            in1=rstd[:, :].rearrange("p (a b) -> p a b", a=2), op0=ALU.mult, op1=ALU.mult))
                        sl = slice((1 - q) * T, (2 - q) * T)
                        if o == 0:
                            dve.wait_ge(S("e_silu"), 1)
                        nc.vector.tensor_tensor(y2, y2, e_r[:, 2 * p:2 * p + 2, sl], ALU.mult).then_inc(S("e_y"), 1)
                        dve.wait_ge(S("e_yh"), o + 1)
                        nc.vector.tensor_tensor(xl[:, 2 + 2 * p:4 + 2 * p, sl], y2,
                                                xh[:, 2 + 2 * p:4 + 2 * p, sl].bitcast(F32), ALU.subtract)\
                            .then_inc(S("e_yl"), 1)
                for n in range(4):
                    q, k = divmod(n, 2)
                    dve.wait_ge(S("e_fh"), n + 1)
                    sl = slice(q * T, (q + 1) * T)
                    nc.vector.tensor_tensor(xl[:, k, sl], ps[:, 1, 0:T], xh[:, k, sl].bitcast(F32), ALU.subtract)\
                        .then_inc(S("e_fl"), 1)

            def odd():
                def first(i, s):
                    unit_done(dve, c, i, s)
                    nc.vector.tensor_copy((o_z, o_q)[s][:, bass.ds(i * 2, 2), :], ps[:, 2 * s:2 * s + 2, 0:T])\
                        .then_inc(S("evac_done"), 1)
                pairs_of(dve, c, 3, first, ahead=dve_split)
                def k_and_v(i, s):
                    unit_done(dve, c, i, s)
                    if s == 0:
                        nc.vector.tensor_copy(o_k[:, bass.ds(i * 2, 2), :], ps[:, 0:2, :]).then_inc(S("evac_done"), 1)
                    else:
                        nc.vector.tensor_copy(o_v[:, :, bass.ds(i * 256, 256)],
                                              ps[:, 2:4, :].rearrange("p a (b n) -> p (a b) n", n=256))\
                            .then_inc(S("evac_done"), 1)
                pairs_of(dve, c, 3, k_and_v, ahead=dve_split)
                dve.wait_ge(S("evac_done"), c.units + CREDIT)
                cos = K("axial_cos").unsqueeze(1).to_broadcast([P, 2, T])
                sin = K("axial_sin").unsqueeze(1).to_broadcast([P, 2, T])
                for n in range(6):
                    buf, k = (o_q, 2 * n) if n < 3 else (o_k, 2 * n - 6)
                    x = buf[:, k:k + 2, 0:T]
                    dve.wait_ge(S("o_swap"), n + 1)
                    if n:
                        dve.wait_ge(S("o_turned"), n)
                    nc.vector.tensor_tensor(o_turn[:, :, :], ps[:, n, :].rearrange("p (a b) -> p a b", a=2), sin, ALU.mult)
                    link(nc.vector.tensor_tensor(x, x, cos, ALU.mult))
                    nc.vector.tensor_tensor(x, x, o_turn[:, :, :], ALU.add).then_inc(S("o_turned"), 1)

                def probs(e):
                    st = o_st[:, e, :]
                    dve.wait_ge(S("o_exp"), e + 1)
                    link(nc.vector.reciprocal(st[:, 4:6], st[:, 2:4]))
                    nc.vector.tensor_scalar(o_p[:, e % 2, 0, :], o_p[:, e % 2, 0, :], st[:, 4:5], None, ALU.mult)
                    link(nc.vector.tensor_tensor(st[:, 5:6], st[:, 5:6], lam[:, 2:3], ALU.mult))
                    nc.vector.scalar_tensor_tensor(out=o_p[:, e % 2, 0, :], in0=o_p[:, e % 2, 1, :], scalar=st[:, 5:6],
                                                   in1=o_p[:, e % 2, 0, :], op0=ALU.mult, op1=ALU.add)\
                        .then_inc(S("o_a"), 1)

                for e in range(13):
                    if e < 12:
                        dve.wait_ge(S("o_scores"), e + 1)
                        b = 4 + 2 * (e % 2)
                        link(nc.vector.tensor_reduce(o_st[:, e, 0:2], ps[:, b:b + 2, :], AX.X, ALU.max, negate=True))
                        nc.vector.tensor_scalar(o_st[:, e, 0:2], o_st[:, e, 0:2], HD ** -0.5, None, ALU.mult)\
                            .then_inc(S("o_max"), 1)
                    if e:
                        probs(e - 1)
                link(nc.vector.memset(o_u[:, :, :], 0.0))
                link(nc.vector.tensor_tensor(o_u[:, :, 1:T + 1], o_z[:, 2:4, :], o_z[:, 4:6, :], ALU.mult))
                for b in range(2):
                    link(nc.vector.tensor_scalar(o_c[:, b, :], o_u[:, b, 0:T], V("conv_w", b), V("conv_b", b),
                                                 ALU.mult, ALU.add))
                    for tap in (1, 2):
                        link(nc.vector.scalar_tensor_tensor(out=o_c[:, b, :], in0=o_u[:, b, tap:tap + T],
                                                            scalar=V("conv_w", 2 * tap + b), in1=o_c[:, b, :],
                                                            op0=ALU.mult, op1=ALU.add))
                nc.vector.tensor_tensor(o_c[:, :, :], o_c[:, :, :], o_z[:, 0:2, :], ALU.mult).then_inc(S("o_conv"), 1)
                link(nc.vector.tensor_scalar(lam[:, 3:4], V("diff_norm"), 1.0 - LAM_INIT, None, ALU.mult))
                dve.wait_ge(S("o_root"), 1)
                link(nc.vector.reciprocal(o_sq[:, :, :], o_sq[:, :, :]))
                nc.vector.scalar_tensor_tensor(out=o_o[:, :, :], in0=o_o[:, :, :], scalar=lam[:, 3:4],
                                               in1=o_sq[:, :, :], op0=ALU.mult, op1=ALU.mult).then_inc(S("o_y"), 1)
                for n, (c0, buf) in enumerate(((0, o_c), (2, o_o))):
                    dve.wait_ge(S("o_yh"), n + 1)
                    k = buf.shape[1]
                    nc.vector.tensor_tensor(xl[:, c0:c0 + k, 0:T], buf[:, :, :],
                                            xh[:, c0:c0 + k, 0:T].bitcast(F32), ALU.subtract).then_inc(S("o_yl"), 1)

            def mamba(layer):
                def unit(i, s):
                    fm_evac(m_in, 0, T)(dve, c, i, s)
                pairs_of(dve, c, 3, unit, ahead=dve_split)
                dve.wait_ge(S("m_sw_hi"), layer + 1)
                nc.vector.tensor_tensor(m_sw_l[:, :, :], m_sw[:, :, :], m_sw_h[:, :, :].bitcast(F32), ALU.subtract)\
                    .then_inc(S("m_sw_lo"), 1)
                dve.wait_ge(S("m_small_mm"), layer + 1)
                nc.vector.tensor_copy(h_small[:, :, :].rearrange("p a b -> p (a b)"), ps[:, 5, 0:NT * 84])\
                    .then_inc(S("m_small"), 1)
                dve.wait_ge(S("m_small"), layer + 1)
                for t in range(NT):
                    ins = nc.vector.tensor_tensor(m_dt[:, 0, 8 * t:8 * t + 8], h_small[:, t, 0:8],
                                                  bcast[:, 8 * layer:8 * layer + 8], ALU.add)
                ins.then_inc(S("m_dt_in"), 1)
                dve.wait_ge(S("m_dt_exp"), layer + 1)
                nc.vector.tensor_scalar(m_dt[:, 2, :], m_dt[:, 1, :], 1.0, None, ALU.add).then_inc(S("m_dt_one"), 1)
                dve.wait_ge(S("m_dt_one"), layer + 1)
                link(nc.vector.tensor_scalar(m_dt[:, 4, :], m_dt[:, 2, :], -1.0, None, ALU.add))
                link(nc.vector.tensor_tensor(m_dt[:, 1, :], m_dt[:, 1, :], m_dt[:, 4, :], ALU.subtract))
                link(nc.vector.reciprocal(m_dt[:, 4, :], m_dt[:, 2, :]))
                link(nc.vector.tensor_tensor(m_dt[:, 1, :], m_dt[:, 1, :], m_dt[:, 4, :], ALU.mult))
                dve.wait_ge(S("m_dt_ln"), layer + 1)
                link(nc.vector.tensor_tensor(m_dt[:, 1, :], m_dt[:, 1, :], m_dt[:, 3, :], ALU.add))
                link(nc.vector.scalar_tensor_tensor(out=m_dt[:, 0, :], in0=m_dt[:, 0, :], scalar=0.0,
                                                    in1=m_dt[:, 1, :], op0=ALU.max, op1=ALU.add))
                for t in range(NT):
                    ins = nc.vector.scalar_tensor_tensor(out=m_dt[:, 4, 8 * t:8 * t + 8], in0=m_dt[:, 0, 8 * t:8 * t + 8],
                                                         scalar=-1.0, in1=m_dt[:, 5, 0:8], op0=ALU.mult, op1=ALU.mult)
                ins.then_inc(S("m_dta"), 1)
                for k in range(8):
                    w = lambda tap: V("conv_w_2", 32 * layer + 8 * tap + k)
                    link(nc.vector.tensor_scalar(m_cv[:, k, :], m_in[:, 4 + k, :], w(3),
                                                 V("conv_b_2", 8 * layer + k), ALU.mult, ALU.add))
                    for back in (1, 2, 3):
                        ins = nc.vector.scalar_tensor_tensor(out=m_cv[:, k, back:T], in0=m_in[:, 4 + k, 0:T - back],
                                                             scalar=w(3 - back), in1=m_cv[:, k, back:T],
                                                             op0=ALU.mult, op1=ALU.add)
                        if k == 7 and back == 3:
                            ins.then_inc(S("m_taps"), 1)
                        else:
                            link(ins)
                dve.wait_ge(S("m_cs_mm"), layer + 1)
                nc.vector.tensor_copy(m_cs[:, :], ps[0:8, 2, 0:T])
                nc.vector.tensor_scalar(m_ncs[:, :], ps[:, 3, 0:16], -1.0, None, ALU.mult).then_inc(S("m_cs"), 1)
                dve.wait_ge(S("m_cs"), layer + 1)
                d0 = 48 + 8 * layer
                for j in range(2):
                    hh = slice(64 * j, 64 * j + 64)
                    ins = nc.vector.tensor_copy(m_d[hh, :], bcast[hh, d0 + j:d0 + 8:2])
                link(ins)
                dve.wait_ge(S("m_cb"), layer + 1)

                def seg(h):
                    dve.wait_ge(S("m_row"), 8 * layer + h + 1)
                    if h >= 2:
                        dve.wait_ge(S("m_o"), 8 * layer + h - 1)
                    row = ps[:, 4 + h % 2, 0:T]
                    e = m_e[:, h % 2, :]
                    for t in range(NT):
                        ins = nc.vector.scalar_tensor_tensor(out=e[:, t * T:t * T + P], in0=row[:, t * P:(t + 1) * P],
                                                             scalar=m_ncs[:, 8 * t + h:8 * t + h + 1],
                                                             in1=K("causal_t"), op0=ALU.add, op1=ALU.add)
                    nc.vector.tensor_scalar(e[:, P:T], row[:, P:T], m_ncs[:, h:h + 1], None, ALU.add)\
                        .then_inc(S("m_seg"), 1)

                seg(0)
                for h in range(8):
                    if h + 1 < 8:
                        seg(h + 1)
                    dve.wait_ge(S("m_exp"), 8 * layer + h + 1)
                    g = h // 4
                    e = m_e[:, h % 2, :]
                    nc.vector.scalar_tensor_tensor(out=e[:, 0:T], in0=e[:, 0:T], scalar=m_dt[:, 0, h:h + 1],
                                                   in1=ps[:, g, 0:T], op0=ALU.mult, op1=ALU.mult)
                    nc.vector.scalar_tensor_tensor(out=e[:, T:T + P], in0=e[:, T:T + P], scalar=m_dt[:, 0, 8 + h:9 + h],
                                                   in1=ps[:, g, T + P:2 * T], op0=ALU.mult, op1=ALU.mult)\
                        .then_inc(S("m_score"), 1)
                    if h % 2:
                        p = h // 2
                        dve.wait_ge(S("m_o"), 8 * layer + h + 1)
                        nc.vector.scalar_tensor_tensor(out=m_y[:, p, :], in0=m_cv[:, p, :], scalar=m_d[:, p:p + 1],
                                                       in1=ps[:, 6 + p % 2, 0:T], op0=ALU.mult, op1=ALU.add)\
                            .then_inc(S("m_y"), 1)
                dve.wait_ge(S("m_y"), 4 * layer + 4)
                nc.vector.tensor_tensor(m_y[:, :, :], m_y[:, :, :], m_in[:, 0:4, :], ALU.mult).then_inc(S("m_gated"), 1)
                dve.wait_ge(S("m_root"), layer + 1)
                link(nc.vector.reciprocal(rstd[:, :], root[:, :]))
                for k in range(4):
                    ins = nc.vector.scalar_tensor_tensor(out=m_y[:, k, :], in0=m_y[:, k, :],
                                                         scalar=V("ssm_norm_2", 4 * layer + k),
                                                         in1=rstd[:, (k // 2) * T:(k // 2 + 1) * T],
                                                         op0=ALU.mult, op1=ALU.mult)
                ins.then_inc(S("m_normed"), 1)
                dve.wait_ge(S("m_yh"), layer + 1)
                nc.vector.tensor_tensor(h_yl[:, :, :], m_y[:, :, :], h_yh[:, :, :].bitcast(F32), ALU.subtract)\
                    .then_inc(S("m_yl"), 1)

            def turn(n, buf, bank, n_chunks, count):
                dve.wait_ge(S("a_swap"), count)
                if count > 1:
                    dve.wait_ge(S("a_turned"), count - 1)
                if n_chunks == 2:
                    spreadto = lambda t: K(t).unsqueeze(1).to_broadcast([P, 2, T])
                    x, t, s = buf, a_turn[:, :, :], ps[:, bank, :].rearrange("p (a b) -> p a b", a=2)
                else:
                    spreadto = K
                    x, t, s = buf, a_turn[:, 0, :], ps[:, bank, 0:T]
                nc.vector.tensor_tensor(t, s, spreadto("rope_sin"), ALU.mult)
                link(nc.vector.tensor_tensor(x, x, spreadto("rope_cos"), ALU.mult))
                nc.vector.tensor_tensor(x, x, t, ALU.add).then_inc(S("a_turned"), 1)

            def choose(layer):
                link(nc.vector.tensor_scalar(a_w[:, :, :], h_small[:, :, 80:84], 0.5, None, ALU.mult))
                for qt in range(NT):
                    nk = (qt + 1) * P
                    dve.wait_ge(S("a_idx"), NT * layer + qt + 1)
                    for h in range(4):
                        link(nc.vector.tensor_scalar(a_relu[:, 0:nk], ps[:, 4 + h, 0:nk], HD ** -0.5, 0.0,
                                                     ALU.mult, ALU.max))
                        w = a_w[:, qt, h:h + 1]
                        if h == 0:
                            link(nc.vector.tensor_scalar(a_isc[:, 0:nk], a_relu[:, 0:nk], w, None, ALU.mult))
                        else:
                            link(nc.vector.scalar_tensor_tensor(out=a_isc[:, 0:nk], in0=a_relu[:, 0:nk], scalar=w,
                                                                in1=a_isc[:, 0:nk], op0=ALU.mult, op1=ALU.add))
                    diag = slice(nk - P, nk)
                    nc.vector.tensor_tensor(a_isc[:, diag], a_isc[:, diag], K("causal"), ALU.add).then_inc(S("a_isc"), 1)
                    dve.wait_ge(S("a_isc"), NT * layer + qt + 1)
                    for _ in range(DSA_KEEP // 8):
                        link(nc.vector.max(a_top[:, :], a_isc[:, 0:nk]))
                        link(nc.vector.match_replace(a_isc[:, 0:nk], a_top[:, :], a_isc[:, 0:nk], TAKEN))
                    b0 = (0, P)[qt]
                    link(nc.vector.tensor_scalar(a_bias[:, 0, b0:b0 + nk], a_isc[:, 0:nk], TAKEN, NEG,
                                                 ALU.not_equal, ALU.mult))
                    bd = a_bias[:, 0, b0 + nk - P:b0 + nk]
                    link(nc.vector.tensor_tensor(bd, bd, K("causal"), ALU.add))

            def attention(layer, which):
                a = 3 * layer + which
                def qk(i, s):
                    fm_evac(a_qk, 0, T)(dve, c, i, s)
                pairs_of(dve, c, 2, qk, ahead=dve_split)
                def vv(i, s):
                    unit_done(dve, c, i, s)
                    nc.vector.tensor_copy(a_v[:, :, s * 256:(s + 1) * 256],
                                          ps[:, 2 * s, :].rearrange("p (a b) -> p a b", a=NT)).then_inc(S("evac_done"), 1)
                pairs_of(dve, c, 1, vv, ahead=dve_split)
                if which == 0:
                    f0 = 32 + 8 * layer
                    for t in range(NT):
                        ins = nc.vector.tensor_tensor(a_f[:, 0, 8 * t:8 * t + 8], h_small[:, t, 8:16],
                                                      bcast[:, f0:f0 + 8], ALU.add)
                    ins.then_inc(S("a_f_in"), 1)
                    dve.wait_ge(S("a_f_ln"), layer + 1)
                    nc.vector.scalar_tensor_tensor(out=a_f[:, 2, :], in0=a_f[:, 0, :], scalar=0.0, in1=a_f[:, 1, :],
                                                   op0=ALU.min, op1=ALU.subtract).then_inc(S("a_logf"), 1)
                    dve.wait_ge(S("a_cf_mm"), layer + 1)
                    nc.vector.tensor_scalar(a_cf[:, :], ps[0:8, 2, 0:T], -1.0, None, ALU.mult)
                    nc.vector.tensor_copy(a_f[:, 3, :], ps[:, 3, 0:16]).then_inc(S("a_cf"), 1)
                    dve.wait_ge(S("a_cf"), layer + 1)
                else:
                    if which == 2:
                        def iq(i, s):
                            unit_done(dve, c, i, s)
                            nc.vector.tensor_copy(a_iq[:, s, :], ps[:, 2 * s, 0:T]).then_inc(S("evac_done"), 1)
                        pairs_of(dve, c, 1, iq, ahead=dve_split)
                        for j in range(2):
                            ins = nc.vector.tensor_copy(a_ik2[:, :, 64 * j:64 * j + 64], h_small[:, :, 16:80])
                        ins.then_inc(S("a_ik2"), 1)
                    dve.wait_ge(S("evac_done"), c.units + CREDIT)
                    r0 = 10 * layer + (0, 0, 4)[which]
                    for n in range(4):
                        turn(n, a_qk[:, 2 * n:2 * n + 2, :], n, 2, r0 + n + 1)
                    if which == 2:
                        dve.wait_ge(S("a_ik_t"), layer + 1)
                        nc.vector.tensor_copy(a_ik[:, :], ps[:, 6, 0:T]).then_inc(S("a_ik"), 1)
                        dve.wait_ge(S("a_ik"), layer + 1)
                        turn(4, a_iq[:, :, :], 4, 2, r0 + 5)
                        turn(5, a_ik[:, :], 5, 1, r0 + 6)
                        choose(layer)
                    else:
                        nc.vector.memset(a_bias[:, 0, P:2 * P], 0.0)
                        nc.vector.tensor_copy(a_bias[:, 0, 0:P], K("causal"))
                        link(nc.vector.tensor_copy(a_bias[:, 0, 2 * P:3 * P], K("causal")))

                def forget_bias(h):
                    dve.wait_ge(S("a_row"), 8 * layer + h + 1)
                    row = ps[:, 2 + h % 2, 0:T]
                    b = a_bias[:, h % 2, :]
                    cq = lambda t: a_f[:, 3, 8 * t + h:8 * t + h + 1]
                    nc.vector.scalar_tensor_tensor(out=b[:, 0:P], in0=row[:, 0:P], scalar=cq(0), in1=K("causal"),
                                                   op0=ALU.add, op1=ALU.add)
                    nc.vector.tensor_scalar(b[:, P:2 * P], row[:, 0:P], cq(1), None, ALU.add)
                    nc.vector.scalar_tensor_tensor(out=b[:, 2 * P:3 * P], in0=row[:, P:T], scalar=cq(1),
                                                   in1=K("causal"), op0=ALU.add, op1=ALU.add).then_inc(S("a_bias"), 1)
                    dve.wait_ge(S("a_bias"), 8 * layer + h + 1)

                for e in range(20):
                    if e < 16:
                        h, qt = divmod(e, 2)
                        nk = (qt + 1) * P
                        if which == 0 and qt == 0:
                            forget_bias(h)
                        b0 = (0, P)[qt]
                        bias = a_bias[:, h % 2 if which == 0 else 0, b0:b0 + nk]
                        dve.wait_ge(S("a_scores"), 16 * a + e + 1)
                        if e >= 2:
                            dve.wait_ge(S("a_t"), 16 * a + e - 1)
                        link(nc.vector.scalar_tensor_tensor(out=a_p[:, e % 2, 0:nk], in0=ps[:, 4 + e % 2, 0:nk],
                                                            scalar=HD ** -0.5, in1=bias, op0=ALU.mult, op1=ALU.add))
                        nc.vector.tensor_reduce(a_st[:, e, 0:1], a_p[:, e % 2, 0:nk], AX.X, ALU.max, negate=True)\
                            .then_inc(S("a_max"), 1)
                    if 1 <= e <= 16:
                        b = e - 1
                        nk = (b % 2 + 1) * P
                        dve.wait_ge(S("a_exp"), 16 * a + b + 1)
                        link(nc.vector.reciprocal(a_st[:, b, 2:3], a_st[:, b, 1:2]))
                        nc.vector.tensor_scalar(a_p[:, b % 2, 0:nk], a_p[:, b % 2, 0:nk], a_st[:, b, 2:3], None, ALU.mult)\
                            .then_inc(S("a_p"), 1)
                    if e >= 7 and e % 4 == 3:
                        p = (e - 7) // 4
                        dve.wait_ge(S("a_yh"), 4 * a + p + 1)
                        nc.vector.tensor_tensor(h_yl[:, p, :], ps[:, p % 2, 0:T], h_yh[:, p, :].bitcast(F32),
                                                ALU.subtract).then_inc(S("a_yl"), 1)

            def merge(layer, n):
                def unit(i, s):
                    u = 2 * i + (c.units + s)
                    if s == 0:
                        dve.wait_ge(S("evac_done"), u + CREDIT)
                        unit_done(dve, c, i, s)
                        nc.vector.tensor_copy(h_gate[:, :, :], ps[:, 0:2, 0:T]).then_inc(S("evac_done"), 1)
                    else:
                        unit_done(dve, c, i, s)
                        dve.wait_ge(S("h_gate"), i + (4 * (4 * layer + n) + 1))
                        dst = h_merged[:, bass.ds(i * 2, 2), :]
                        to = dst if n == 0 else h_prod[:, :, :]
                        nc.vector.tensor_tensor(to, ps[:, 2:4, 0:T], h_gate[:, :, :], ALU.mult).then_inc(S("evac_done"), 1)
                        if n:
                            dve.wait_ge(S("evac_done"), u + 1 + CREDIT)
                            nc.vector.tensor_tensor(dst, dst, h_prod[:, :, :], ALU.add).then_inc(S("h_merged"), 1)
                pairs_of(dve, c, 4, unit, ahead=dve_split, w=(UNIT // 2, UNIT // 4))

            def merged(layer):
                dve.wait_ge(S("h_merged_hi"), layer + 1)
                nc.vector.tensor_tensor(xl[:, :, 0:T], h_merged[:, :, :], xh[:, :, 0:T].bitcast(F32), ALU.subtract)\
                    .then_inc(S("h_merged_lo"), 1)

            def add_plain(n, n0):
                def add(i, s):
                    dst = h_out[:, bass.ds(i * 2 + (n0 + s), 1), :]
                    src = ps[:, 2 * s:2 * s + 1, 0:T]
                    if n == 0:
                        ins = nc.vector.tensor_copy(dst, src)
                    else:
                        ins = nc.vector.tensor_tensor(dst, src, dst, ALU.add)
                    ins.then_inc(S("evac_done"), 1)
                return add

            for stage, *args in schedule:
                if stage == "gains":
                    norm_gains(*args)
                elif stage == "norm":
                    norm(args[0], args[1], args[3], args[2])
                elif stage == "renorm":
                    dve.wait_ge(S("root_ready"), c.of["norm"] + 1)
                    link(nc.vector.reciprocal(rstd[:, 0:T], root[:, 0:T]))
                    src, gain = args
                    dst = hT if src is hT else sq
                    for k in range(DC):
                        ins = nc.vector.scalar_tensor_tensor(out=dst[:, k, 0:T], in0=src[:, k, 0:T], scalar=gain(k),
                                                             in1=rstd[:, 0:T], op0=ALU.mult, op1=ALU.mult)
                    if src is not hT:
                        link(ins)
                        ins = nc.vector.tensor_tensor(hT[:, :, 0:T], hT[:, :, 0:T], sq[:, :, 0:T], ALU.add)
                    ins.then_inc(S("renormed"), 1)
                    c.add(norm=1, renorm=1)
                elif stage == "ffn":
                    ffn(args[2], args[4], args[5], args[3])
                elif stage == "even":
                    even()
                elif stage == "odd":
                    odd()
                elif stage == "out":
                    mod_blocks(args[2], 1, 2)
                    gate0 = 8 * N_MOD * args[2] + 24 + 16
                    def out_unit(i, s):
                        unit_done(dve, c, i, s)
                        for b in range(2):
                            n = i * 4 + (2 * s + b)
                            for j in range(args[1] // T):
                                sl = slice(j * T, (j + 1) * T)
                                ins = nc.vector.scalar_tensor_tensor(
                                    out=hT[:, bass.ds(n, 1), sl], in0=ps[:, 2 * s + b:2 * s + b + 1, sl],
                                    scalar=mod[:, bass.ds(n + gate0, 1), j], in1=hT[:, bass.ds(n, 1), sl],
                                    op0=ALU.mult, op1=ALU.add)
                        ins.then_inc(S("evac_done"), 1)
                    pairs_of(dve, c, 2, out_unit, ahead=dve_split)
                elif stage == "mamba":
                    mamba(args[0])
                elif stage == "attention":
                    attention(args[0], args[1])
                elif stage == "merge":
                    merge(*args)
                elif stage == "wout":
                    merged(args[0])
                    pairs_of(dve, c, 2, lambda i, s: fm_evac(h_out, 0, T)(dve, c, i, s), ahead=dve_split)
                elif stage == "store":
                    for t in range(NT):
                        dve.wait_ge(S("y_t"), t + 1)
                        nc.vector.tensor_copy(y_tok[:, t, :].rearrange("p (a b) -> p a b", a=2),
                                              ps[:, 2 * t:2 * t + 2, :]).then_inc(S("y_copied"), 1)


def kernel(**inputs):
    import concourse.bacc as bacc
    from concourse.bass_utils import run_bass_kernel_spmd

    nc = bacc.Bacc("TRN2", target_bir_lowering=False, num_devices=1)
    table, const_at = constants()
    arrays, io = {"consts": table}, {}
    for name in NAMES:
        arrays[name] = np.ascontiguousarray(inputs[name])
    for name, a in arrays.items():
        io[name] = nc.dram_tensor(name, a.shape, F32, kind="ExternalInput").ap()
    io["out"] = nc.dram_tensor("out", (1, T, D), F32, kind="ExternalOutput").ap()
    chunked = lambda a, pat: io[a].rearrange(pat, p=P)
    io["vectors"] = [
        ("ada_b", chunked("ada_b", "l (b p) -> (l b) p")),
        ("norm_ffn1", chunked("norm_ffn1", "l (b p) -> (l b) p")),
        ("norm_mix", chunked("norm_mix", "l (b p) -> (l b) p")),
        ("norm_ffn2", chunked("norm_ffn2", "l (b p) -> (l b) p")),
        ("final_norm", chunked("final_norm", "(b p) -> b p")),
        ("c", chunked("c", "l (b p) -> (l b) p")),
        ("c_ctx", chunked("c_ctx", "(b p) -> b p")),
        ("gla_norm", io["gla_norm"]),
        ("diff_norm", io["diff_norm"]),
        ("conv_w", chunked("conv_w", "l k (b p) -> (l k b) p")),
        ("conv_b", chunked("conv_b", "l (b p) -> (l b) p")),
        ("norm_mix_pre_2", chunked("norm_mix_pre_2", "l (b p) -> (l b) p")),
        ("conv_w_2", chunked("conv_w_2", "l k (b p) -> (l k b) p")),
        ("conv_b_2", chunked("conv_b_2", "l (b p) -> (l b) p")),
        ("ssm_norm_2", chunked("ssm_norm_2", "l (b p) -> (l b) p")),
        ("norm_mix_post_2", chunked("norm_mix_post_2", "l (b p) -> (l b) p")),
        ("norm_ffn_pre_2", chunked("norm_ffn_pre_2", "l (b p) -> (l b) p")),
        ("norm_ffn_post_2", chunked("norm_ffn_post_2", "l (b p) -> (l b) p")),
        ("b_gate_2", chunked("b_gate_2", "l (b p) -> (l b) p")),
    ]
    build(nc, io, const_at)
    r = run_bass_kernel_spmd(nc, [arrays], core_ids=[0])
    return r.results[0]["out"]
```

```python
import math
from collections import Counter
from contextlib import ExitStack

import concourse.bass as bass
import numpy as np
from concourse import mybir

F32 = mybir.dt.float32
F32R = mybir.dt.float32r
U32 = mybir.dt.uint32
ALU = mybir.AluOpType
ACT = mybir.ActivationFunctionType
AX = mybir.AxisListType

P = 128
D = 1024
DC = D // P
T = 256
NT = T // P
FFN = 2816
HALVES = (12, 10)
UNIT = 2048
EPS = 1e-6
HD = 64
NEG = -1e30
TAKEN = -3e38
N_MOD = 9
MOD_UNITS = 4 * N_MOD
MOD_FIRST = 8
LAM_INIT = 0.8 - 0.6 * math.exp(-0.3)
DSA_KEEP = 64
Z0, DT0, FQ0, FV0, FF0, MQ0, MV0, DQ0, DV0, IQ0, IK0 = (
    0, 1536, 1544, 2568, 3080, 3088, 4112, 4624, 5648, 6160, 6416)


def constants():
    parts = {}
    eye = np.eye(P)
    parts["ident"] = eye
    parts["ones"] = np.ones((P, P))
    parts["eps"] = np.full((P, 1), EPS)
    t = np.arange(T)
    d = np.arange(HD)
    ang = 2 * np.pi * np.outer(d, d) / HD
    parts["dft_cos"] = np.kron(np.eye(2), np.cos(ang))
    parts["dft_sin"] = np.kron(np.eye(2), np.sin(ang))
    ang = 2 * np.pi * (np.outer(t, t) % T) / T
    scale = 1 / math.sqrt(T * HD)
    tiles = lambda a: a.reshape(NT, P, -1).transpose(1, 0, 2).reshape(P, -1)
    parts["dft_tok_cos"] = tiles(np.cos(ang) * scale)
    parts["dft_tok_nsin"] = tiles(-np.sin(ang) * scale)
    f32 = np.float32
    inv = (f32(10000.0) ** (-np.arange(0, HD, 2, dtype=f32) / f32(HD))).astype(f32)
    ang = (t[:, None].astype(f32) * inv[None]).astype(f32)
    row = np.concatenate([ang, ang], 1).T
    parts["rope_cos"] = np.cos(np.concatenate([row, row]))
    parts["rope_sin"] = np.sin(np.concatenate([row, row]))
    swap = np.zeros((P, P))
    for h in range(2):
        for i in range(32):
            swap[64 * h + 32 + i, 64 * h + i] = -1
            swap[64 * h + i, 64 * h + 32 + i] = 1
    parts["rope_swap"] = swap
    inv = (f32(10000.0) ** (-np.arange(16, dtype=f32) / f32(16))).astype(f32)
    rowang = ((t // 64)[:, None].astype(f32) * inv).astype(f32)
    colang = ((t % 64)[:, None].astype(f32) * inv).astype(f32)
    one = np.concatenate([rowang, rowang, colang, colang], 1).T
    parts["axial_cos"] = np.cos(np.concatenate([one, one]))
    parts["axial_sin"] = np.sin(np.concatenate([one, one]))
    swap = np.zeros((P, P))
    for h in range(4):
        for i in range(16):
            swap[32 * h + 16 + i, 32 * h + i] = -1
            swap[32 * h + i, 32 * h + 16 + i] = 1
    parts["axial_swap"] = swap
    i = np.arange(P)
    same = (i[:, None] // 64) == (i[None] // 64)
    parts["cum_fwd"] = (same & (i[:, None] <= i[None])).astype(float)
    parts["cum_bwd"] = (same & (i[:, None] >= i[None])).astype(float)
    parts["cum_all"] = tiles((t[:, None] <= t[None]).astype(float))
    parts["causal"] = np.where(i[None] <= i[:, None], 0.0, NEG)
    parts["causal_t"] = np.where(i[:, None] <= i[None], 0.0, NEG)
    spread = np.zeros((P, 8, P))
    for h in range(8):
        spread[h, h] = 1
    parts["spread"] = spread.reshape(P, -1)
    at, n = {}, 0
    for name, a in parts.items():
        at[name] = (n, n + a.shape[1])
        n += a.shape[1]
    return np.concatenate([np.asarray(a, np.float32) for a in parts.values()], 1), at

NAMES = (
    "x", "c", "ctx", "c_ctx", "ada_w", "ada_b", "norm_ffn1", "norm_mix", "norm_ffn2", "ffn1_w_in",
    "ffn1_w_out", "ffn2_w_in", "ffn2_w_out", "mix_w_out", "even_w_in", "gla_gate_w", "gla_gate_b",
    "gla_norm", "odd_w_in", "conv_w", "conv_b", "lambda_q1", "lambda_k1", "lambda_q2", "lambda_k2",
    "diff_norm", "final_norm", "norm_mix_pre_2", "w_in_2", "conv_w_2", "conv_b_2", "dt_bias_2",
    "a_log_2", "d_skip_2", "ssm_norm_2", "fox_fbias_2", "w_gate_2", "b_gate_2", "w_branch_2",
    "w_out_2", "norm_mix_post_2", "norm_ffn_pre_2", "w_ffn_in_2", "w_ffn_out_2", "norm_ffn_post_2",
)


def build(nc, io, const_at):
    ctx = ExitStack()
    with ctx:
        SLAB = 212704
        base = (nc.sbuf_base + 31) // 32 * 32
        ctx.enter_context(nc.sbuf_tensor("slab", [P, SLAB // 4], F32))

        class Region:

            def __init__(self, start, end=SLAB):
                self.at, self.end = start, end

            def __call__(self, name, shape, dt=F32):
                t = nc.alloc_sbuf_tensor_at(name, shape, dt, offset=base + self.at)
                self.at += (4 * int(np.prod(shape[1:])) + 31) // 32 * 32
                assert self.at <= self.end, (name, self.at, self.end)
                return t

        fixed = Region(0)
        n_const = max(b for _, b in const_at.values())
        consts = fixed("consts", [P, n_const])
        K = lambda name: consts[:, const_at[name][0]:const_at[name][1]]
        vec = fixed("vec", [P, 512])
        mod = fixed("mod", [P, 2 * 8 * N_MOD, 2])
        gains = fixed("gains", [P, 2, 3, DC, 2])
        cond32 = fixed("cond32", [P, 2, DC])
        cond_h = fixed("cond_h", [P, DC, 2], F32R)
        cond_l = fixed("cond_l", [P, DC, 2], F32R)
        bcast = fixed("bcast", [P, 64])
        lam = fixed("lam", [P, 4])
        sq2_at = fixed.at
        rstd = fixed("rstd", [P, 2 * T])
        root = fixed("root", [P, 2 * T])
        sq2 = Region(sq2_at)("sq2", [P, 2, 2 * T])
        ss = fixed("ss", [P, 2 * T])
        root_col = fixed("root_col", [P, 2 * NT])
        rstd_col = fixed("rstd_col", [P, 2 * NT])
        raw = fixed("raw", [P, 2, 2, UNIT // 2])
        whi = fixed("whi", [P, 2, 2, UNIT // 2], F32R)
        wlo = fixed("wlo", [P, 2, 2, UNIT // 2], F32R)
        hT = fixed("hT", [P, DC, 2 * T])
        xh_at = fixed.at
        xh = fixed("xh", [P, DC, 2 * T], F32R)
        xl_at = fixed.at
        xl = fixed("xl", [P, DC, 2 * T], F32R)
        overlay = fixed.at

        first = Region(overlay)
        hid_h = first("hid_h", [P, max(HALVES), 2 * T], F32R)
        hid_l = first("hid_l", [P, max(HALVES), 2 * T], F32R)
        act32 = first("act32", [P, 2, 2 * T])
        hid32 = first("hid32", [P, 2, 2 * T])
        out_at = first.at
        mod_w = first("mod_w", [P, 2, DC, 2 * P])
        mod_acc = first("mod_acc", [P, 2, 2 * 2 * P])
        mod_prod = first("mod_prod", [P, 2, 2 * P])
        normed = Region(overlay)("normed", [P, DC, 2 * T])
        start = Region(overlay)
        tok = start("tok", [P, 2 * NT, D])
        rows = start("rows", [P, 4, P])
        lam_in = start("lam_in", [HD, 4])
        lam_prod = start("lam_prod", [HD, 2])
        small_rows = start("small_rows", [1, 64])
        mod_rows = start("mod_rows", [2, MOD_FIRST * 2 * P])
        last = Region(overlay)
        y_tok = last("y_tok", [P, NT, D])


        ev = Region(overlay)
        e_z = ev("e_z", [P, 8, 2 * T])
        e_r = ev("e_r", [P, 6, 2 * T])
        e_v = ev("e_v", [P, 2 * NT, 768])
        e_small_at = ev.at
        e_small = ev("e_small", [P, DC, 32])
        e_small_h = ev("e_small_h", [P, DC, 32], F32R)
        e_small_l = ev("e_small_l", [P, DC, 32], F32R)
        e_gT = ev("e_gT", [33, 2 * T])
        e_gw = ev("e_gw", [33, 2, 384])
        in_place = Region(e_small_at, ev.at)
        e_up = in_place("e_up", [P, 3, P])
        e_dn = in_place("e_dn", [P, 3, P])
        e_log = ev("e_log", [P, 4, 384])
        e_kk = ev("e_kk", [P, 3, P])
        e_last = ev("e_last", [P, 2, NT, 3, 2])
        e_kd = ev("e_kd", [P, 3, T])
        e_qd = ev("e_qd", [P, 3, T])
        e_kkT = ev("e_kkT", [P, 2, NT, 384])
        e_S = ev("e_S", [P, 2, 5, 3, P])
        e_ab = e_kkT[:, 0, :, 0:2 * P]
        at_xh = Region(xh_at, xh_at + 8 * T * 2)
        e_att = at_xh("e_att", [P, 2, 512])
        at_xl = Region(xl_at, xl_at + 8 * T * 2)
        e_osq = at_xl("e_osq", [P, 512])
        e_y = at_xl("e_y", [P, 512])

        od = Region(overlay)
        o_z = od("o_z", [P, 6, T])
        o_q = od("o_q", [P, 6, T])
        o_k = od("o_k", [P, 6, 2 * T])
        o_v = od("o_v", [P, 2 * NT, 768])
        o_turn = od("o_turn", [P, 2, T])
        o_p = od("o_p", [P, 2, 2, 2 * T])
        o_aT = od("o_aT", [P, 2, 2 * T])
        o_o = od("o_o", [P, 6, T])
        o_sq = od("o_sq", [P, 6, T])
        o_u = od("o_u", [P, 2, T + 2])
        o_c = od("o_c", [P, 2, T])
        o_st = od("o_st", [P, 12, 6])

        h_out = Region(out_at)("h_out", [P, DC, T])
        hy = Region(overlay)
        h_small = hy("h_small", [P, NT, 84])
        h_yh = hy("h_yh", [P, 4, T], F32R)
        h_yl = hy("h_yl", [P, 4, T], F32R)
        h_gates = hy("h_gates", [P, DC, T])
        h_merged = hT[:, :, T:2 * T]
        branch = hy.at
        hm = Region(branch)
        m_in = hm("m_in", [P, 12, T])
        m_cv = hm("m_cv", [P, 8, T])
        m_sw = hm("m_sw", [P, DC, 84])
        m_sw_h = hm("m_sw_h", [P, DC, 84], F32R)
        m_sw_l = hm("m_sw_l", [P, DC, 84], F32R)
        m_x = hm("m_x", [P, NT, 512])
        m_dt = hm("m_dt", [P, 6, 16])
        m_cs = hm("m_cs", [8, T])
        m_ncs = hm("m_ncs", [P, 16])
        m_e = hm("m_e", [P, 2, 384])
        m_y = hm("m_y", [P, 4, T])
        m_sq = hm("m_sq", [P, 4, T])
        m_d = hm("m_d", [P, 4])
        ha = Region(branch)
        second = Region(hm.at)
        qk_set = [r(f"a_qk{j}", [P, 8, T]) for j, r in enumerate((second, ha))]
        v_set = [r(f"a_v{j}", [P, NT, 512]) for j, r in enumerate((second, ha))]
        a_iq = second("a_iq", [P, 2, T])
        a_p = ha("a_p", [P, 2, T])
        a_pT = ha("a_pT", [P, 2, T])
        a_st = ha("a_st", [P, 16, 3])
        a_bias = ha("a_bias", [P, 2, 384])
        a_turn = ha("a_turn", [P, 2, T])
        a_f = ha("a_f", [P, 4, 16])
        a_cf = ha("a_cf", [8, T])
        a_ik2 = ha("a_ik2", [P, NT, P])
        a_ik = ha("a_ik", [P, T])
        a_isc = ha("a_isc", [P, T])
        a_relu = ha("a_relu", [P, T])
        a_top = ha("a_top", [P, 8])
        a_w = ha("a_w", [P, NT, 4])

        ps = ctx.enter_context(nc.psum_tensor("ps", [P, 8, 512], F32))

        sems = {}

        def S(name):
            if name not in sems:
                sems[name] = ctx.enter_context(nc.semaphore(name))
            return sems[name]

        vec_at, row_parts, n = {}, [], 0
        for name, ap in io["vectors"]:
            r = ap.shape[0]
            vec_at[name] = n
            done = 0
            while done < r:
                m = min(r - done, P - n % P)
                row_parts.append((n // P, n % P, m, ap[done:done + m, :]))
                done += m
                n += m
        n_rows = n
        assert n_rows <= 512
        V = lambda name, i=0, k=1: vec[:, vec_at[name] + i:vec_at[name] + i + k]

        def e_keys(dr, q):
            sl = slice((1 - q) * T, (2 - q) * T)
            return (e_kd, e_qd) if dr == 0 else (e_z[:, 5:8, sl], e_z[:, 2:5, sl])

        class Count:
            def __init__(self):
                self.units = 0
                self.hidden = 0
                self.of = Counter()

            def add(self, **events):
                self.of.update(events)

        CREDIT = 2
        HALF_CREDIT = 2 * CREDIT

        def halves(i, u, h):
            return 4 * i + (2 * u + h + 1)

        def half_free(i, u, h):
            return halves(i, u - CREDIT, h) + HALF_CREDIT

        def sp_units(sp, c, pairs, source, width, beside=None):
            def pair(i):
                for s in range(2):
                    for half in range(2):
                        sp.wait_ge(S("lo_ready"), half_free(i, c.units + s, half))
                        src = source(i, s, half)
                        dst = raw[:, s, half, 0:width // 2]
                        sp.dma_start(dst.rearrange("p (k n) -> p k n", n=src.shape[2]), src)\
                            .then_inc(S(f"raw_landed{s}{half}"), 16)
                    if beside:
                        beside(i, s)
            if pairs == 1:
                pair(0)
            else:
                with sp.Fori(0, pairs) as i:
                    pair(i)
            c.units += 2 * pairs

        def columns(w, k0, kc, n0, step, width):
            v = w[k0 * P:(k0 + kc) * P, :].rearrange("(c p) n -> p c n", p=P)
            return lambda i, s, half: v[:, half * kc // 2:(half + 1) * kc // 2,
                                        bass.ds(i * (2 * step) + (n0 + step * s), width)]

        def act_split(act, i, s, u, which=range(2)):
            for h in which:
                act.wait_ge(S(f"raw_landed{s}{h}"), (i + u // 2) * 16 + 16)
                act.wait_ge(S("mm_done"), half_free(i, u, h))
                nc.scalar.activation(whi[:, s, h, :], raw[:, s, h, :], ACT.Copy).then_inc(S("hi_ready"), 1)

        def dve_split(dve, i, s, u, which=range(2)):
            for h in which:
                dve.wait_ge(S("hi_ready"), halves(i, u, h))
                nc.vector.tensor_tensor(wlo[:, s, h, :], raw[:, s, h, :], whi[:, s, h, :].bitcast(F32),
                                        ALU.subtract).then_inc(S("lo_ready"), 1)

        def pairs_of(eng, c, pairs, body, ahead=None, final=False, first=False, before=None):
            def pair(i, last):
                for s in range(2):
                    if before:
                        before(i, s)
                    if ahead is not None and not (last and s == 1):
                        ahead(eng, i, 1 - s, c.units + s + 1)
                    body(i, s)
            begin, end = int(first), pairs - int(final)
            if first:
                pair(0, False)
            if end - begin >= 2:
                with eng.Fori(begin, end) as i:
                    pair(i, False)
            elif end - begin == 1:
                pair(begin, False)
            if final:
                pair(pairs - 1, True)
            c.units += 2 * pairs

        def pe_banks_free(pe, c, i, s):
            pe.wait_ge(S("evac_done"), 2 * i + (c.units + s + 1))

        def pe_half_ready(pe, c, i, s, h):
            pe.wait_ge(S("lo_ready"), halves(i, c.units + s, h) + HALF_CREDIT)

        def three(dst, w_h, w_l, x_h, x_l, start, stop):
            nc.tensor.matmul(dst, w_h, x_h, start=start, stop=False)
            nc.tensor.matmul(dst, w_h, x_l, start=False, stop=False)
            return nc.tensor.matmul(dst, w_l, x_h, start=False, stop=stop)

        def half_of(s, h, chunks, width):
            v = lambda w: w[:, s, h, 0:chunks * width].rearrange("p (k n) -> p k n", n=width)
            return v(whi), v(wlo)

        def pe_blocks(pe, c, i, s, kc, n_tok, x_h, x_l, blocks, width, x_ready=None):
            pe_banks_free(pe, c, i, s)
            for h in range(2):
                pe_half_ready(pe, c, i, s, h)
                w_h, w_l = half_of(s, h, kc // 2, width)
                for b in range(blocks):
                    for j in range(kc // 2):
                        k = h * (kc // 2) + j
                        if x_ready and b == 0:
                            x_ready(k)
                        m = three(ps[:, 2 * s + b, 0:n_tok], w_h[:, j, b * P:(b + 1) * P],
                                  w_l[:, j, b * P:(b + 1) * P], x_h[:, k, 0:n_tok], x_l[:, k, 0:n_tok],
                                  k == 0, k == kc - 1)
                m.then_inc(S("mm_done"), 1)

        def pe_tokens(pe, c, i, s, kc, n_tiles, x_h, x_l, width):
            pe_banks_free(pe, c, i, s)
            flat = ps[:, 2 * s:2 * s + 2, :].rearrange("p a b -> p (a b)")
            for h in range(2):
                pe_half_ready(pe, c, i, s, h)
            for t in range(n_tiles):
                for k in range(kc):
                    w_h, w_l = half_of(s, 2 * k // kc, kc // 2, width)
                    tt, j = slice(t * P, (t + 1) * P), k % (kc // 2)
                    m = three(flat[:, t * width:(t + 1) * width], x_h[:, k, tt], x_l[:, k, tt],
                              w_h[:, j, :], w_l[:, j, :], k == 0, k == kc - 1)
            m.then_inc(S("mm_done"), 2)

        def unit_done(eng, c, i, s, h=1):
            eng.wait_ge(S("mm_done"), halves(i, c.units + s, h) + HALF_CREDIT)

        def is_first(i, s):
            return isinstance(i, int) and i == 0 and s == 0

        class Link:

            def __init__(self, eng, name):
                self.eng, self.sem, self.n = eng, S(name), 0

            def __call__(self, ins):
                self.n += 1
                ins.then_inc(self.sem, 1)
                self.eng.wait_ge(self.sem, self.n)

        def fm_evac(dst, c0, n_tok):
            def body(dve, c, i, s):
                unit_done(dve, c, i, s)
                nc.vector.tensor_copy(dst[:, bass.ds(i * 4 + (c0 + 2 * s), 2), 0:n_tok],
                                      ps[:, 2 * s:2 * s + 2, 0:n_tok]).then_inc(S("evac_done"), 1)
            return body

        def mod_columns(layer, m):
            v = io["ada_w"][layer].rearrange("(c p) n -> p c n", p=P)
            return v[:, :, bass.ds(m * 256, 256)]

        def mod_landings(layer, m0):
            return 16 * ((MOD_UNITS * layer + m0 - MOD_FIRST) // 2 + 1)

        DVE_STEPS, POOL_STEPS = DC, 2 * DC - 1

        def mod_step(steps, layer, m0, i, s):
            return 2 * steps * i + steps * (MOD_UNITS * layer + m0 + s)

        def parts(pairs, mod_part):
            if not mod_part:
                return [(0, pairs, None)]
            layer, m0, n = mod_part
            return [(0, n, (layer, m0))] + ([(n, pairs - n, None)] if n < pairs else [])

        class Beside:

            def __init__(self, n, places):
                self.units = [("qk", i) for i in range(4)] + [("v", i) for i in range(2)] if n < 3 else []
                if n == 2:
                    self.units += [("iq", i) for i in range(2)]
                self.units += [("gate", i) for i in range(4)]
                blocks = [(j, b) for j, (kind, _) in enumerate(self.units) for b in range(1 if kind == "iq" else 2)]
                place = [p * places // len(blocks) for p in range(len(blocks))]
                self.blocks = [[x for x, at in zip(blocks, place) if at == p] for p in range(places)]
                self.first = [min(at for (j, _), at in zip(blocks, place) if j == u) for u in range(len(self.units))]
                self.last = [max(at for (j, _), at in zip(blocks, place) if j == u) for u in range(len(self.units))]

            def splits(self, lo, hi):
                ends = self.first[1:] + [self.first[-1] + 3]
                return [(j + 1, h) for j, (p, end) in enumerate(zip(self.first, ends))
                        for h, at in enumerate((p, (p + end) // 2)) if lo <= at < hi]

            def reads(self, lo, hi):
                return [j for j, p in enumerate(self.last) if lo <= p < hi]

        MAMBA_PLACES, ATTENTION_PLACES, DSA_PLACES = 12, 32, 4
        places_of = lambda n: (MAMBA_PLACES, ATTENTION_PLACES, ATTENTION_PLACES, DSA_PLACES)[n]


        schedule = []
        none = (None,) * 4
        beside = {("ffn1", 0): ((0, 8, 6), (0, 20, 4), (0, 28, 4), (1, 0, 4)),
                  ("ffn2", 0): ((1, 8, 6), (1, 20, 4), (1, 28, 4), None)}
        for layer, mixer, w_in in ((0, "even", io["even_w_in"][0]), (1, "odd", io["odd_w_in"][0])):
            nc_ = 2 - layer
            b0 = 8 * N_MOD * layer
            g = lambda n, l=layer: (lambda k, j: gains[:, l, n, k, j:j + 1])
            sh = lambda n, b0=b0: (lambda k, j: mod[:, b0 + 24 * n + k, j:j + 1])
            schedule += [
                ("gains", layer, 0, "norm_ffn1"),
                ("norm", hT, 2, sh(0), g(0)),
                ("ffn", io["ffn1_w_in"][layer], io["ffn1_w_out"][layer], 2 * T, (layer, 0), False,
                 beside.get(("ffn1", layer), none)),
                ("gains", layer, 1, "norm_mix"),
                ("norm", hT, 2, sh(1), g(1)),
                (mixer, w_in),
                ("out", io["mix_w_out"][layer], nc_ * T, layer),
                ("gains", layer, 2, "norm_ffn2"),
                ("norm", hT, nc_, sh(2), g(2)),
                ("ffn", io["ffn2_w_in"][layer], io["ffn2_w_out"][layer], nc_ * T, (layer, 2), False,
                 beside.get(("ffn2", layer), none)),
            ]
        schedule += [("renorm", hT, lambda k: V("final_norm", k), True)]
        for layer in range(2):
            gain = lambda name, l=layer: (lambda k, j=0: V(name, DC * l + k))
            w_in = io["w_in_2"][layer]
            schedule += [
                ("norm", hT, 1, None, gain("norm_mix_pre_2")),
                ("mamba", layer, w_in),
                ("beside", layer, 0, w_in),
                ("branch", layer, 0),
                ("beside", layer, 1, w_in),
                ("attention", layer, 0),
                ("branch", layer, 1),
                ("beside", layer, 2, w_in),
                ("attention", layer, 1),
                ("branch", layer, 2),
                ("beside", layer, 3, w_in),
                ("attention", layer, 2),
                ("branch", layer, 3),
                ("wout", layer, io["w_out_2"][layer]),
                ("renorm", h_out, gain("norm_mix_post_2"), True),
                ("norm", hT, 1, None, gain("norm_ffn_pre_2")),
                ("ffn", io["w_ffn_in_2"][layer], io["w_ffn_out_2"][layer], T, None, layer == 1, none),
                ("renorm", h_out, gain("norm_ffn_post_2"), layer == 0),
            ]
        schedule += [("store",)]

        block = ctx.enter_context(nc.Block())

        @block.sync
        def _(sp):
            c = Count()
            early = const_at["eps"][1]
            sp.dma_start(consts[:, 0:early], io["consts"][:, 0:early]).then_inc(S("consts_in"), 16)
            for tile, r0, m, src in row_parts:
                sp.dma_start(rows[r0:r0 + m, tile, :], src).then_inc(S("rows_in"), 16)
            for t in range(NT):
                sp.dma_start(tok[:, t, :], io["x"][0, t * P:(t + 1) * P, :]).then_inc(S("tok_in"), 16)
                sp.dma_start(tok[:, NT + t, :], io["ctx"][0, t * P:(t + 1) * P, :]).then_inc(S("tok_in"), 16)
            sp_units(sp, c, MOD_FIRST // 2, columns(io["ada_w"][0], 0, DC, 0, 256, 256), UNIT)
            sp.dma_start(consts[:, early:], io["consts"][:, early:]).then_inc(S("consts_in"), 16)
            for j, name in enumerate(("lambda_q1", "lambda_k1", "lambda_q2", "lambda_k2")):
                sp.dma_start(lam_in[:, j:j + 1], io[name].rearrange("a d -> d a")).then_inc(S("lam_landed"), 16)
            for j, name in enumerate(("dt_bias_2", "a_log_2", "fox_fbias_2", "d_skip_2")):
                sp.dma_start(small_rows[0:1, 16 * j:16 * j + 16],
                             io[name].rearrange("(o l) h -> o (l h)", o=1)).then_inc(S("lam_landed"), 16)

            def mod_unit(layer, m0):
                def load(i, s):
                    sp.wait_ge(S("mod_mm"), 2 * i + (MOD_UNITS * layer + m0 + s - 1))
                    sp.dma_start(mod_w[:, s, :, :], mod_columns(layer, i * 2 + (m0 + s))).then_inc(S(f"mod_landed{s}"), 16)
                return load

            def ffn(w_in, w_out, mods):
                v = w_in.rearrange("(c p) (g f) -> p c g f", p=P, g=2)
                j0 = 0
                for n, half in enumerate(HALVES):
                    up = lambda p0: lambda i, s, g: v[:, :, g, bass.ds(i * 256 + (j0 + 2 * p0 + s) * P, P)]
                    for p0, pairs, mod_part in parts(half // 2, mods[2 * n]):
                        sp_units(sp, c, pairs, up(p0), UNIT, mod_part and mod_unit(*mod_part))
                    for p0, pairs, mod_part in parts(4, mods[2 * n + 1]):
                        sp_units(sp, c, pairs, columns(w_out, j0, half, 2 * p0 * P, P, P), half * P,
                                 mod_part and mod_unit(*mod_part))
                    j0 += half


            def even(w_in):
                sp_units(sp, c, 2, columns(w_in, 0, DC, 0, 256, 256), UNIT)
                sp.wait_ge(S("norm_lo"), c.of["norm_hi"])
                sp.dma_start(e_small[:, :, :], w_in[:, 2560:2592].rearrange("(c p) n -> p c n", p=P))\
                    .then_inc(S("e_small_in"), 16)
                sp.wait_ge(S("e_gw_zero"), 1)
                for dr in range(2):
                    sp.dma_start(e_gw[16 * dr:16 * dr + 16, dr, :], io["gla_gate_w"][0, dr, :, :])\
                        .then_inc(S("e_gw_in"), 16)
                    sp.dma_start(e_gw[32:33, dr, :], io["gla_gate_b"][0, dr:dr + 1, :]).then_inc(S("e_gw_in"), 16)
                v = w_in.rearrange("(c p) n -> p c n", p=P)
                sp_units(sp, c, 3, lambda i, s, half: v[:, 4 * half:4 * half + 4,
                                                        bass.ds(i * 256 + (1792, 1024)[s], 256)], UNIT)

            def odd(w_in):
                v = w_in.rearrange("(c p) n -> p c n", p=P)
                for lo, hi in ((0, 768), (1536, 2304)):
                    sp_units(sp, c, 3, lambda i, s, half: v[:, 4 * half:4 * half + 4,
                                                            bass.ds(i * 256 + (lo, hi)[s], 256)], UNIT)

            def mamba(layer, w_in):
                sp_units(sp, c, 3, columns(w_in, 0, DC, Z0, 256, 256), UNIT)
                sp.wait_ge(S("norm_lo"), c.of["norm_hi"])
                for at, n0, n in ((0, DT0, 8), (8, FF0, 8), (16, IK0, 68)):
                    sp.dma_start(m_sw[:, :, at:at + n], w_in[:, n0:n0 + n].rearrange("(c p) n -> p c n", p=P))\
                        .then_inc(S("m_sw_in"), 16)

            def beside_and_branch(layer, n, w_in):
                if n < 3:
                    q0, v0 = ((FQ0, FV0), (MQ0, MV0), (DQ0, DV0))[n]
                    sp_units(sp, c, 2, columns(w_in, 0, DC, q0, 256, 256), UNIT)
                    sp_units(sp, c, 1, columns(w_in, 0, DC, v0, 256, 256), UNIT)
                if n == 2:
                    sp_units(sp, c, 1, columns(w_in, 0, DC, IQ0, P, P), DC * P)
                sp_units(sp, c, 2, columns(io["w_gate_2"][layer], 0, DC, n * D, 256, 256), UNIT)
                sp_units(sp, c, 1, columns(io["w_branch_2"][layer, n], 0, 4, 0, 512, 512), UNIT)


            for stage, *args in schedule:
                if stage == "norm":
                    c.add(norm_hi=DC * args[1])
                elif stage == "ffn":
                    ffn(args[0], args[1], args[5])
                elif stage in ("even", "odd"):
                    {"even": even, "odd": odd}[stage](*args)
                elif stage == "out":
                    sp_units(sp, c, 2, columns(args[0], 0, DC, 0, 256, 256), UNIT)
                elif stage == "mamba":
                    mamba(*args)
                elif stage == "beside":
                    beside_and_branch(*args)
                elif stage == "wout":
                    sp_units(sp, c, 2, columns(args[1], 0, DC, 0, 256, 256), UNIT)
                elif stage == "store":
                    sp.wait_ge(S("y_copied"), 2)
                    for t in range(NT):
                        sp.dma_start(io["out"][0, t * P:(t + 1) * P, :], y_tok[:, t, :]).then_inc(S("stored"), 16)
                    sp.wait_ge(S("stored"), 16 * NT)

        @block.tensor
        def _(pe):
            c = Count()
            pe.sem_inc(S("mm_done"), HALF_CREDIT)
            ident = K("ident")
            pe.wait_ge(S("consts_in"), 16)
            pe.wait_ge(S("rows_in"), 16 * len(row_parts))
            for t in range((n_rows + P - 1) // P):
                m = min(P, n_rows - t * P)
                ins = nc.tensor.transpose(ps[:, 7, t * P:t * P + m], rows[0:m, t, :], ident[0:m, 0:m])
            ins.then_inc(S("vec_t"), 1)
            pe.wait_ge(S("tok_in"), 16 * 2 * NT)
            for k in range(DC):
                if k == 7:
                    pe.wait_ge(S("vec_ready"), 1)
                for t in range(2 * NT):
                    ins = nc.tensor.transpose(ps[:, k, t * P:(t + 1) * P], tok[:, t, k * P:(k + 1) * P], ident)
                ins.then_inc(S("h_t"), 1)
            pe.wait_ge(S("h_in"), DC)
            pe.wait_ge(S("cond_lo"), 1)
            def mod_first(i, s):
                pe_banks_free(pe, c, i, s)
                for h in range(2):
                    pe_half_ready(pe, c, i, s, h)
                for k in range(DC):
                    w_h, w_l = half_of(s, k // 4, 4, 2 * P)
                    m = three(ps[0:2, 2 * s, 0:2 * P], cond_h[:, k, :], cond_l[:, k, :],
                              w_h[:, k % 4, :], w_l[:, k % 4, :], k == 0, k == DC - 1)
                m.then_inc(S("mm_done"), 2)
            pairs_of(pe, c, MOD_FIRST // 2, mod_first)
            pe.wait_ge(S("evac_done"), c.units + CREDIT)
            for b in range(2 * MOD_FIRST):
                ins = nc.tensor.transpose(ps[:, 5, 2 * b:2 * b + 2], mod_rows[:, b * P:(b + 1) * P], ident[0:2, 0:2])
            ins.then_inc(S("mod_mm"), MOD_FIRST)

            def mod_unit(layer, m0):
                def multiply(i, s):
                    u = 2 * i + (MOD_UNITS * layer + m0 + s)
                    pe.wait_ge(S("mod_sum0"), mod_step(DVE_STEPS, layer, m0, i, s + 1))
                    pe.wait_ge(S("mod_sum1"), mod_step(POOL_STEPS, layer, m0, i, s + 1))
                    pe.wait_ge(S("mod_evac"), u - 1)
                    for b in range(2):
                        for j in range(2):
                            m = nc.tensor.matmul(ps[:, 6 + s, 2 * b + j:2 * b + j + 1],
                                                 mod_acc[:, s, (2 * j + b) * P:(2 * j + b + 1) * P], K("ones")[:, 0:1],
                                                 start=True, stop=True)
                    m.then_inc(S("mod_mm"), 1)
                return multiply

            def ss_sum(n_tiles):
                c.add(blocks=DC)
                pe.wait_ge(S("sq_added"), c.of["blocks"] + CREDIT)
                if c.of["norm"]:
                    pe.wait_ge(S("root_ready"), c.of["norm"])
                for t in range(n_tiles):
                    m = nc.tensor.matmul(ps[:, 4, t:t + 1], ss[:, t * P:(t + 1) * P], K("ones")[:, 0:1],
                                         start=True, stop=True)
                m.then_inc(S("ss_mm"), 1)

            def spread_rstd(n_tiles):
                pe.wait_ge(S("rstd_col"), c.of["norm"] + 1)
                for t in range(n_tiles):
                    m = nc.tensor.matmul(ps[:, 5, t * P:(t + 1) * P], rstd_col[:, t:t + 1].to_broadcast([P, P]), ident,
                                         start=True, stop=True)
                m.then_inc(S("rstd_mm"), 1)
                c.add(norm=1)

            def norm_ready(n_cond):
                base = c.of["norm_hi"]
                c.add(norm_hi=DC * n_cond)
                return lambda k: pe.wait_ge(S("norm_lo"), base + (k + 1) * n_cond)

            ss_sum(2 * NT)
            pe.wait_ge(S("lam_prod"), 1)
            nc.tensor.matmul(ps[:, 6, 0:2], K("ones")[0:HD, :], lam_prod[:, :], start=True, stop=True)
            nc.tensor.matmul(ps[:, 6, 64:128], K("ones")[0:1, :], small_rows[0:1, :], start=True, stop=True)\
                .then_inc(S("bcast_mm"), 1)
            pe.wait_ge(S("bcast_ready"), 1)
            pe.wait_ge(S("consts_in"), 32)

            def ffn(n_tok, mods):
                for n, half in enumerate(HALVES):
                    def up(i, s):
                        pe_banks_free(pe, c, i, s)
                        for g in range(2):
                            pe_half_ready(pe, c, i, s, g)
                            w_h, w_l = half_of(s, g, DC, P)
                            for k in range(DC):
                                if n == 0 and g == 0 and is_first(i, s):
                                    x_ready(k)
                                m = three(ps[:, 2 * s + g, 0:n_tok], w_h[:, k, :], w_l[:, k, :],
                                          xh[:, k, 0:n_tok], xl[:, k, 0:n_tok], k == 0, k == DC - 1)
                            m.then_inc(S("mm_done"), 1)
                    hidden = c.hidden + CREDIT
                    def hidden_ready(k):
                        pe.wait_ge(S("hid_l_ready"), hidden + k + 1)
                    def down(i, s):
                        pe_blocks(pe, c, i, s, half, n_tok, hid_h, hid_l, 1, P,
                                  hidden_ready if is_first(i, s) else None)
                    for body, total, mod_part in ((up, half // 2, mods[2 * n]), (down, 4, mods[2 * n + 1])):
                        for p0, pairs, part in parts(total, mod_part):
                            beside = part and mod_unit(*part)
                            pairs_of(pe, c, pairs, lambda i, s: (body(i, s), beside and beside(i, s)), first=p0 == 0)
                    c.hidden += half
                ss_sum(n_tok // P)


            def even():
                pairs_of(pe, c, 2, lambda i, s: pe_blocks(pe, c, i, s, DC, 2 * T, xh, xl, 2, 256,
                                                          x_ready if is_first(i, s) else None), first=True)
                def r_and_v(i, s):
                    if s == 0:
                        pe_blocks(pe, c, i, s, DC, 2 * T, xh, xl, 2, 256)
                    else:
                        pe_tokens(pe, c, i, s, DC, 2 * NT, xh, xl, 256)
                pairs_of(pe, c, 3, r_and_v)
                pe.wait_ge(S("e_small_lo"), 1)
                pe.wait_ge(S("evac_done"), c.units + CREDIT)
                for k in range(DC):
                    m = three(ps[0:32, 6, :], e_small_h[:, k, :], e_small_l[:, k, :], xh[:, k, :], xl[:, k, :],
                              k == 0, k == DC - 1)
                m.then_inc(S("e_gates_mm"), 1)
                pe.wait_ge(S("e_gT"), 1)
                pe.wait_ge(S("e_gw_in"), 16 * 4)

                def logits(q):
                    for n in range(4):
                        tile = (NT, 0)[q] + n // 2
                        nc.tensor.matmul(ps[:, (0, 1, 4, 5)[n], 0:384], e_gT[:, tile * P:(tile + 1) * P],
                                         e_gw[:, n % 2, :], start=True, stop=True).then_inc(S("e_logits"), 1)

                def running(q, n):
                    it = 4 * q + n
                    pe.wait_ge(S("e_log"), it + 1)
                    if n >= 2:
                        pe.wait_ge(S("e_exp"), it - 1)
                    elif n == 1 and q:
                        pe.wait_ge(S("e_y"), 3 * q)
                    for p in range(3):
                        m = nc.tensor.matmul(ps[:, (2, 7)[n % 2], p * P:(p + 1) * P], e_log[:, n, p * P:(p + 1) * P],
                                             K(("cum_fwd", "cum_bwd")[n % 2]), start=True, stop=True)
                    m.then_inc(S("e_cum"), 1)

                def att(q, p):
                    for dr in range(2):
                        kd, qd = e_keys(dr, q)
                        for t in range(NT):
                            tt = slice(t * P, (t + 1) * P)
                            for h in range(2):
                                hh = slice(64 * h, 64 * h + 64)
                                m = nc.tensor.matmul(ps[:, 4 + h, (2 * dr + t) * P:(2 * dr + t + 1) * P],
                                                     kd[hh, p, tt], qd[hh, p, tt], start=True, stop=True)
                    m.then_inc(S("e_att_mm"), 1)

                logits(0)
                for q in range(2):
                    tile0 = (NT, 0)[q]
                    running(q, 0)
                    for n in range(4):
                        it = 4 * q + n
                        if n < 3:
                            running(q, n + 1)
                        pe.wait_ge(S("e_decayed"), it + 1)
                        if it:
                            pe.wait_ge(S("e_kkT"), it)
                        if n == 0 and q:
                            pe.wait_ge(S("e_oroot"), 3 * q)
                        for p in range(3):
                            m = nc.tensor.transpose(ps[:, 3, p * P:(p + 1) * P], e_kk[:, p, :], ident)
                        m.then_inc(S("e_kk_t"), 1)
                    if q == 0:
                        logits(1)
                    pe.wait_ge(S("e_kkT"), 4 * q + 4)
                    pe.wait_ge(S("e_exp"), 4 * q + 4)
                    for step in range(8):
                        dr = step % 2
                        ch = step // 2 if dr == 0 else 3 - step // 2
                        if step >= 2 or q:
                            pe.wait_ge(S("e_state"), 8 * q + step - 1)
                        rows_ = slice(64 * (ch % 2), 64 * (ch % 2) + 64)
                        for h in range(6):
                            m = nc.tensor.matmul(
                                ps[64 * (h % 2):64 * (h % 2) + 64, (6, 2)[dr], (h // 2) * P:(h // 2 + 1) * P],
                                e_kkT[rows_, dr, ch // 2, h * 64:(h + 1) * 64],
                                e_v[rows_, tile0 + ch // 2, h * P:(h + 1) * P], start=True, stop=True)
                        m.then_inc(S("e_kv"), 1)
                    pe.wait_ge(S("e_state"), 8 * q + 8)
                    pe.wait_ge(S("e_log"), 8)
                    att(q, 0)
                    for p in range(3):
                        o = 3 * q + p
                        bank = (6, 0)[o % 2]
                        pe.wait_ge(S("e_att"), o + 1)
                        if o >= 2:
                            pe.wait_ge(S("e_y"), o - 1)
                        for h in range(2):
                            hh = slice(64 * h, 64 * h + 64)
                            for t in range(NT):
                                dst = ps[:, bank + h, t * P:(t + 1) * P]
                                vv = e_v[:, tile0 + t, (2 * p + h) * P:(2 * p + h + 1) * P]
                                for dr in range(2):
                                    nc.tensor.matmul(dst, vv, e_att[:, h, (2 * dr + t) * P:(2 * dr + t + 1) * P],
                                                     start=dr == 0, stop=False)
                                for dr in range(2):
                                    qd = e_keys(dr, q)[1]
                                    for half in range(2):
                                        ch = 2 * t + half
                                        cc = slice(ch * 64, ch * 64 + 64)
                                        m = nc.tensor.matmul(ps[:, bank + h, ch * 64:ch * 64 + 64],
                                                             e_S[hh, dr, ch if dr == 0 else 3 - ch, p, :],
                                                             qd[hh, p, cc], start=False,
                                                             stop=dr == 1 and half == 1)
                        m.then_inc(S("e_o"), 1)
                        if p < 2:
                            att(q, p + 1)
                        pe.wait_ge(S("e_osq"), o + 1)
                        if o:
                            pe.wait_ge(S("e_oroot"), o)
                        nc.tensor.matmul(ps[:, 3, :], K("ones"), e_osq[:, :], start=True, stop=True)\
                            .then_inc(S("e_oss"), 1)
                for n in range(4):
                    q, k = divmod(n, 2)
                    if n:
                        pe.wait_ge(S("e_fab"), n)
                    for t in range(NT):
                        m = nc.tensor.matmul(ps[:, 4, t * T:(t + 1) * T],
                                             e_z[:, k, q * T + t * P:q * T + (t + 1) * P],
                                             consts[:, const_at["dft_cos"][0]:const_at["dft_sin"][1]],
                                             start=True, stop=True)
                    m.then_inc(S("e_f1"), 1)
                    pe.wait_ge(S("e_fab"), n + 1)
                    if n:
                        pe.wait_ge(S("e_fl"), n)
                    for t in range(NT):
                        nc.tensor.matmul(ps[:, 5, 0:T], e_ab[:, t, 0:P], K("dft_tok_cos")[:, t * T:(t + 1) * T],
                                         start=t == 0, stop=False)
                        m = nc.tensor.matmul(ps[:, 5, 0:T], e_ab[:, t, P:2 * P],
                                             K("dft_tok_nsin")[:, t * T:(t + 1) * T],
                                             start=False, stop=t == NT - 1)
                    m.then_inc(S("e_f2"), 1)
                pe.wait_ge(S("e_fl"), 4)
                pe.wait_ge(S("e_yl"), 6)

            def odd():
                pairs_of(pe, c, 3, lambda i, s: pe_blocks(pe, c, i, s, DC, T, xh, xl, 2, 256,
                                                          x_ready if is_first(i, s) else None), first=True)
                def k_and_v(i, s):
                    if s == 0:
                        pe_blocks(pe, c, i, s, DC, 2 * T, xh, xl, 2, 256)
                    else:
                        pe_tokens(pe, c, i, s, DC, 2 * NT, xh, xl, 256)
                pairs_of(pe, c, 3, k_and_v)
                pe.wait_ge(S("evac_done"), c.units + CREDIT)
                for n in range(6):
                    buf, k = (o_q, 2 * n) if n < 3 else (o_k, 2 * n - 6)
                    for j in range(2):
                        m = nc.tensor.matmul(ps[:, n, j * T:(j + 1) * T], K("axial_swap"), buf[:, k + j, 0:T],
                                             start=True, stop=True)
                    m.then_inc(S("o_swap"), 1)

                def scores(e):
                    h, qt = divmod(e, 2)
                    if e >= 2:
                        pe.wait_ge(S("o_exp"), e - 1)
                    for s in range(2):
                        rr = slice(64 * s, 64 * s + 64)
                        m = nc.tensor.matmul(ps[:, 4 + 2 * (e % 2) + s, :], o_q[rr, h, qt * P:(qt + 1) * P],
                                             o_k[rr, h, :], start=True, stop=True)
                    m.then_inc(S("o_scores"), 1)

                pe.wait_ge(S("o_turned"), 6)
                scores(0)
                def squares(p):
                    pe.wait_ge(S("o_sq"), p + 1)
                    nc.tensor.matmul(ps[:, 4 + p, :], K("ones"),
                                     o_sq[:, 2 * p:2 * p + 2, :].rearrange("p a b -> p (a b)"),
                                     start=True, stop=True).then_inc(S("o_ss"), 1)

                for e in range(13):
                    if e + 1 < 12:
                        scores(e + 1)
                    if e < 12:
                        pe.wait_ge(S("o_a"), e + 1)
                        if e >= 2:
                            pe.wait_ge(S("o_aT"), e - 1)
                        for kt in range(2 * NT):
                            m = nc.tensor.transpose(ps[:, 2 + e % 2, kt * P:(kt + 1) * P],
                                                    o_p[:, e % 2, 0, kt * P:(kt + 1) * P], ident)
                        m.then_inc(S("o_t"), 1)
                    if e == 11:
                        for p in range(2):
                            squares(p)
                    if e:
                        h, qt = divmod(e - 1, 2)
                        pe.wait_ge(S("o_aT"), e)
                        if qt == 0 and h >= 2:
                            pe.wait_ge(S("o_out"), h - 1)
                        for kt in range(2 * NT):
                            m = nc.tensor.matmul(ps[:, h % 2, qt * P:(qt + 1) * P], o_v[:, kt, h * P:(h + 1) * P],
                                                 o_aT[:, (e - 1) % 2, kt * P:(kt + 1) * P],
                                                 start=kt == 0, stop=kt == 2 * NT - 1)
                        m.then_inc(S("o_pv"), 1)
                squares(2)
                pe.wait_ge(S("o_yl"), 2)

            def fm_pairs(pairs, kc, blocks, width, x_h=xh, x_l=xl):
                pairs_of(pe, c, pairs, lambda i, s: pe_blocks(pe, c, i, s, kc, T, x_h, x_l, blocks, width))

            def beside_block(beside, j, b):
                i, s = divmod(j, 2)
                kind, last = beside.units[j][0], beside.units[j][0] == "iq" or b == 1
                width = P if kind == "iq" else 256
                if b == 0:
                    pe_banks_free(pe, c, i, s)
                    for h in range(2):
                        pe_half_ready(pe, c, i, s, h)
                for k in range(DC):
                    w_h, w_l = half_of(s, k // 4, 4, width)
                    cols = slice(b * P, (b + 1) * P)
                    dst = ps[:, s, b * T:(b + 1) * T]
                    if kind == "v":
                        m = three(dst, xh[:, k, cols], xl[:, k, cols], w_h[:, k % 4, :], w_l[:, k % 4, :],
                                  k == 0, k == DC - 1)
                    else:
                        m = three(dst, w_h[:, k % 4, cols], w_l[:, k % 4, cols], xh[:, k, 0:T], xl[:, k, 0:T],
                                  k == 0, k == DC - 1)
                    if last and k % 4 == 3:
                        m.then_inc(S("mm_done"), 1)

            def beside_blocks(beside, place):
                for j, b in beside.blocks[place]:
                    beside_block(beside, j, b)

            def branch(layer, n):
                pe.wait_ge(S("evac_done"), c.units + CREDIT)
                for s in range(2):
                    for h in range(2):
                        pe_half_ready(pe, c, 0, s, h)
                    for b in range(4):
                        for k in range(4):
                            w_h, w_l = half_of(s, k // 2, 2, 512)
                            cols = slice(b * P, (b + 1) * P)
                            m = three(ps[:, 2 * s + b // 2, (b % 2) * T:(b % 2 + 1) * T], w_h[:, k % 2, cols],
                                      w_l[:, k % 2, cols], h_yh[:, k, :], h_yl[:, k, :], k == 0, k == 3)
                            if b == 3 and k % 2:
                                m.then_inc(S("mm_done"), 1)
                c.units += 2

            def mamba(layer):
                beside = Beside(0, MAMBA_PLACES)
                pairs_of(pe, c, 3, lambda i, s: pe_blocks(pe, c, i, s, DC, T, xh, xl, 2, 256,
                                                          x_ready if is_first(i, s) else None), first=True)
                pe.wait_ge(S("m_sw_lo"), layer + 1)
                for t in range(NT):
                    tt = slice(t * P, (t + 1) * P)
                    for k in range(DC):
                        m = three(ps[:, 5, t * 84:(t + 1) * 84], xh[:, k, tt], xl[:, k, tt],
                                  m_sw_h[:, k, :], m_sw_l[:, k, :], k == 0, k == DC - 1)
                m.then_inc(S("m_small_mm"), 1)
                pe.wait_ge(S("evac_done"), c.units + CREDIT)
                beside_blocks(beside, 0)
                pe.wait_ge(S("m_dt"), 3 * layer + 3)
                for t in range(NT):
                    nc.tensor.matmul(ps[0:8, 2, 0:T], m_dt[:, 4, 8 * t:8 * t + 8], K("cum_all")[:, t * T:(t + 1) * T],
                                     start=t == 0, stop=t == NT - 1)
                for o in range(NT):
                    for t in range(NT):
                        m = nc.tensor.matmul(ps[:, 3, 8 * o:8 * o + 8],
                                             K("cum_all")[:, t * T + o * P:t * T + (o + 1) * P],
                                             m_dt[:, 4, 8 * t:8 * t + 8], start=t == 0, stop=t == NT - 1)
                m.then_inc(S("m_cs_mm"), 1)
                beside_blocks(beside, 1)
                pe.wait_ge(S("m_conv"), 2 * layer + 1)
                pe.wait_ge(S("m_small"), layer + 1)
                for t in range(NT):
                    for k in range(4):
                        m = nc.tensor.transpose(ps[:, 4 + t, k * P:(k + 1) * P], m_cv[:, k, t * P:(t + 1) * P], ident)
                m.then_inc(S("m_x_t"), 1)
                pe.wait_ge(S("m_conv"), 2 * layer + 2)
                pe.wait_ge(S("m_cs"), layer + 1)
                for g in range(2):
                    for t in range(NT):
                        m = nc.tensor.matmul(ps[:, 2 + g, t * T:(t + 1) * T], m_cv[:, 4 + g, t * P:(t + 1) * P],
                                             m_cv[:, 6 + g, :], start=True, stop=True)
                m.then_inc(S("m_cb"), 1)
                pe.wait_ge(S("m_x"), layer + 1)

                def spread(h):
                    if h >= 2:
                        pe.wait_ge(S("m_seg"), 8 * layer + h - 1)
                    nc.tensor.matmul(ps[:, 4 + h % 2, 0:T], K("spread")[0:8, h * P:(h + 1) * P], m_cs[:, :],
                                     start=True, stop=True).then_inc(S("m_row"), 1)
                spread(0)
                for h in range(8):
                    if h + 1 < 8:
                        spread(h + 1)
                    beside_blocks(beside, 2 + h)
                    pe.wait_ge(S("m_score"), 8 * layer + h + 1)
                    p = h // 2
                    if h % 2 == 0 and p >= 2:
                        pe.wait_ge(S("m_y"), 4 * layer + p - 1)
                    hh = slice(64 * (h % 2), 64 * (h % 2) + 64)
                    nc.tensor.matmul(ps[hh, 6 + p % 2, 0:T], m_x[:, 0, h * 64:(h + 1) * 64], m_e[:, h % 2, 0:T],
                                     start=True, stop=False)
                    nc.tensor.matmul(ps[hh, 6 + p % 2, P:T], m_x[:, 1, h * 64:(h + 1) * 64], m_e[:, h % 2, T:T + P],
                                     start=False, stop=True).then_inc(S("m_o"), 1)
                beside_blocks(beside, 10)
                pe.wait_ge(S("m_sq"), layer + 1)
                for g in range(2):
                    for k in range(2):
                        m = nc.tensor.matmul(ps[:, 2 + g, 0:T], K("ones"), m_sq[:, 2 * g + k, :],
                                             start=k == 0, stop=k == 1)
                m.then_inc(S("m_ss"), 1)
                beside_blocks(beside, 11)
                c.units += len(beside.units)
                pe.wait_ge(S("m_yl"), layer + 1)

            def turn(buf, k, n_chunks, bank):
                for j in range(n_chunks):
                    x = buf[:, k + j, :] if n_chunks == 2 else buf[:, :]
                    m = nc.tensor.matmul(ps[:, bank, j * T:(j + 1) * T], K("rope_swap"), x, start=True, stop=True)
                m.then_inc(S("a_swap"), 1)

            def attention(layer, which):
                a = 3 * layer + which
                n = which + 1
                beside = Beside(n, places_of(n))
                a_qk, a_v = qk_set[which % 2], v_set[which % 2]
                pe.wait_ge(S("evac_done"), c.units + CREDIT)
                if which == 0:
                    pe.wait_ge(S("a_f"), 2 * layer + 2)
                    for t in range(NT):
                        nc.tensor.matmul(ps[0:8, 2, 0:T], a_f[:, 2, 8 * t:8 * t + 8],
                                         K("cum_all")[:, t * T:(t + 1) * T], start=t == 0, stop=t == NT - 1)
                    for o in range(NT):
                        for t in range(NT):
                            m = nc.tensor.matmul(ps[:, 3, 8 * o:8 * o + 8],
                                                 K("cum_all")[:, t * T + o * P:t * T + (o + 1) * P],
                                                 a_f[:, 2, 8 * t:8 * t + 8], start=t == 0, stop=t == NT - 1)
                    m.then_inc(S("a_cf_mm"), 1)
                    pe.wait_ge(S("a_cf"), layer + 1)
                else:
                    r0 = 10 * layer + (0, 0, 4)[which]
                    for m in range(4):
                        turn(a_qk, 2 * m, 2, m)
                    if which == 2:
                        turn(a_iq, 0, 2, 4)
                        pe.wait_ge(S("a_ik2"), layer + 1)
                        for t in range(NT):
                            m = nc.tensor.transpose(ps[:, 6, t * P:(t + 1) * P], a_ik2[:, t, :], ident)
                        m.then_inc(S("a_ik_t"), 1)
                        pe.wait_ge(S("a_ik"), layer + 1)
                        turn(a_ik, 0, 1, 5)
                    pe.wait_ge(S("a_turned"), r0 + (0, 4, 6)[which])
                    if which == 2:
                        for place in range(2):
                            beside_blocks(beside, place)
                    if which == 2:
                        for qt in range(NT):
                            if qt:
                                pe.wait_ge(S("a_isc"), NT * layer + qt)
                            for h in range(4):
                                hh = slice(64 * (h % 2), 64 * (h % 2) + 64)
                                m = nc.tensor.matmul(ps[:, 4 + h, 0:(qt + 1) * P], a_iq[hh, h // 2, qt * P:(qt + 1) * P],
                                                     a_ik[hh, 0:(qt + 1) * P], start=True, stop=True)
                            m.then_inc(S("a_idx"), 1)
                            beside_blocks(beside, 2 + qt)
                        pe.wait_ge(S("a_isc"), NT * layer + NT)

                def spread(h):
                    if h:
                        pe.wait_ge(S("a_bias"), 8 * layer + h)
                    nc.tensor.matmul(ps[:, 7, 0:T], K("spread")[0:8, h * P:(h + 1) * P], a_cf[:, :],
                                     start=True, stop=True).then_inc(S("a_row"), 1)

                def scores(e):
                    h, qt = divmod(e, 2)
                    if which == 0 and qt == 0:
                        spread(h)
                    if e >= 2:
                        pe.wait_ge(S("a_max"), 16 * a + e - 1)
                    hh = slice(64 * (h % 2), 64 * (h % 2) + 64)
                    nc.tensor.matmul(ps[:, 4 + e % 2, 0:(qt + 1) * P], a_qk[hh, h // 2, qt * P:(qt + 1) * P],
                                     a_qk[hh, 4 + h // 2, 0:(qt + 1) * P], start=True, stop=True)\
                        .then_inc(S("a_scores"), 1)

                def turned(e):
                    pe.wait_ge(S("a_p"), 16 * a + e + 1)
                    if e:
                        pe.wait_ge(S("a_pT"), 16 * a + e)
                    for kt in range(e % 2 + 1):
                        m = nc.tensor.transpose(ps[:, 6, kt * P:(kt + 1) * P],
                                                a_p[:, e % 2, kt * P:(kt + 1) * P], ident)
                    m.then_inc(S("a_t"), 1)

                def weighted(e):
                    h, qt = divmod(e, 2)
                    p = h // 2
                    pe.wait_ge(S("a_pT"), 16 * a + e + 1)
                    if e % 4 == 0 and p >= 2:
                        pe.wait_ge(S("a_yl"), 4 * a + p - 1)
                    hh = slice(64 * (h % 2), 64 * (h % 2) + 64)
                    for kt in range(qt + 1):
                        m = nc.tensor.matmul(ps[hh, 2 + p % 2, qt * P:(qt + 1) * P], a_v[:, kt, h * 64:(h + 1) * 64],
                                             a_pT[:, e % 2, kt * P:(kt + 1) * P], start=kt == 0, stop=kt == qt)
                    m.then_inc(S("a_pv"), 1)

                scores(0)
                if which < 2:
                    for e in range(16):
                        if e + 1 < 16:
                            scores(e + 1)
                        beside_blocks(beside, 2 * e)
                        turned(e)
                        beside_blocks(beside, 2 * e + 1)
                        weighted(e)
                else:
                    for e in range(17):
                        if e + 1 < 16:
                            scores(e + 1)
                        if e < 16:
                            turned(e)
                        if e:
                            weighted(e - 1)
                pe.wait_ge(S("a_yl"), 4 * a + 4)
                c.units += len(beside.units)


            for stage, *args in schedule:
                if stage == "norm":
                    spread_rstd(NT * args[1])
                    x_ready = norm_ready(args[1])
                elif stage == "renorm":
                    spread_rstd(NT)
                    c.add(renorm=DC)
                    if args[2]:
                        ss_sum(NT)
                elif stage == "ffn":
                    ffn(args[2], args[5])
                elif stage == "even":
                    even()
                elif stage == "odd":
                    odd()
                elif stage == "out":
                    pairs_of(pe, c, 2, lambda i, s: pe_blocks(pe, c, i, s, DC, args[1], xh, xl, 2, 256))
                    ss_sum(args[1] // P)
                elif stage == "mamba":
                    mamba(args[0])
                elif stage == "attention":
                    attention(*args)
                elif stage == "branch":
                    branch(*args)
                elif stage == "wout":
                    pe.wait_ge(S("h_merged_lo"), args[0] + 1)
                    fm_pairs(2, DC, 2, 256)
                    ss_sum(NT)
                elif stage == "store":
                    pe.wait_ge(S("evac_done"), c.units + CREDIT)
                    if c.of["renorm"]:
                        pe.wait_ge(S("renormed"), c.of["renorm"])
                    for t in range(NT):
                        for k in range(DC):
                            ins = nc.tensor.transpose(ps[:, 2 * t + k // 4, (k % 4) * P:(k % 4 + 1) * P],
                                                      hT[:, k, t * P:(t + 1) * P], ident)
                        ins.then_inc(S("y_t"), 1)

        @block.scalar
        def _(act):
            c = Count()
            link = Link(act, "act_link")
            act.wait_ge(S("vec_ready"), 1)
            nc.scalar.activation(cond32[:, 0, :], V("c", 0, DC), ACT.Silu)
            nc.scalar.activation(cond32[:, 1, :], V("c_ctx", 0, DC), ACT.Silu).then_inc(S("cond32"), 1)
            act.wait_ge(S("cond32"), 1)
            nc.scalar.activation(cond_h[:, :, :], cond32[:, :, :].rearrange("p j k -> p k j"), ACT.Copy)\
                .then_inc(S("cond32"), 1)
            act_split(act, 0, 0, 0)
            def square(src, blk, slot, n):
                act.wait_ge(S("sq_added"), blk + (c.of["blocks"] + 1))
                nc.scalar.activation(sq2[:, slot:slot + 1, 0:n], src[:, bass.ds(blk, 1), 0:n], ACT.Square)\
                    .then_inc(S("sq_ready"), 1)

            def square_unit(src, i, s, per_unit, n):
                act.wait_ge(S("evac_done"), 2 * i + (c.units + s + 1 + CREDIT))
                for b in range(per_unit):
                    square(src, i * (2 * per_unit) + (s * per_unit + b), s if per_unit == 1 else b, n)

            for k in range(DC):
                act.wait_ge(S("h_in"), k + 1)
                square(hT, k, k % 2, 2 * T)
            c.add(blocks=DC)
            pairs_of(act, c, MOD_FIRST // 2, lambda i, s: None, ahead=act_split)
            act.wait_ge(S("bcast_mm"), 1)
            nc.scalar.activation(lam[:, 0:2], ps[:, 6, 0:2], ACT.Exp).then_inc(S("lam_exp"), 1)

            def root_of_sums(n_tiles):
                act.wait_ge(S("ss_mm"), c.of["norm"] + 1)
                nc.scalar.activation(root_col[:, 0:n_tiles], ps[:, 4, 0:n_tiles], ACT.Sqrt, bias=K("eps"), scale=1.0 / D)\
                    .then_inc(S("root_ready"), 1)

            def norm(src, nc_, shift, gain):
                o = c.of
                root_of_sums(NT * nc_)
                for k in range(DC):
                    for j in range(nc_):
                        e = o["norm_hi"] + k * nc_ + j
                        act.wait_ge(S("norm_prod"), e + 1)
                        sl = slice(j * T, (j + 1) * T)
                        nc.scalar.activation(xh[:, k, sl], normed[:, k, sl], ACT.Identity,
                                             bias=shift(k, j) if shift else 0.0).then_inc(S("norm_hi"), 1)
                c.add(norm=1, norm_hi=DC * nc_)

            def ffn(n_tok, final, mods, gate):
                for n, half in enumerate(HALVES):
                    def up(i, s):
                        unit_done(act, c, i, s, 0)
                        nc.scalar.activation(act32[:, s, 0:n_tok], ps[:, 2 * s, 0:n_tok], ACT.Silu)\
                            .then_inc(S("act_ready"), 1)
                        act.wait_ge(S("evac_done"), 2 * i + (c.units + s + 1 + CREDIT))
                        nc.scalar.activation(hid_h[:, bass.ds(i * 2 + (hid0 + s), 1), 0:n_tok],
                                             hid32[:, s:s + 1, 0:n_tok], ACT.Copy).then_inc(S("hid_h_ready"), 1)
                    hid0 = 0
                    for p0, pairs, _ in parts(half // 2, mods[2 * n]):
                        hid0 = 2 * p0
                        pairs_of(act, c, pairs, up, ahead=act_split)
                    c.hidden += half
                    for _, pairs, _ in parts(4, mods[2 * n + 1]):
                        dst = hT if gate else h_out
                        pairs_of(act, c, pairs, lambda i, s: n == 1 and square_unit(dst, i, s, 1, n_tok),
                                 ahead=act_split, final=final and n == 1)
                c.add(blocks=DC)


            def even():
                pairs_of(act, c, 2, lambda i, s: None, ahead=act_split)
                pairs_of(act, c, 3, lambda i, s: None, ahead=act_split)
                act.wait_ge(S("e_small_in"), 16)
                nc.scalar.activation(e_small_h[:, :, :], e_small[:, :, :], ACT.Copy).then_inc(S("e_small_hi"), 1)
                act.wait_ge(S("evac_done"), c.units + CREDIT)
                nc.scalar.activation(e_r[:, :, :], e_r[:, :, :], ACT.Silu).then_inc(S("e_silu"), 1)
                def logs(q):
                    for n in range(4):
                        act.wait_ge(S("e_logits"), 4 * q + n + 1)
                        link(nc.scalar.activation(e_log[:, n, :], ps[:, (0, 1, 4, 5)[n], 0:384], ACT.Abs))
                    link(nc.scalar.activation(e_log[:, :, :], e_log[:, :, :], ACT.Exp, scale=-1.0))
                    nc.scalar.activation(e_log[:, :, :], e_log[:, :, :], ACT.Ln, bias=1.0).then_inc(S("e_ln"), 1)

                def decays(q, n):
                    it = 4 * q + n
                    act.wait_ge(S("e_cum"), it + 1)
                    if it:
                        act.wait_ge(S("e_decayed"), it)
                    flat = ps[:, (2, 7)[n % 2], 0:384].rearrange("p (a b) -> p a b", b=P)
                    nc.scalar.activation(e_up[:, :, :], flat, ACT.Exp, scale=1.0 / 16)
                    nc.scalar.activation(e_dn[:, :, :], flat, ACT.Exp, scale=-1.0 / 16).then_inc(S("e_exp"), 1)

                logs(0)
                for q in range(2):
                    decays(q, 0)
                    for n in range(4):
                        it = 4 * q + n
                        if n < 3:
                            decays(q, n + 1)
                        act.wait_ge(S("e_kk_t"), it + 1)
                        if q and n == 0:
                            act.wait_ge(S("e_kv"), 8 * q)
                        nc.scalar.activation(e_kkT[:, n % 2, n // 2, :], ps[:, 3, 0:384], ACT.Copy)\
                            .then_inc(S("e_kkT"), 1)
                    if q == 0:
                        logs(1)
                    for p in range(3):
                        o = 3 * q + p
                        bank = (6, 0)[o % 2]
                        act.wait_ge(S("e_o"), o + 1)
                        if o:
                            act.wait_ge(S("e_oss"), o)
                        nc.scalar.activation(e_osq[:, :].rearrange("p (a b) -> p a b", a=2), ps[:, bank:bank + 2, 0:T], ACT.Square).then_inc(S("e_osq"), 1)
                        act.wait_ge(S("e_oss"), o + 1)
                        if o:
                            act.wait_ge(S("e_y"), o)
                        nc.scalar.activation(root[:, :], ps[:, 3, :], ACT.Sqrt, bias=K("eps"), scale=1.0 / P)\
                            .then_inc(S("e_oroot"), 1)
                        act.wait_ge(S("e_y"), o + 1)
                        sl = slice((1 - q) * T, (2 - q) * T)
                        nc.scalar.activation(xh[:, 2 + 2 * p:4 + 2 * p, sl],
                                             e_y[:, :].rearrange("p (a b) -> p a b", a=2), ACT.Copy)\
                            .then_inc(S("e_yh"), 1)
                act.wait_ge(S("e_yl"), 6)
                for n in range(4):
                    q, k = divmod(n, 2)
                    act.wait_ge(S("e_f1"), n + 1)
                    if n:
                        act.wait_ge(S("e_f2"), n)
                    nc.scalar.activation(e_ab, ps[:, 4, :].rearrange("p (a b) -> p a b", a=NT), ACT.Copy)\
                        .then_inc(S("e_fab"), 1)
                    act.wait_ge(S("e_f2"), n + 1)
                    nc.scalar.activation(xh[:, k, q * T:(q + 1) * T], ps[:, 5, 0:T], ACT.Copy)\
                        .then_inc(S("e_fh"), 1)

            def odd():
                pairs_of(act, c, 3, lambda i, s: None, ahead=act_split)
                pairs_of(act, c, 3, lambda i, s: None, ahead=act_split)
                def roots(p):
                    act.wait_ge(S("o_ss"), p + 1)
                    nc.scalar.activation(o_sq[:, 2 * p:2 * p + 2, :],
                                         ps[:, 4 + p, :].rearrange("p (a n) -> p a n", n=T),
                                         ACT.Sqrt, bias=K("eps"), scale=1.0 / P).then_inc(S("o_root"), 1)

                for e in range(14):
                    if e < 12:
                        act.wait_ge(S("o_max"), e + 1)
                        if e >= 2:
                            act.wait_ge(S("o_t"), e - 1)
                        for s in range(2):
                            ins = nc.scalar.activation(o_p[:, e % 2, s, :], ps[:, 4 + 2 * (e % 2) + s, :], ACT.Exp,
                                                       bias=o_st[:, e, s:s + 1], scale=HD ** -0.5,
                                                       accum_out=o_st[:, e, 2 + s:3 + s])
                        ins.then_inc(S("o_exp"), 1)
                    if 1 <= e <= 12:
                        a = e - 1
                        act.wait_ge(S("o_t"), a + 1)
                        if a >= 2:
                            act.wait_ge(S("o_pv"), a - 1)
                        nc.scalar.activation(o_aT[:, a % 2, :], ps[:, 2 + a % 2, :], ACT.Copy).then_inc(S("o_aT"), 1)
                        if e == 12:
                            for p in range(2):
                                roots(p)
                    if e >= 2 and e % 2 == 1:
                        h = (e - 3) // 2
                        act.wait_ge(S("o_pv"), 2 * h + 2)
                        nc.scalar.activation(o_o[:, h, :], ps[:, h % 2, 0:T], ACT.Copy).then_inc(S("o_out"), 1)
                        if h % 2:
                            act.wait_ge(S("o_out"), h + 1)
                            nc.scalar.activation(o_sq[:, h - 1:h + 1, :], o_o[:, h - 1:h + 1, :], ACT.Square)\
                                .then_inc(S("o_sq"), 1)
                roots(2)
                act.wait_ge(S("o_conv"), 2)
                nc.scalar.activation(xh[:, 0:2, 0:T], o_c[:, :, :], ACT.Copy).then_inc(S("o_yh"), 1)
                act.wait_ge(S("o_y"), 1)
                nc.scalar.activation(xh[:, 2:8, 0:T], o_o[:, :, :], ACT.Copy).then_inc(S("o_yh"), 1)

            def beside_act(beside, layer, n, splits, reads):
                for j, h in splits:
                    act_split(act, j // 2, j % 2, c.units + j % 2, (h,))
                for j in reads:
                    kind, i = beside.units[j]
                    unit_done(act, c, j // 2, j % 2)
                    both = ps[:, j % 2, :].rearrange("p (a b) -> p a b", a=2)
                    if kind == "qk":
                        ins = nc.scalar.activation(qk_set[n % 2][:, 2 * i:2 * i + 2, :], both, ACT.Copy)
                    elif kind == "v":
                        ins = nc.scalar.activation(v_set[n % 2][:, :, i * 256:(i + 1) * 256], both, ACT.Copy)
                    elif kind == "iq":
                        ins = nc.scalar.activation(a_iq[:, i, :], ps[:, j % 2, 0:T], ACT.Copy)
                    else:
                        if n >= 2:
                            act.wait_ge(S("h_merged"), 6 * layer + 2 * (n - 1))
                        for b in range(2):
                            ins = nc.scalar.activation(h_gates[:, 2 * i + b, :], both[:, b, :], ACT.Identity,
                                                       bias=V("b_gate_2", 32 * layer + DC * n + 2 * i + b))
                    ins.then_inc(S("evac_done"), 1)

            def gates(beside):
                c.units += len(beside.units)
                act.wait_ge(S("evac_done"), c.units + CREDIT)
                nc.scalar.activation(h_gates[:, :, :], h_gates[:, :, :], ACT.Sigmoid).then_inc(S("h_gate"), 1)

            def branch(layer, n):
                pairs_of(act, c, 1, lambda i, s: None, ahead=act_split)

            def mamba(layer):
                beside = Beside(0, MAMBA_PLACES)
                places = lambda lo, hi: beside_act(beside, layer, 0, beside.splits(lo, hi), beside.reads(lo - 1, hi - 1))
                pairs_of(act, c, 3, lambda i, s: None, ahead=act_split)
                act.wait_ge(S("m_sw_in"), 48 * (layer + 1))
                nc.scalar.activation(m_sw_h[:, :, :], m_sw[:, :, :], ACT.Copy).then_inc(S("m_sw_hi"), 1)
                act.wait_ge(S("evac_done"), c.units + CREDIT)
                places(0, 1)
                act.wait_ge(S("m_dt"), 3 * layer + 1)
                link(nc.scalar.activation(m_dt[:, 1, :], m_dt[:, 0, :], ACT.Abs))
                nc.scalar.activation(m_dt[:, 1, :], m_dt[:, 1, :], ACT.Exp, scale=-1.0).then_inc(S("m_dt_act"), 1)
                nc.scalar.activation(m_dt[:, 5, 0:8], bcast[:, 16 + 8 * layer:24 + 8 * layer], ACT.Exp)
                act.wait_ge(S("m_dt"), 3 * layer + 2)
                nc.scalar.activation(m_dt[:, 3, :], m_dt[:, 2, :], ACT.Ln).then_inc(S("m_dt_act"), 1)
                places(1, 2)
                nc.scalar.activation(m_in[:, 0:4, :], m_in[:, 0:4, :], ACT.Silu)
                for half in range(2):
                    act.wait_ge(S("m_taps"), 2 * layer + half + 1)
                    x = m_cv[:, 4 * half:4 * half + 4, :]
                    nc.scalar.activation(x, x, ACT.Silu).then_inc(S("m_conv"), 1)
                act.wait_ge(S("m_x_t"), layer + 1)
                nc.scalar.activation(m_x[:, :, :], ps[:, 4:6, :], ACT.Copy).then_inc(S("m_x"), 1)
                for h in range(8):
                    act.wait_ge(S("m_seg"), 8 * layer + h + 1)
                    nc.scalar.activation(m_e[:, h % 2, :], m_e[:, h % 2, :], ACT.Exp).then_inc(S("m_exp"), 1)
                    places(2 + h, 3 + h)
                places(10, 11)
                act.wait_ge(S("m_gated"), layer + 1)
                nc.scalar.activation(m_sq[:, :, :], m_y[:, :, :], ACT.Square).then_inc(S("m_sq"), 1)
                act.wait_ge(S("m_ss"), layer + 1)
                nc.scalar.activation(root[:, :].rearrange("p (a b) -> p a b", a=2), ps[:, 2:4, 0:T], ACT.Sqrt,
                                     bias=K("eps"), scale=1.0 / T).then_inc(S("m_root"), 1)
                places(11, 15)
                act.wait_ge(S("m_normed"), layer + 1)
                nc.scalar.activation(h_yh[:, :, :], m_y[:, :, :], ACT.Copy).then_inc(S("m_yh"), 1)
                gates(beside)

            def attention(layer, which):
                a = 3 * layer + which
                n = which + 1
                beside = Beside(n, places_of(n))
                act.wait_ge(S("evac_done"), c.units + CREDIT)
                if which == 2:
                    beside_act(beside, layer, n, beside.splits(0, 1), [])
                    for place in range(1, 4):
                        beside_act(beside, layer, n, beside.splits(place, place + 1), beside.reads(place - 1, place))
                    beside_act(beside, layer, n, beside.splits(4, 8), beside.reads(3, 4))
                if which == 0:
                    act.wait_ge(S("a_f"), 2 * layer + 1)
                    link(nc.scalar.activation(a_f[:, 1, :], a_f[:, 0, :], ACT.Abs))
                    link(nc.scalar.activation(a_f[:, 1, :], a_f[:, 1, :], ACT.Exp, scale=-1.0))
                    nc.scalar.activation(a_f[:, 1, :], a_f[:, 1, :], ACT.Ln, bias=1.0).then_inc(S("a_f_ln"), 1)
                def exponentials(e):
                    nk = (e % 2 + 1) * P
                    act.wait_ge(S("a_max"), 16 * a + e + 1)
                    nc.scalar.activation(a_p[:, e % 2, 0:nk], a_p[:, e % 2, 0:nk], ACT.Exp, bias=a_st[:, e, 0:1],
                                         accum_out=a_st[:, e, 1:2]).then_inc(S("a_exp"), 1)

                exponentials(0)
                for e in range(18):
                    if e >= 4 and e % 4 == 0:
                        p = (e - 4) // 4
                        act.wait_ge(S("a_pv"), 16 * a + 4 * p + 4)
                        nc.scalar.activation(h_yh[:, p, :], ps[:, 2 + p % 2, 0:T], ACT.Copy).then_inc(S("a_yh"), 1)
                    if which < 2:
                        beside_act(beside, layer, n, beside.splits(2 * e, 2 * e + 2), beside.reads(2 * e - 2, 2 * e - 1))
                    if e < 16:
                        nk = (e % 2 + 1) * P
                        act.wait_ge(S("a_t"), 16 * a + e + 1)
                        if e >= 2:
                            act.wait_ge(S("a_pv"), 16 * a + e - 1)
                        nc.scalar.activation(a_pT[:, e % 2, 0:nk], ps[:, 6, 0:nk], ACT.Copy).then_inc(S("a_pT"), 1)
                    if which < 2:
                        beside_act(beside, layer, n, [], beside.reads(2 * e - 1, 2 * e))
                    if e + 1 < 16:
                        exponentials(e + 1)
                gates(beside)

            def merged(layer):
                act.wait_ge(S("h_merged"), 6 * (layer + 1))
                act.wait_ge(S("mm_done"), 2 * c.units + HALF_CREDIT)
                nc.scalar.activation(xh[:, :, 0:T], h_merged, ACT.Copy).then_inc(S("h_merged_hi"), 1)

            for stage, *args in schedule:
                if stage == "norm":
                    norm(*args)
                elif stage == "renorm":
                    root_of_sums(NT)
                    for k in range(DC * args[2]):
                        act.wait_ge(S("renormed"), c.of["renorm"] + k + 1)
                        square(hT, k, k % 2, T)
                    c.add(norm=1, renorm=DC, blocks=DC * args[2])
                elif stage == "ffn":
                    ffn(args[2], args[4], args[5], args[3])
                elif stage == "even":
                    even()
                elif stage == "odd":
                    odd()
                elif stage == "out":
                    pairs_of(act, c, 2, lambda i, s: square_unit(hT, i, s, 2, args[1]), ahead=act_split)
                    c.add(blocks=DC)
                elif stage == "mamba":
                    mamba(args[0])
                elif stage == "attention":
                    attention(*args)
                elif stage == "branch":
                    branch(*args)
                elif stage == "wout":
                    merged(args[0])
                    pairs_of(act, c, 2, lambda i, s: square_unit(h_out, i, s, 2, T), ahead=act_split)
                    c.add(blocks=DC)

        @block.gpsimd
        def _(pool):
            pool.wait_ge(S("cond32"), 1)
            pool.sem_inc(S("mod_sum1"), POOL_STEPS * MOD_FIRST)

            def mod_unit(layer, m0, i, s):
                step = mod_step(POOL_STEPS, layer, m0, i, s)
                acc = mod_acc[:, s, 2 * P:4 * P]
                pool.wait_ge(S(f"mod_landed{s}"), 16 * i + mod_landings(layer, m0))
                pool.wait_ge(S("mod_mm"), 2 * i + (MOD_UNITS * layer + m0 + s - 1))
                for k in range(DC):
                    if k == 1:
                        pool.wait_ge(S("mod_sum1"), step)
                    nc.gpsimd.tensor_tensor(acc if k == 0 else mod_prod[:, k % 2, :], mod_w[:, s, k, :],
                                            cond32[:, 1, k:k + 1].to_broadcast([P, 2 * P]), ALU.mult)\
                        .then_inc(S("mod_sum1"), 1)
                    if k:
                        pool.wait_ge(S("mod_sum1"), step + 2 * k)
                        nc.gpsimd.tensor_tensor(acc, acc, mod_prod[:, k % 2, :], ALU.add).then_inc(S("mod_sum1"), 1)

            for stage, *args in schedule:
                if stage == "ffn":
                    for mod_part in args[5]:
                        if mod_part:
                            layer, m0, pairs = mod_part
                            with pool.Fori(0, pairs) as i:
                                for s in range(2):
                                    mod_unit(layer, m0, i, s)

        @block.vector
        def _(dve):
            c = Count()
            link = Link(dve, "dve_link")
            dve.sem_inc(S("lo_ready"), HALF_CREDIT)
            dve.sem_inc(S("evac_done"), CREDIT)
            dve.sem_inc(S("hid_l_ready"), CREDIT)
            dve.sem_inc(S("sq_added"), CREDIT)
            dve.wait_ge(S("vec_t"), 1)
            nc.vector.tensor_copy(vec[:, 0:n_rows], ps[:, 7, 0:n_rows]).then_inc(S("vec_ready"), 1)
            for k in range(DC):
                dve.wait_ge(S("h_t"), k + 1)
                nc.vector.tensor_copy(hT[:, k, :], ps[:, k, :]).then_inc(S("h_in"), 1)
            dve.wait_ge(S("cond32"), 2)
            nc.vector.tensor_tensor(cond_l[:, :, :], cond32[:, :, :].rearrange("p j k -> p k j"),
                                    cond_h[:, :, :].bitcast(F32), ALU.subtract).then_inc(S("cond_lo"), 1)

            def sq_open():
                link(nc.vector.memset(ss[:, :], 0.0))

            def sq_add(blk, slot, n):
                n_done = blk + (c.of["blocks"] + CREDIT)
                dve.wait_ge(S("sq_ready"), blk + (c.of["blocks"] + 1))
                dve.wait_ge(S("sq_added"), n_done)
                nc.vector.tensor_tensor(ss[:, 0:n], ss[:, 0:n], sq2[:, slot, 0:n], ALU.add).then_inc(S("sq_added"), 1)

            def sq_lag(i, s, per_unit, n):
                if is_first(i, s):
                    sq_open()
                else:
                    for b in range(per_unit):
                        sq_add(i * (2 * per_unit) + ((s - 1) * per_unit + b), (1 - s) if per_unit == 1 else b, n)

            def sq_close(per_unit, n):
                for b in range(per_unit):
                    sq_add(DC - per_unit + b, 1 if per_unit == 1 else b, n)
                c.add(blocks=DC)

            def sq_all(n):
                sq_open()
                for k in range(DC):
                    sq_add(k, k % 2, n)
                c.add(blocks=DC)

            sq_all(2 * T)
            def mod_bias(at, bank, n=2):
                return nc.vector.tensor_tensor(mod[:, bass.ds(at, n), :], ps[:, bank, 0:2 * n].rearrange("p (a j) -> p a j", j=2),
                                               vec[:, bass.ds(at + vec_at["ada_b"], n)].unsqueeze(2).to_broadcast([P, n, 2]),
                                               ALU.add)

            def mod_first(i, s):
                unit_done(dve, c, i, s)
                nc.vector.tensor_copy(mod_rows[:, bass.ds(i * (4 * P) + 2 * P * s, 2 * P)], ps[0:2, 2 * s, 0:2 * P])\
                    .then_inc(S("evac_done"), 1)
            dve_split(dve, 0, 0, 0)
            pairs_of(dve, c, MOD_FIRST // 2, mod_first, ahead=dve_split)
            dve.wait_ge(S("mod_mm"), MOD_FIRST)
            mod_bias(0, 5, 2 * MOD_FIRST).then_inc(S("mod_evac"), MOD_FIRST)
            dve.wait_ge(S("lam_landed"), 16 * 8)
            for j in range(2):
                ins = nc.vector.tensor_tensor(lam_prod[:, j:j + 1], lam_in[:, 2 * j:2 * j + 1],
                                              lam_in[:, 2 * j + 1:2 * j + 2], ALU.mult)
            ins.then_inc(S("lam_prod"), 1)
            dve.wait_ge(S("lam_exp"), 1)
            link(nc.vector.tensor_tensor(lam[:, 2:3], lam[:, 1:2], lam[:, 0:1], ALU.subtract))
            link(nc.vector.tensor_scalar(lam[:, 2:3], lam[:, 2:3], -LAM_INIT, None, ALU.add))
            dve.wait_ge(S("bcast_mm"), 1)
            nc.vector.tensor_copy(bcast[:, :], ps[:, 6, 64:128]).then_inc(S("bcast_ready"), 1)

            dve.sem_inc(S("mod_sum0"), DVE_STEPS * MOD_FIRST)

            def mod_unit(layer, m0):
                def multiply(i, s):
                    step = mod_step(DVE_STEPS, layer, m0, i, s)
                    acc = mod_acc[:, s, 0:2 * P]
                    dve.wait_ge(S(f"mod_landed{s}"), 16 * i + mod_landings(layer, m0))
                    dve.wait_ge(S("mod_mm"), 2 * i + (MOD_UNITS * layer + m0 + s - 1))
                    for k in range(DC):
                        if k == 0:
                            ins = nc.vector.tensor_scalar(acc, mod_w[:, s, k, :], cond32[:, 0, k:k + 1], None, ALU.mult)
                        else:
                            dve.wait_ge(S("mod_sum0"), step + k)
                            ins = nc.vector.scalar_tensor_tensor(out=acc, in0=mod_w[:, s, k, :],
                                                                 scalar=cond32[:, 0, k:k + 1], in1=acc,
                                                                 op0=ALU.mult, op1=ALU.add)
                        ins.then_inc(S("mod_sum0"), 1)
                return multiply

            def mod_read(layer, m0):
                def read(i, s):
                    dve.wait_ge(S("mod_mm"), 2 * i + (MOD_UNITS * layer + m0 + s + 1))
                    mod_bias(i * 4 + (8 * N_MOD * layer + 2 * (m0 + s)), 6 + s).then_inc(S("mod_evac"), 1)
                return read

            def mod_blocks(layer, n, b):
                dve.wait_ge(S("mod_evac"), MOD_UNITS * layer + 4 * (3 * n + b) + 4)
                at = 8 * N_MOD * layer + 24 * n + 8 * b
                return mod[:, at:at + 8, :]

            def norm_gains(layer, n, name):
                scale = mod_blocks(layer, n, 1)
                for j in range(2):
                    link(nc.vector.scalar_tensor_tensor(out=gains[:, layer, n, :, j], in0=scale[:, :, j], scalar=1.0,
                                                        in1=V(name, DC * layer, DC), op0=ALU.add, op1=ALU.mult))

            def rstd_of_root(n_tiles):
                dve.wait_ge(S("root_ready"), c.of["norm"] + 1)
                nc.vector.reciprocal(rstd_col[:, 0:n_tiles], root_col[:, 0:n_tiles]).then_inc(S("rstd_col"), 1)
                dve.wait_ge(S("rstd_mm"), c.of["norm"] + 1)

            def norm(src, nc_, gain, shift):
                rstd_of_root(NT * nc_)
                e0 = c.of["norm_hi"]
                pieces = [(k, j) for k in range(DC) for j in range(nc_)]
                def low(e):
                    k, j = pieces[e]
                    sl = slice(j * T, (j + 1) * T)
                    dve.wait_ge(S("norm_hi"), e0 + e + 1)
                    nc.vector.scalar_tensor_tensor(out=xl[:, k, sl], in0=normed[:, k, sl],
                                                   scalar=shift(k, j) if shift else 0.0,
                                                   in1=xh[:, k, sl].bitcast(F32), op0=ALU.add,
                                                   op1=ALU.subtract).then_inc(S("norm_lo"), 1)
                for e, (k, j) in enumerate(pieces):
                    sl = slice(j * T, (j + 1) * T)
                    nc.vector.scalar_tensor_tensor(out=normed[:, k, sl], in0=src[:, k, sl], scalar=gain(k, j),
                                                   in1=ps[:, 5, sl], op0=ALU.mult, op1=ALU.mult)\
                        .then_inc(S("norm_prod"), 1)
                    if e >= 2:
                        low(e - 2)
                for e in (len(pieces) - 2, len(pieces) - 1):
                    low(e)
                c.add(norm=1, norm_hi=DC * nc_)

            def ffn(n_tok, final, mods, gate):
                for n, half in enumerate(HALVES):
                    a0 = c.hidden
                    def up(i, s):
                        a = 2 * i + (a0 + hid0 + s)
                        dve.wait_ge(S("act_ready"), a + 1)
                        dve.wait_ge(S("hid_l_ready"), a + 1)
                        unit_done(dve, c, i, s)
                        nc.vector.tensor_tensor(hid32[:, s, 0:n_tok], act32[:, s, 0:n_tok],
                                                ps[:, 2 * s + 1, 0:n_tok], ALU.mult).then_inc(S("evac_done"), 1)
                        dve.wait_ge(S("hid_h_ready"), a + 1)
                        to = bass.ds(i * 2 + (hid0 + s), 1)
                        nc.vector.tensor_tensor(hid_l[:, to, 0:n_tok], hid32[:, s:s + 1, 0:n_tok],
                                                hid_h[:, to, 0:n_tok].bitcast(F32), ALU.subtract)\
                            .then_inc(S("hid_l_ready"), 1)
                    hid0 = 0
                    for p0, pairs, mod_part in parts(half // 2, mods[2 * n]):
                        hid0 = 2 * p0
                        beside = mod_part and mod_read(*mod_part)
                        pairs_of(dve, c, pairs, lambda i, s: (up(i, s), beside and beside(i, s)), ahead=dve_split,
                                 before=mod_part and mod_unit(*mod_part))
                    c.hidden += half
                    if gate and n == 0:
                        g = mod_blocks(gate[0], gate[1], 2)
                        link(nc.vector.tensor_scalar(g, g, 0.5, None, ALU.mult))
                    for p0, pairs, mod_part in parts(4, mods[2 * n + 1]):
                        beside = mod_part and mod_read(*mod_part)
                        add = add_gated(gate, n_tok // T, 2 * p0) if gate else add_plain(n, 2 * p0)
                        def down(i, s):
                            unit_done(dve, c, i, s)
                            add(i, s)
                            if n == 1:
                                sq_lag(i, s, 1, n_tok)
                            if beside:
                                beside(i, s)
                        pairs_of(dve, c, pairs, down, ahead=dve_split, final=final and n == 1, first=n == 1,
                                 before=mod_part and mod_unit(*mod_part))
                sq_close(1, n_tok)

            def add_gated(gate, nc_, n0):
                gate0 = 8 * N_MOD * gate[0] + 24 * gate[1] + 16
                def add(i, s):
                    to = bass.ds(i * 2 + (n0 + s), 1)
                    for j in range(nc_):
                        sl = slice(j * T, (j + 1) * T)
                        ins = nc.vector.scalar_tensor_tensor(
                            out=hT[:, to, sl], in0=ps[:, 2 * s:2 * s + 1, sl],
                            scalar=mod[:, bass.ds(i * 2 + (gate0 + n0 + s), 1), j], in1=hT[:, to, sl],
                            op0=ALU.mult, op1=ALU.add)
                    ins.then_inc(S("evac_done"), 1)
                return add


            def even():
                link(nc.vector.memset(e_gw[:, :, :], 0.0))
                nc.vector.memset(e_gT[32:33, :], 1.0).then_inc(S("e_gw_zero"), 1)
                nc.vector.memset(e_S[:, :, 0, :, :], 0.0)
                def to_z(i, s):
                    fm_evac(e_z, 0, 2 * T)(dve, c, i, s)
                pairs_of(dve, c, 2, to_z, ahead=dve_split)
                def r_and_v(i, s):
                    unit_done(dve, c, i, s)
                    if s == 0:
                        nc.vector.tensor_copy(e_r[:, bass.ds(i * 2, 2), :], ps[:, 0:2, :]).then_inc(S("evac_done"), 1)
                    else:
                        nc.vector.tensor_copy(e_v[:, :, bass.ds(i * 256, 256)],
                                              ps[:, 2:4, :].rearrange("p a (b n) -> p (a b) n", n=256))\
                            .then_inc(S("evac_done"), 1)
                pairs_of(dve, c, 3, r_and_v, ahead=dve_split)
                dve.wait_ge(S("e_small_hi"), 1)
                nc.vector.tensor_tensor(e_small_l[:, :, :], e_small[:, :, :], e_small_h[:, :, :].bitcast(F32),
                                        ALU.subtract).then_inc(S("e_small_lo"), 1)
                dve.wait_ge(S("e_gates_mm"), 1)
                nc.vector.tensor_copy(e_gT[0:32, :], ps[0:32, 6, :]).then_inc(S("e_gT"), 1)
                nc.vector.memset(e_att[:, :, :], 0.0)
                def logs(q):
                    dve.wait_ge(S("e_ln"), q + 1)
                    for n in range(4):
                        nc.vector.scalar_tensor_tensor(out=e_log[:, n, :], in0=ps[:, (0, 1, 4, 5)[n], 0:384], scalar=0.0,
                                                       in1=e_log[:, n, :], op0=ALU.min, op1=ALU.subtract)\
                            .then_inc(S("e_log"), 1)

                def att(o):
                    dve.wait_ge(S("e_att_mm"), o + 1)
                    if o:
                        dve.wait_ge(S("e_o"), o)
                    for dr in range(2):
                        mask = K(("cum_fwd", "cum_bwd")[dr]).bitcast(U32)
                        cols = slice(2 * dr * P, 2 * dr * P + 2 * P)
                        for h in range(2):
                            ins = nc.vector.copy_predicated(
                                e_att[:, h, cols].rearrange("p (a b) -> p a b", b=P),
                                mask.unsqueeze(1).to_broadcast([P, 2, P]),
                                ps[:, 4 + h, cols].rearrange("p (a b) -> p a b", b=P))
                    ins.then_inc(S("e_att"), 1)

                logs(0)
                for q in range(2):
                    for n in range(4):
                        it, tile, dr = 4 * q + n, n // 2, n % 2
                        tt = slice((1 - q) * T + tile * P, (1 - q) * T + (tile + 1) * P)
                        t0 = slice(tile * P, (tile + 1) * P)
                        dve.wait_ge(S("e_exp"), it + 1)
                        if q and n == 0:
                            dve.wait_ge(S("e_o"), 3 * q)
                        kd, qd = e_keys(dr, q)
                        edge = e_up[:, :, 63:128:64] if dr == 0 else e_up[:, :, 0:128:64]
                        link(nc.vector.tensor_copy(e_last[:, dr, tile, :, :], edge))
                        nc.vector.scalar_tensor_tensor(out=qd[:, :, t0], in0=e_z[:, 2:5, tt], scalar=0.125,
                                                       in1=e_up[:, :, :], op0=ALU.mult, op1=ALU.mult)
                        link(nc.vector.tensor_tensor(kd[:, :, t0], e_z[:, 5:8, tt], e_dn[:, :, :], ALU.mult))
                        if it:
                            dve.wait_ge(S("e_kk_t"), it)
                        nc.vector.tensor_tensor(
                            e_kk[:, :, :].rearrange("p a (b n) -> p (a b) n", n=64),
                            kd[:, :, t0].rearrange("p a (b n) -> p a b n", n=64).rearrange("p a b n -> p a b n"),
                            e_last[:, dr, tile, :, :].unsqueeze(3).to_broadcast([P, 3, 2, 64]), ALU.mult)\
                            .then_inc(S("e_decayed"), 1)
                    if q:
                        link(nc.vector.tensor_copy(e_S[:, :, 0, :, :], e_S[:, :, 4, :, :]))
                    for step in range(8):
                        dr, n = step % 2, step // 2
                        ch = n if dr == 0 else 3 - n
                        if q == 0 and step == 4:
                            logs(1)
                        dve.wait_ge(S("e_kv"), 8 * q + step + 1)
                        if step >= 2:
                            dve.wait_ge(S("e_state"), 8 * q + step - 1)
                        for p in range(3):
                            ins = nc.vector.scalar_tensor_tensor(
                                out=e_S[:, dr, n + 1, p, :], in0=e_S[:, dr, n, p, :],
                                scalar=e_last[:, dr, ch // 2, p, ch % 2:ch % 2 + 1],
                                in1=ps[:, (6, 2)[dr], p * P:(p + 1) * P], op0=ALU.mult, op1=ALU.add)
                        ins.then_inc(S("e_state"), 1)
                    att(3 * q)
                    for p in range(3):
                        o = 3 * q + p
                        bank = (6, 0)[o % 2]
                        if p < 2:
                            att(o + 1)
                        dve.wait_ge(S("e_oroot"), o + 1)
                        y2 = e_y[:, :].rearrange("p (a b) -> p a b", a=2)
                        link(nc.vector.reciprocal(rstd[:, :], root[:, :]))
                        if o:
                            dve.wait_ge(S("e_yl"), o)
                        link(nc.vector.scalar_tensor_tensor(out=y2, in0=ps[:, bank:bank + 2, 0:T], scalar=V("gla_norm"),
                                                            in1=rstd[:, :].rearrange("p (a b) -> p a b", a=2), op0=ALU.mult, op1=ALU.mult))
                        sl = slice((1 - q) * T, (2 - q) * T)
                        if o == 0:
                            dve.wait_ge(S("e_silu"), 1)
                        nc.vector.tensor_tensor(y2, y2, e_r[:, 2 * p:2 * p + 2, sl], ALU.mult).then_inc(S("e_y"), 1)
                        dve.wait_ge(S("e_yh"), o + 1)
                        nc.vector.tensor_tensor(xl[:, 2 + 2 * p:4 + 2 * p, sl], y2,
                                                xh[:, 2 + 2 * p:4 + 2 * p, sl].bitcast(F32), ALU.subtract)\
                            .then_inc(S("e_yl"), 1)
                for n in range(4):
                    q, k = divmod(n, 2)
                    dve.wait_ge(S("e_fh"), n + 1)
                    sl = slice(q * T, (q + 1) * T)
                    nc.vector.tensor_tensor(xl[:, k, sl], ps[:, 5, 0:T], xh[:, k, sl].bitcast(F32), ALU.subtract)\
                        .then_inc(S("e_fl"), 1)

            def odd():
                def first(i, s):
                    unit_done(dve, c, i, s)
                    nc.vector.tensor_copy((o_z, o_q)[s][:, bass.ds(i * 2, 2), :], ps[:, 2 * s:2 * s + 2, 0:T])\
                        .then_inc(S("evac_done"), 1)
                pairs_of(dve, c, 3, first, ahead=dve_split)
                def k_and_v(i, s):
                    unit_done(dve, c, i, s)
                    if s == 0:
                        nc.vector.tensor_copy(o_k[:, bass.ds(i * 2, 2), :], ps[:, 0:2, :]).then_inc(S("evac_done"), 1)
                    else:
                        nc.vector.tensor_copy(o_v[:, :, bass.ds(i * 256, 256)],
                                              ps[:, 2:4, :].rearrange("p a (b n) -> p (a b) n", n=256))\
                            .then_inc(S("evac_done"), 1)
                pairs_of(dve, c, 3, k_and_v, ahead=dve_split)
                dve.wait_ge(S("evac_done"), c.units + CREDIT)
                cos = K("axial_cos").unsqueeze(1).to_broadcast([P, 2, T])
                sin = K("axial_sin").unsqueeze(1).to_broadcast([P, 2, T])
                for n in range(6):
                    buf, k = (o_q, 2 * n) if n < 3 else (o_k, 2 * n - 6)
                    x = buf[:, k:k + 2, 0:T]
                    dve.wait_ge(S("o_swap"), n + 1)
                    if n:
                        dve.wait_ge(S("o_turned"), n)
                    nc.vector.tensor_tensor(o_turn[:, :, :], ps[:, n, :].rearrange("p (a b) -> p a b", a=2), sin, ALU.mult)
                    link(nc.vector.tensor_tensor(x, x, cos, ALU.mult))
                    nc.vector.tensor_tensor(x, x, o_turn[:, :, :], ALU.add).then_inc(S("o_turned"), 1)

                def probs(e):
                    st = o_st[:, e, :]
                    dve.wait_ge(S("o_exp"), e + 1)
                    link(nc.vector.reciprocal(st[:, 4:6], st[:, 2:4]))
                    nc.vector.tensor_scalar(o_p[:, e % 2, 0, :], o_p[:, e % 2, 0, :], st[:, 4:5], None, ALU.mult)
                    link(nc.vector.tensor_tensor(st[:, 5:6], st[:, 5:6], lam[:, 2:3], ALU.mult))
                    nc.vector.scalar_tensor_tensor(out=o_p[:, e % 2, 0, :], in0=o_p[:, e % 2, 1, :], scalar=st[:, 5:6],
                                                   in1=o_p[:, e % 2, 0, :], op0=ALU.mult, op1=ALU.add)\
                        .then_inc(S("o_a"), 1)

                def maxima(e):
                    dve.wait_ge(S("o_scores"), e + 1)
                    b = 4 + 2 * (e % 2)
                    link(nc.vector.tensor_reduce(o_st[:, e, 0:2], ps[:, b:b + 2, :], AX.X, ALU.max, negate=True))
                    nc.vector.tensor_scalar(o_st[:, e, 0:2], o_st[:, e, 0:2], HD ** -0.5, None, ALU.mult)\
                        .then_inc(S("o_max"), 1)

                def taps(b):
                    link(nc.vector.tensor_scalar(o_c[:, b, :], o_u[:, b, 0:T], V("conv_w", b), V("conv_b", b),
                                                 ALU.mult, ALU.add))
                    for tap in (1, 2):
                        link(nc.vector.scalar_tensor_tensor(out=o_c[:, b, :], in0=o_u[:, b, tap:tap + T],
                                                            scalar=V("conv_w", 2 * tap + b), in1=o_c[:, b, :],
                                                            op0=ALU.mult, op1=ALU.add))
                    nc.vector.tensor_tensor(o_c[:, b, :], o_c[:, b, :], o_z[:, b, :], ALU.mult).then_inc(S("o_conv"), 1)

                maxima(0)
                for e in range(12):
                    probs(e)
                    if e + 1 < 12:
                        maxima(e + 1)
                    if e == 3:
                        link(nc.vector.memset(o_u[:, :, :], 0.0))
                        link(nc.vector.tensor_tensor(o_u[:, :, 1:T + 1], o_z[:, 2:4, :], o_z[:, 4:6, :], ALU.mult))
                    elif e in (5, 7):
                        taps((e - 5) // 2)
                link(nc.vector.tensor_scalar(lam[:, 3:4], V("diff_norm"), 1.0 - LAM_INIT, None, ALU.mult))
                for p in range(3):
                    hh = slice(2 * p, 2 * p + 2)
                    dve.wait_ge(S("o_root"), p + 1)
                    link(nc.vector.reciprocal(o_sq[:, hh, :], o_sq[:, hh, :]))
                    ins = nc.vector.scalar_tensor_tensor(out=o_o[:, hh, :], in0=o_o[:, hh, :], scalar=lam[:, 3:4],
                                                         in1=o_sq[:, hh, :], op0=ALU.mult, op1=ALU.mult)
                ins.then_inc(S("o_y"), 1)
                for n, (c0, buf) in enumerate(((0, o_c), (2, o_o))):
                    dve.wait_ge(S("o_yh"), n + 1)
                    k = buf.shape[1]
                    nc.vector.tensor_tensor(xl[:, c0:c0 + k, 0:T], buf[:, :, :],
                                            xh[:, c0:c0 + k, 0:T].bitcast(F32), ALU.subtract).then_inc(S("o_yl"), 1)

            def beside_dve(splits):
                for j, h in splits:
                    dve_split(dve, j // 2, j % 2, c.units + j % 2, (h,))

            def mamba(layer):
                pairs_of(dve, c, 3, lambda i, s: fm_evac(m_in, 0, T)(dve, c, i, s), ahead=dve_split)
                beside = Beside(0, MAMBA_PLACES)
                dve.wait_ge(S("m_sw_hi"), layer + 1)
                nc.vector.tensor_tensor(m_sw_l[:, :, :], m_sw[:, :, :], m_sw_h[:, :, :].bitcast(F32), ALU.subtract)\
                    .then_inc(S("m_sw_lo"), 1)
                dve.wait_ge(S("evac_done"), c.units + CREDIT)
                early, late = beside.splits(0, 1), beside.splits(1, 2)
                beside_dve(early[:2])
                def conv(k):
                    w = lambda tap: V("conv_w_2", 32 * layer + 8 * tap + k)
                    link(nc.vector.tensor_scalar(m_cv[:, k, :], m_in[:, 4 + k, :], w(3),
                                                 V("conv_b_2", 8 * layer + k), ALU.mult, ALU.add))
                    for back in (1, 2, 3):
                        ins = nc.vector.scalar_tensor_tensor(out=m_cv[:, k, back:T], in0=m_in[:, 4 + k, 0:T - back],
                                                             scalar=w(3 - back), in1=m_cv[:, k, back:T],
                                                             op0=ALU.mult, op1=ALU.add)
                        if k % 4 == 3 and back == 3:
                            ins.then_inc(S("m_taps"), 1)
                        else:
                            link(ins)

                for k in range(4):
                    conv(k)
                dve.wait_ge(S("m_small_mm"), layer + 1)
                nc.vector.tensor_copy(h_small[:, :, :].rearrange("p a b -> p (a b)"), ps[:, 5, 0:NT * 84])\
                    .then_inc(S("m_small"), 1)
                dve.wait_ge(S("m_small"), layer + 1)
                for t in range(NT):
                    ins = nc.vector.tensor_tensor(m_dt[:, 0, 8 * t:8 * t + 8], h_small[:, t, 0:8],
                                                  bcast[:, 8 * layer:8 * layer + 8], ALU.add)
                ins.then_inc(S("m_dt"), 1)
                dve.wait_ge(S("m_dt_act"), 2 * layer + 1)
                nc.vector.tensor_scalar(m_dt[:, 2, :], m_dt[:, 1, :], 1.0, None, ALU.add).then_inc(S("m_dt"), 1)
                dve.wait_ge(S("m_dt"), 3 * layer + 2)
                link(nc.vector.tensor_scalar(m_dt[:, 4, :], m_dt[:, 2, :], -1.0, None, ALU.add))
                link(nc.vector.tensor_tensor(m_dt[:, 1, :], m_dt[:, 1, :], m_dt[:, 4, :], ALU.subtract))
                link(nc.vector.reciprocal(m_dt[:, 4, :], m_dt[:, 2, :]))
                link(nc.vector.tensor_tensor(m_dt[:, 1, :], m_dt[:, 1, :], m_dt[:, 4, :], ALU.mult))
                dve.wait_ge(S("m_dt_act"), 2 * layer + 2)
                link(nc.vector.tensor_tensor(m_dt[:, 1, :], m_dt[:, 1, :], m_dt[:, 3, :], ALU.add))
                link(nc.vector.scalar_tensor_tensor(out=m_dt[:, 0, :], in0=m_dt[:, 0, :], scalar=0.0,
                                                    in1=m_dt[:, 1, :], op0=ALU.max, op1=ALU.add))
                for t in range(NT):
                    ins = nc.vector.scalar_tensor_tensor(out=m_dt[:, 4, 8 * t:8 * t + 8], in0=m_dt[:, 0, 8 * t:8 * t + 8],
                                                         scalar=-1.0, in1=m_dt[:, 5, 0:8], op0=ALU.mult, op1=ALU.mult)
                ins.then_inc(S("m_dt"), 1)
                for k in range(4, 8):
                    conv(k)
                    if k == 4:
                        beside_dve(early[2:])
                    elif k < 7:
                        beside_dve(late[2 * (k - 5):2 * (k - 4)])
                dve.wait_ge(S("m_cs_mm"), layer + 1)
                nc.vector.tensor_copy(m_cs[:, :], ps[0:8, 2, 0:T])
                nc.vector.tensor_scalar(m_ncs[:, :], ps[:, 3, 0:16], -1.0, None, ALU.mult).then_inc(S("m_cs"), 1)
                dve.wait_ge(S("m_cs"), layer + 1)
                d0 = 48 + 8 * layer
                for j in range(2):
                    hh = slice(64 * j, 64 * j + 64)
                    ins = nc.vector.tensor_copy(m_d[hh, :], bcast[hh, d0 + j:d0 + 8:2])
                link(ins)
                dve.wait_ge(S("m_cb"), layer + 1)

                def seg(h):
                    dve.wait_ge(S("m_row"), 8 * layer + h + 1)
                    if h >= 2:
                        dve.wait_ge(S("m_o"), 8 * layer + h - 1)
                    row = ps[:, 4 + h % 2, 0:T]
                    e = m_e[:, h % 2, :]
                    for t in range(NT):
                        ins = nc.vector.scalar_tensor_tensor(out=e[:, t * T:t * T + P], in0=row[:, t * P:(t + 1) * P],
                                                             scalar=m_ncs[:, 8 * t + h:8 * t + h + 1],
                                                             in1=K("causal_t"), op0=ALU.add, op1=ALU.add)
                    nc.vector.tensor_scalar(e[:, P:T], row[:, P:T], m_ncs[:, h:h + 1], None, ALU.add)\
                        .then_inc(S("m_seg"), 1)

                beside_dve(late[4:])
                seg(0)
                for h in range(8):
                    if h + 1 < 8:
                        seg(h + 1)
                    dve.wait_ge(S("m_exp"), 8 * layer + h + 1)
                    g = h // 4
                    e = m_e[:, h % 2, :]
                    nc.vector.scalar_tensor_tensor(out=e[:, 0:T], in0=e[:, 0:T], scalar=m_dt[:, 0, h:h + 1],
                                                   in1=ps[:, 2 + g, 0:T], op0=ALU.mult, op1=ALU.mult)
                    nc.vector.scalar_tensor_tensor(out=e[:, T:T + P], in0=e[:, T:T + P], scalar=m_dt[:, 0, 8 + h:9 + h],
                                                   in1=ps[:, 2 + g, T + P:2 * T], op0=ALU.mult, op1=ALU.mult)\
                        .then_inc(S("m_score"), 1)
                    if h % 2:
                        p = h // 2
                        dve.wait_ge(S("m_o"), 8 * layer + h + 1)
                        nc.vector.scalar_tensor_tensor(out=m_y[:, p, :], in0=m_cv[:, p, :], scalar=m_d[:, p:p + 1],
                                                       in1=ps[:, 6 + p % 2, 0:T], op0=ALU.mult, op1=ALU.add)\
                            .then_inc(S("m_y"), 1)
                    beside_dve(beside.splits(2 + h, 3 + h))
                beside_dve(beside.splits(10, 11))
                dve.wait_ge(S("m_y"), 4 * layer + 4)
                nc.vector.tensor_tensor(m_y[:, :, :], m_y[:, :, :], m_in[:, 0:4, :], ALU.mult).then_inc(S("m_gated"), 1)
                dve.wait_ge(S("m_root"), layer + 1)
                link(nc.vector.reciprocal(rstd[:, :], root[:, :]))
                for k in range(4):
                    ins = nc.vector.scalar_tensor_tensor(out=m_y[:, k, :], in0=m_y[:, k, :],
                                                         scalar=V("ssm_norm_2", 4 * layer + k),
                                                         in1=rstd[:, (k // 2) * T:(k // 2 + 1) * T],
                                                         op0=ALU.mult, op1=ALU.mult)
                ins.then_inc(S("m_normed"), 1)
                beside_dve(beside.splits(11, 15))
                c.units += len(beside.units)
                dve.wait_ge(S("m_yh"), layer + 1)
                nc.vector.tensor_tensor(h_yl[:, :, :], m_y[:, :, :], h_yh[:, :, :].bitcast(F32), ALU.subtract)\
                    .then_inc(S("m_yl"), 1)

            def turn(n, buf, bank, n_chunks, count):
                dve.wait_ge(S("a_swap"), count)
                if count > 1:
                    dve.wait_ge(S("a_turned"), count - 1)
                if n_chunks == 2:
                    spreadto = lambda t: K(t).unsqueeze(1).to_broadcast([P, 2, T])
                    x, t, s = buf, a_turn[:, :, :], ps[:, bank, :].rearrange("p (a b) -> p a b", a=2)
                else:
                    spreadto = K
                    x, t, s = buf, a_turn[:, 0, :], ps[:, bank, 0:T]
                nc.vector.tensor_tensor(t, s, spreadto("rope_sin"), ALU.mult)
                link(nc.vector.tensor_tensor(x, x, spreadto("rope_cos"), ALU.mult))
                nc.vector.tensor_tensor(x, x, t, ALU.add).then_inc(S("a_turned"), 1)

            def choose(layer, beside):
                link(nc.vector.tensor_scalar(a_w[:, :, :], h_small[:, :, 80:84], 0.5, None, ALU.mult))
                for qt in range(NT):
                    nk = (qt + 1) * P
                    if qt == 0:
                        beside_dve(beside.splits(1, 2))
                    dve.wait_ge(S("a_idx"), NT * layer + qt + 1)
                    if qt == 0:
                        beside_dve(beside.splits(2, 3))
                    for h in range(4):
                        link(nc.vector.tensor_scalar(a_relu[:, 0:nk], ps[:, 4 + h, 0:nk], HD ** -0.5, 0.0,
                                                     ALU.mult, ALU.max))
                        w = a_w[:, qt, h:h + 1]
                        if h == 0:
                            link(nc.vector.tensor_scalar(a_isc[:, 0:nk], a_relu[:, 0:nk], w, None, ALU.mult))
                        else:
                            link(nc.vector.scalar_tensor_tensor(out=a_isc[:, 0:nk], in0=a_relu[:, 0:nk], scalar=w,
                                                                in1=a_isc[:, 0:nk], op0=ALU.mult, op1=ALU.add))
                    diag = slice(nk - P, nk)
                    nc.vector.tensor_tensor(a_isc[:, diag], a_isc[:, diag], K("causal"), ALU.add).then_inc(S("a_isc"), 1)
                    dve.wait_ge(S("a_isc"), NT * layer + qt + 1)
                    if qt == 0:
                        beside_dve(beside.splits(3, 4))
                    for _ in range(DSA_KEEP // 8):
                        link(nc.vector.max(a_top[:, :], a_isc[:, 0:nk]))
                        link(nc.vector.match_replace(a_isc[:, 0:nk], a_top[:, :], a_isc[:, 0:nk], TAKEN))
                    b0 = (0, P)[qt]
                    link(nc.vector.tensor_scalar(a_bias[:, 0, b0:b0 + nk], a_isc[:, 0:nk], TAKEN, NEG,
                                                 ALU.not_equal, ALU.mult))
                    bd = a_bias[:, 0, b0 + nk - P:b0 + nk]
                    link(nc.vector.tensor_tensor(bd, bd, K("causal"), ALU.add))

            def attention(layer, which):
                a = 3 * layer + which
                n = which + 1
                beside = Beside(n, places_of(n))
                a_qk = qk_set[which % 2]
                if which == 0:
                    f0 = 32 + 8 * layer
                    for t in range(NT):
                        ins = nc.vector.tensor_tensor(a_f[:, 0, 8 * t:8 * t + 8], h_small[:, t, 8:16],
                                                      bcast[:, f0:f0 + 8], ALU.add)
                    ins.then_inc(S("a_f"), 1)
                    dve.wait_ge(S("a_f_ln"), layer + 1)
                    nc.vector.scalar_tensor_tensor(out=a_f[:, 2, :], in0=a_f[:, 0, :], scalar=0.0, in1=a_f[:, 1, :],
                                                   op0=ALU.min, op1=ALU.subtract).then_inc(S("a_f"), 1)
                    dve.wait_ge(S("a_cf_mm"), layer + 1)
                    nc.vector.tensor_scalar(a_cf[:, :], ps[0:8, 2, 0:T], -1.0, None, ALU.mult)
                    nc.vector.tensor_copy(a_f[:, 3, :], ps[:, 3, 0:16]).then_inc(S("a_cf"), 1)
                    dve.wait_ge(S("a_cf"), layer + 1)
                else:
                    if which == 2:
                        beside_dve(beside.splits(0, 1))
                        for j in range(2):
                            ins = nc.vector.tensor_copy(a_ik2[:, :, 64 * j:64 * j + 64], h_small[:, :, 16:80])
                        ins.then_inc(S("a_ik2"), 1)
                    dve.wait_ge(S("evac_done"), c.units + CREDIT)
                    r0 = 10 * layer + (0, 0, 4)[which]
                    for m in range(4):
                        turn(m, a_qk[:, 2 * m:2 * m + 2, :], m, 2, r0 + m + 1)
                    if which == 2:
                        dve.wait_ge(S("a_ik_t"), layer + 1)
                        nc.vector.tensor_copy(a_ik[:, :], ps[:, 6, 0:T]).then_inc(S("a_ik"), 1)
                        dve.wait_ge(S("a_ik"), layer + 1)
                        turn(4, a_iq[:, :, :], 4, 2, r0 + 5)
                        turn(5, a_ik[:, :], 5, 1, r0 + 6)
                        choose(layer, beside)
                        beside_dve(beside.splits(4, 8))
                    else:
                        nc.vector.memset(a_bias[:, 0, P:2 * P], 0.0)
                        nc.vector.tensor_copy(a_bias[:, 0, 0:P], K("causal"))
                        link(nc.vector.tensor_copy(a_bias[:, 0, 2 * P:3 * P], K("causal")))

                def forget_bias(h):
                    dve.wait_ge(S("a_row"), 8 * layer + h + 1)
                    row = ps[:, 7, 0:T]
                    b = a_bias[:, h % 2, :]
                    cq = lambda t: a_f[:, 3, 8 * t + h:8 * t + h + 1]
                    nc.vector.scalar_tensor_tensor(out=b[:, 0:P], in0=row[:, 0:P], scalar=cq(0), in1=K("causal"),
                                                   op0=ALU.add, op1=ALU.add)
                    nc.vector.tensor_scalar(b[:, P:2 * P], row[:, 0:P], cq(1), None, ALU.add)
                    nc.vector.scalar_tensor_tensor(out=b[:, 2 * P:3 * P], in0=row[:, P:T], scalar=cq(1),
                                                   in1=K("causal"), op0=ALU.add, op1=ALU.add).then_inc(S("a_bias"), 1)
                    dve.wait_ge(S("a_bias"), 8 * layer + h + 1)

                def masked(e):
                    h, qt = divmod(e, 2)
                    nk = (qt + 1) * P
                    if which == 0 and qt == 0:
                        forget_bias(h)
                    b0 = (0, P)[qt]
                    bias = a_bias[:, h % 2 if which == 0 else 0, b0:b0 + nk]
                    dve.wait_ge(S("a_scores"), 16 * a + e + 1)
                    if e >= 2:
                        dve.wait_ge(S("a_t"), 16 * a + e - 1)
                    link(nc.vector.scalar_tensor_tensor(out=a_p[:, e % 2, 0:nk], in0=ps[:, 4 + e % 2, 0:nk],
                                                        scalar=HD ** -0.5, in1=bias, op0=ALU.mult, op1=ALU.add))
                    nc.vector.tensor_reduce(a_st[:, e, 0:1], a_p[:, e % 2, 0:nk], AX.X, ALU.max, negate=True)\
                        .then_inc(S("a_max"), 1)

                masked(0)
                for e in range(18):
                    if e < 16:
                        nk = (e % 2 + 1) * P
                        dve.wait_ge(S("a_exp"), 16 * a + e + 1)
                        link(nc.vector.reciprocal(a_st[:, e, 2:3], a_st[:, e, 1:2]))
                        nc.vector.tensor_scalar(a_p[:, e % 2, 0:nk], a_p[:, e % 2, 0:nk], a_st[:, e, 2:3], None, ALU.mult)\
                            .then_inc(S("a_p"), 1)
                    if e >= 5 and e % 4 == 1:
                        p = (e - 5) // 4
                        dve.wait_ge(S("a_yh"), 4 * a + p + 1)
                        nc.vector.tensor_tensor(h_yl[:, p, :], ps[:, 2 + p % 2, 0:T], h_yh[:, p, :].bitcast(F32),
                                                ALU.subtract).then_inc(S("a_yl"), 1)
                    if which < 2:
                        beside_dve(beside.splits(2 * e, 2 * e + 2))
                    if e + 1 < 16:
                        masked(e + 1)
                c.units += len(beside.units)

            def branch(layer, n):
                def unit(i, s):
                    unit_done(dve, c, i, s)
                    dve.wait_ge(S("h_gate"), 4 * layer + n + 1)
                    dst, gate = h_merged[:, 4 * s:4 * s + 4, :], h_gates[:, 4 * s:4 * s + 4, :]
                    nc.vector.tensor_tensor(gate if n else dst, ps[:, 2 * s:2 * s + 2, :].rearrange("p a (b t) -> p (a b) t", t=T),
                                            gate, ALU.mult).then_inc(S("evac_done"), 1)
                    if n:
                        dve.wait_ge(S("evac_done"), c.units + s + 1 + CREDIT)
                        nc.vector.tensor_tensor(dst, dst, gate, ALU.add).then_inc(S("h_merged"), 1)
                pairs_of(dve, c, 1, unit, ahead=dve_split)

            def merged(layer):
                dve.wait_ge(S("h_merged_hi"), layer + 1)
                nc.vector.tensor_tensor(xl[:, :, 0:T], h_merged, xh[:, :, 0:T].bitcast(F32), ALU.subtract)\
                    .then_inc(S("h_merged_lo"), 1)

            def add_plain(n, n0):
                def add(i, s):
                    dst = h_out[:, bass.ds(i * 2 + (n0 + s), 1), :]
                    src = ps[:, 2 * s:2 * s + 1, 0:T]
                    if n == 0:
                        ins = nc.vector.tensor_copy(dst, src)
                    else:
                        ins = nc.vector.tensor_tensor(dst, src, dst, ALU.add)
                    ins.then_inc(S("evac_done"), 1)
                return add

            for stage, *args in schedule:
                if stage == "gains":
                    norm_gains(*args)
                elif stage == "norm":
                    norm(args[0], args[1], args[3], args[2])
                elif stage == "renorm":
                    src, gain = args[:2]
                    rstd_of_root(NT)
                    for k in range(DC + 1):
                        if k < DC:
                            dst = hT if src is hT else normed
                            ins = nc.vector.scalar_tensor_tensor(out=dst[:, k, 0:T], in0=src[:, k, 0:T], scalar=gain(k),
                                                                 in1=ps[:, 5, 0:T], op0=ALU.mult, op1=ALU.mult)
                            ins.then_inc(S("renormed" if src is hT else "post_normed"), 1)
                        if k and src is not hT:
                            dve.wait_ge(S("post_normed"), c.of["post"] + k)
                            nc.vector.tensor_tensor(hT[:, k - 1, 0:T], hT[:, k - 1, 0:T], normed[:, k - 1, 0:T], ALU.add)\
                                .then_inc(S("renormed"), 1)
                    c.add(norm=1, renorm=DC, post=DC * (src is not hT))
                    if args[2]:
                        sq_all(T)
                elif stage == "ffn":
                    ffn(args[2], args[4], args[5], args[3])
                elif stage == "even":
                    even()
                elif stage == "odd":
                    odd()
                elif stage == "out":
                    mod_blocks(args[2], 1, 2)
                    gate0 = 8 * N_MOD * args[2] + 24 + 16
                    def out_unit(i, s):
                        unit_done(dve, c, i, s)
                        for b in range(2):
                            n = i * 4 + (2 * s + b)
                            for j in range(args[1] // T):
                                sl = slice(j * T, (j + 1) * T)
                                ins = nc.vector.scalar_tensor_tensor(
                                    out=hT[:, bass.ds(n, 1), sl], in0=ps[:, 2 * s + b:2 * s + b + 1, sl],
                                    scalar=mod[:, bass.ds(n + gate0, 1), j], in1=hT[:, bass.ds(n, 1), sl],
                                    op0=ALU.mult, op1=ALU.add)
                        ins.then_inc(S("evac_done"), 1)
                        sq_lag(i, s, 2, args[1])
                    pairs_of(dve, c, 2, out_unit, ahead=dve_split, first=True)
                    sq_close(2, args[1])
                elif stage == "mamba":
                    mamba(args[0])
                elif stage == "attention":
                    attention(*args)
                elif stage == "branch":
                    branch(*args)
                elif stage == "wout":
                    merged(args[0])
                    pairs_of(dve, c, 2, lambda i, s: (fm_evac(h_out, 0, T)(dve, c, i, s), sq_lag(i, s, 2, T)),
                             ahead=dve_split, first=True)
                    sq_close(2, T)
                elif stage == "store":
                    for t in range(NT):
                        dve.wait_ge(S("y_t"), t + 1)
                        nc.vector.tensor_copy(y_tok[:, t, :].rearrange("p (a b) -> p a b", a=2),
                                              ps[:, 2 * t:2 * t + 2, :]).then_inc(S("y_copied"), 1)


def kernel(**inputs):
    import concourse.bacc as bacc
    from concourse.bass_utils import run_bass_kernel_spmd

    nc = bacc.Bacc("TRN2", target_bir_lowering=False, num_devices=1)
    table, const_at = constants()
    arrays, io = {"consts": table}, {}
    for name in NAMES:
        arrays[name] = np.ascontiguousarray(inputs[name])
    for name, a in arrays.items():
        io[name] = nc.dram_tensor(name, a.shape, F32, kind="ExternalInput").ap()
    io["out"] = nc.dram_tensor("out", (1, T, D), F32, kind="ExternalOutput").ap()
    chunked = lambda a, pat: io[a].rearrange(pat, p=P)
    io["vectors"] = [
        ("ada_b", chunked("ada_b", "l (b p) -> (l b) p")),
        ("norm_ffn1", chunked("norm_ffn1", "l (b p) -> (l b) p")),
        ("norm_mix", chunked("norm_mix", "l (b p) -> (l b) p")),
        ("norm_ffn2", chunked("norm_ffn2", "l (b p) -> (l b) p")),
        ("final_norm", chunked("final_norm", "(b p) -> b p")),
        ("c", chunked("c", "l (b p) -> (l b) p")),
        ("c_ctx", chunked("c_ctx", "(b p) -> b p")),
        ("gla_norm", io["gla_norm"]),
        ("diff_norm", io["diff_norm"]),
        ("conv_w", chunked("conv_w", "l k (b p) -> (l k b) p")),
        ("conv_b", chunked("conv_b", "l (b p) -> (l b) p")),
        ("norm_mix_pre_2", chunked("norm_mix_pre_2", "l (b p) -> (l b) p")),
        ("conv_w_2", chunked("conv_w_2", "l k (b p) -> (l k b) p")),
        ("conv_b_2", chunked("conv_b_2", "l (b p) -> (l b) p")),
        ("ssm_norm_2", chunked("ssm_norm_2", "l (b p) -> (l b) p")),
        ("norm_mix_post_2", chunked("norm_mix_post_2", "l (b p) -> (l b) p")),
        ("norm_ffn_pre_2", chunked("norm_ffn_pre_2", "l (b p) -> (l b) p")),
        ("norm_ffn_post_2", chunked("norm_ffn_post_2", "l (b p) -> (l b) p")),
        ("b_gate_2", chunked("b_gate_2", "l (b p) -> (l b) p")),
    ]
    build(nc, io, const_at)
    r = run_bass_kernel_spmd(nc, [arrays], core_ids=[0])
    return r.results[0]["out"]
```
